# Optimizing a Trainium2 kernel written in Bass

```python
import math
import jax, jax.numpy as jnp
from jax import lax
import numpy as np

D_MODEL = 2048
BATCH = 1
SEQ = 256
DEPTH = 1

CHUNK = 64
N_META = 16
D_RWKV = 1024
RWKV_HEAD = 64
N_RWKV_HEADS = D_RWKV // RWKV_HEAD
D_DECAY_LORA = 64
D_AAA_LORA = 64
D_CONV = 1024
CONV_GROUP = 64
CONV_WIDTH = 3
RMS_EPS = 1e-6
LNX_EPS = 64e-5

RW_COLS = 4 * D_RWKV + D_DECAY_LORA + D_AAA_LORA
CV_COLS = 4 * D_CONV
IN_COLS = RW_COLS + CV_COLS
D_MIX = D_RWKV + D_CONV


def _rmsnorm(x, g):
    xf = x.astype(jnp.float32)
    y = xf * lax.rsqrt(jnp.mean(xf * xf, axis=-1, keepdims=True) + RMS_EPS)
    return (y * g.astype(jnp.float32)).astype(x.dtype)

def _rwkv7_recurrence(r, decay, k, v, kk, b):
    bsz, L, H, N = r.shape
    xs = tuple(jnp.moveaxis(t.astype(jnp.float32), 1, 0) for t in (r, decay, k, v, kk, b))

    def step(S, inp):
        r_t, w_t, k_t, v_t, kk_t, b_t = inp
        sa = jnp.einsum('bhvk,bhk->bhv', S, kk_t)
        S = (S * w_t[:, :, None, :]
             - sa[..., None] * b_t[:, :, None, :]
             + v_t[..., None] * k_t[:, :, None, :])
        y_t = jnp.einsum('bhvk,bhk->bhv', S, r_t)
        return S, y_t

    S0 = jnp.zeros((bsz, H, N, N), jnp.float32)
    S, y_meta = lax.scan(step, S0, tuple(t[:N_META] for t in xs))
    real = tuple(t[N_META:].reshape((-1, CHUNK) + t.shape[1:]) for t in xs)

    def chunk_step(S, chunk):
        return lax.scan(step, S, chunk)

    S, y_real = lax.scan(chunk_step, S, real)
    y = jnp.concatenate([y_meta, y_real.reshape((-1,) + y_real.shape[2:])], axis=0)
    return jnp.moveaxis(y, 0, 1).astype(r.dtype)

def _causal_depthwise_conv(u, w):
    C = u.shape[-1]
    return lax.conv_general_dilated(
        u, w[:, None, :].astype(u.dtype),
        window_strides=(1,), padding=[(CONV_WIDTH - 1, 0)],
        dimension_numbers=('NWC', 'WIO', 'NWC'),
        feature_group_count=C)

def first_inputs(seed: int = 0) -> dict:
    key = jax.random.key(seed)
    ks = jax.random.split(key, 20)
    f32 = jnp.float32
    x = jax.random.normal(ks[0], (BATCH, SEQ, D_MODEL), f32)
    meta_tokens = jax.random.normal(ks[1], (N_META, D_MODEL), f32)
    norm_in_g = 1.0 + 0.05 * jax.random.normal(ks[2], (DEPTH, D_MODEL), f32)
    w_in = jax.random.normal(ks[3], (DEPTH, D_MODEL, IN_COLS), f32) * D_MODEL ** -0.5
    mu_shift = jax.random.uniform(ks[4], (DEPTH, RW_COLS), f32)
    w0 = jax.random.uniform(ks[5], (DEPTH, D_RWKV), f32, minval=-6.0, maxval=1.0)
    w_lora_up = jax.random.normal(ks[6], (DEPTH, D_DECAY_LORA, D_RWKV), f32) * D_DECAY_LORA ** -0.5
    a0 = 0.1 * jax.random.normal(ks[7], (DEPTH, D_RWKV), f32)
    a_lora_up = jax.random.normal(ks[8], (DEPTH, D_AAA_LORA, D_RWKV), f32) * D_AAA_LORA ** -0.5
    k_k = 0.85 + 0.05 * jax.random.normal(ks[9], (DEPTH, D_RWKV), f32)
    k_a = 1.0 + 0.05 * jax.random.normal(ks[10], (DEPTH, D_RWKV), f32)
    r_k = 0.1 * jax.random.normal(ks[11], (DEPTH, N_RWKV_HEADS, RWKV_HEAD), f32)
    lnx_g = 1.0 + 0.05 * jax.random.normal(ks[12], (DEPTH, D_RWKV), f32)
    lnx_b = 0.01 * jax.random.normal(ks[13], (DEPTH, D_RWKV), f32)
    conv_w = jax.random.normal(ks[14], (DEPTH, CONV_WIDTH, D_CONV), f32) * CONV_WIDTH ** -0.5
    w_out = jax.random.normal(ks[15], (DEPTH, D_MIX, D_MODEL), f32) * D_MIX ** -0.5
    norm_f_g = 1.0 + 0.05 * jax.random.normal(ks[16], (D_MODEL,), f32)
    return {"x": x, "meta_tokens": meta_tokens, "norm_in_g": norm_in_g, "w_in": w_in,
            "mu_shift": mu_shift, "w0": w0, "w_lora_up": w_lora_up, "a0": a0,
            "a_lora_up": a_lora_up, "k_k": k_k, "k_a": k_a, "r_k": r_k,
            "lnx_g": lnx_g, "lnx_b": lnx_b, "conv_w": conv_w, "w_out": w_out,
            "norm_f_g": norm_f_g}

def first_block(x, meta_tokens, norm_in_g, w_in, mu_shift, w0, w_lora_up, a0, a_lora_up,
              k_k, k_a, r_k, lnx_g, lnx_b, conv_w, w_out, norm_f_g):
    bsz = x.shape[0]
    meta = jnp.broadcast_to(meta_tokens[None].astype(x.dtype), (bsz, N_META, D_MODEL))
    h_res = jnp.concatenate([meta, x], axis=1)
    L = h_res.shape[1]
    H, N = N_RWKV_HEADS, RWKV_HEAD

    for l in range(DEPTH):
        hn = _rmsnorm(h_res, norm_in_g[l])
        P = hn @ w_in[l]
        Pr, Pc = P[..., :RW_COLS], P[..., RW_COLS:]

        prev = jnp.pad(Pr[:, :-1], ((0, 0), (1, 0), (0, 0)))
        Pr = Pr + (prev - Pr) * mu_shift[l]
        r = Pr[..., 0 * D_RWKV:1 * D_RWKV]
        k = Pr[..., 1 * D_RWKV:2 * D_RWKV]
        v = Pr[..., 2 * D_RWKV:3 * D_RWKV]
        g_r = Pr[..., 3 * D_RWKV:4 * D_RWKV]
        wl = Pr[..., 4 * D_RWKV:4 * D_RWKV + D_DECAY_LORA]
        al = Pr[..., 4 * D_RWKV + D_DECAY_LORA:]

        w_raw = -jax.nn.softplus(-(w0[l] + jnp.tanh(wl) @ w_lora_up[l])) - 0.5
        decay = jnp.exp(-jnp.exp(w_raw.astype(jnp.float32)))
        a = jax.nn.sigmoid(a0[l] + al @ a_lora_up[l])

        kk = (k * k_k[l]).reshape(bsz, L, H, N)
        kk = kk / jnp.maximum(jnp.linalg.norm(kk.astype(jnp.float32), axis=-1, keepdims=True), 1e-12).astype(kk.dtype)
        k = k * (1.0 + (a - 1.0) * k_a[l])

        rh = r.reshape(bsz, L, H, N)
        kh = k.reshape(bsz, L, H, N)
        vh = v.reshape(bsz, L, H, N)
        ah = a.reshape(bsz, L, H, N)
        y = _rwkv7_recurrence(rh, decay.reshape(bsz, L, H, N), kh, vh, kk, kk * ah)

        yf = y.astype(jnp.float32)
        mean = jnp.mean(yf, axis=-1, keepdims=True)
        var = jnp.mean(jnp.square(yf - mean), axis=-1, keepdims=True)
        yn = ((yf - mean) * lax.rsqrt(var + LNX_EPS)).reshape(bsz, L, D_RWKV)
        yn = (yn * lnx_g[l] + lnx_b[l]).astype(x.dtype)
        bonus = jnp.sum(rh * kh * r_k[l], axis=-1, keepdims=True) * vh
        y_a = (yn + bonus.reshape(bsz, L, D_RWKV)) * jax.nn.silu(g_r)

        Bg = Pc[..., 0 * D_CONV:1 * D_CONV]
        Cg = Pc[..., 1 * D_CONV:2 * D_CONV]
        hc = Pc[..., 2 * D_CONV:3 * D_CONV]
        g_c = Pc[..., 3 * D_CONV:4 * D_CONV]
        y_b = Bg * _causal_depthwise_conv(Cg * hc, conv_w[l]) * jax.nn.silu(g_c)

        mix = jnp.concatenate([y_a, y_b], axis=-1)
        h_res = h_res + mix @ w_out[l]

    out = _rmsnorm(h_res, norm_f_g)
    return out[:, N_META:]


DEPTH_2 = 2

EXPAND = 2
D_INNER = EXPAND * D_MODEL
HEAD_DIM = 128
N_HEADS = D_INNER // HEAD_DIM
N_LEFT_CHUNKS = 8
BAND = (N_LEFT_CHUNKS + 1) * CHUNK
REL_CLIP = 256
N_REL = 2 * REL_CLIP + 1
Q_BLOCK = 128
N_A_LAYERS = DEPTH_2 // 2
N_B_LAYERS = DEPTH_2 - N_A_LAYERS
EPS = 1e-6
NEG_INF = -1e30


def rms_norm(x, g):
    xf = x.astype(jnp.float32)
    y = xf * lax.rsqrt(jnp.mean(xf * xf, axis=-1, keepdims=True) + EPS)
    return (y * g.astype(jnp.float32)).astype(x.dtype)

def split_heads(t):
    return t.reshape(t.shape[0], t.shape[1], N_HEADS, HEAD_DIM)

def chunked_relbias_attention(q, k, v, rel_bias):
    b, s = q.shape[0], q.shape[1]
    n_chunks = s // CHUNK
    pad = N_LEFT_CHUNKS * CHUNK
    k_pad = jnp.pad(k, ((0, 0), (pad, 0), (0, 0), (0, 0)))
    v_pad = jnp.pad(v, ((0, 0), (pad, 0), (0, 0), (0, 0)))
    qi = jnp.arange(CHUNK)[:, None]
    kj = jnp.arange(BAND)[None, :]
    rel_idx = jnp.clip(pad + qi - kj, -REL_CLIP, REL_CLIP) + REL_CLIP
    bias = rel_bias.astype(jnp.float32)[:, rel_idx]
    scale = HEAD_DIM ** -0.5
    band_pos = jnp.arange(BAND)

    def one_chunk(c):
        start = c * CHUNK
        q_c = lax.dynamic_slice_in_dim(q, start, CHUNK, axis=1)
        k_c = lax.dynamic_slice_in_dim(k_pad, start, BAND, axis=1)
        v_c = lax.dynamic_slice_in_dim(v_pad, start, BAND, axis=1)
        sc = jnp.einsum('bqhd,bkhd->bhqk', q_c, k_c).astype(jnp.float32) * scale + bias
        valid = (start + band_pos) >= pad
        sc = jnp.where(valid[None, None, None, :], sc, NEG_INF)
        p = jax.nn.softmax(sc, axis=-1).astype(v.dtype)
        return jnp.einsum('bhqk,bkhd->bqhd', p, v_c)

    out = lax.map(one_chunk, jnp.arange(n_chunks))
    return jnp.moveaxis(out, 0, 1).reshape(b, s, N_HEADS, HEAD_DIM)

def forgetting_attention(q, k, v, cum_logf_h):
    s = q.shape[1]
    scale = HEAD_DIM ** -0.5
    outs = []
    for i in range(s // Q_BLOCK):
        q0 = i * Q_BLOCK
        end = q0 + Q_BLOCK
        q_b = q[:, q0:end]
        k_b = k[:, :end]
        v_b = v[:, :end]
        sc = jnp.einsum('bqhd,bkhd->bhqk', q_b, k_b).astype(jnp.float32) * scale
        decay = cum_logf_h[:, :, q0:end, None] - cum_logf_h[:, :, None, :end]
        causal = (q0 + jnp.arange(Q_BLOCK))[:, None] >= jnp.arange(end)[None, :]
        sc = jnp.where(causal[None, None], sc + decay, NEG_INF)
        p = jax.nn.softmax(sc, axis=-1).astype(v.dtype)
        outs.append(jnp.einsum('bhqk,bkhd->bqhd', p, v_b))
    return jnp.concatenate(outs, axis=1)

def second_inputs(seed: int = 0) -> dict:
    key = jax.random.key(seed)
    ks = jax.random.split(key, 16)
    f32 = jnp.float32
    d_scale = D_MODEL ** -0.5
    out_scale = 0.5 * D_INNER ** -0.5
    x = jax.random.normal(ks[0], (BATCH, SEQ, D_MODEL), f32)
    a_norm = 1.0 + 0.02 * jax.random.normal(ks[1], (N_A_LAYERS, D_MODEL), f32)
    a_w_in = d_scale * jax.random.normal(ks[2], (N_A_LAYERS, D_MODEL, 4 * D_INNER), f32)
    a_rel_bias = 0.1 * jax.random.normal(ks[3], (N_A_LAYERS, N_HEADS, N_REL), f32)
    a_w_out = out_scale * jax.random.normal(ks[4], (N_A_LAYERS, D_INNER, D_MODEL), f32)
    kv_norm = 1.0 + 0.02 * jax.random.normal(ks[5], (D_MODEL,), f32)
    kv_w = d_scale * jax.random.normal(ks[6], (D_MODEL, 2 * D_INNER), f32)
    f_w = d_scale * jax.random.normal(ks[7], (D_MODEL, N_HEADS), f32)
    f_b = jnp.linspace(1.0, 5.0, N_HEADS, dtype=f32) + 0.1 * jax.random.normal(ks[8], (N_HEADS,), f32)
    b_norm = 1.0 + 0.02 * jax.random.normal(ks[9], (N_B_LAYERS, D_MODEL), f32)
    b_w_in = d_scale * jax.random.normal(ks[10], (N_B_LAYERS, D_MODEL, 2 * D_INNER), f32)
    b_w_out = out_scale * jax.random.normal(ks[11], (N_B_LAYERS, D_INNER, D_MODEL), f32)
    final_norm = 1.0 + 0.02 * jax.random.normal(ks[12], (D_MODEL,), f32)
    return {"x": x, "a_norm": a_norm, "a_w_in": a_w_in, "a_rel_bias": a_rel_bias,
            "a_w_out": a_w_out, "kv_norm": kv_norm, "kv_w": kv_w, "f_w": f_w,
            "f_b": f_b, "b_norm": b_norm, "b_w_in": b_w_in, "b_w_out": b_w_out,
            "final_norm": final_norm}

def second_block(x, a_norm, a_w_in, a_rel_bias, a_w_out, kv_norm, kv_w, f_w, f_b,
              b_norm, b_w_in, b_w_out, final_norm):
    b, s, _ = x.shape
    k_sh = v_sh = cum_logf_h = None
    for layer in range(DEPTH_2):
        if layer < N_A_LAYERS:
            h = rms_norm(x, a_norm[layer])
            q, k, v, g = jnp.split(h @ a_w_in[layer], 4, axis=-1)
            o = chunked_relbias_attention(split_heads(q), split_heads(k), split_heads(v),
                                          a_rel_bias[layer]).reshape(b, s, D_INNER)
            x = x + (o * jax.nn.silu(g)) @ a_w_out[layer]
        else:
            if layer == N_A_LAYERS:
                h_kv = rms_norm(x, kv_norm)
                k_s, v_s = jnp.split(h_kv @ kv_w, 2, axis=-1)
                k_sh, v_sh = split_heads(k_s), split_heads(v_s)
                logf = jax.nn.log_sigmoid((h_kv @ f_w + f_b).astype(jnp.float32))
                cum_logf_h = jnp.transpose(jnp.cumsum(logf, axis=1), (0, 2, 1))
            lb = layer - N_A_LAYERS
            h = rms_norm(x, b_norm[lb])
            q, g = jnp.split(h @ b_w_in[lb], 2, axis=-1)
            o = forgetting_attention(split_heads(q), k_sh, v_sh, cum_logf_h).reshape(b, s, D_INNER)
            x = x + (o * jax.nn.silu(g)) @ b_w_out[lb]
    return rms_norm(x, final_norm)


def setup_inputs(seed=0):
    out = dict(first_inputs(seed))
    for name, value in second_inputs(seed + 1).items():
        if name != "x":
            out[name + "_2"] = value
    return out


def reference(
    x, meta_tokens, norm_in_g, w_in, mu_shift, w0, w_lora_up, a0, a_lora_up, k_k, k_a, r_k,
    lnx_g, lnx_b, conv_w, w_out, norm_f_g, a_norm_2, a_w_in_2, a_rel_bias_2, a_w_out_2,
    kv_norm_2, kv_w_2, f_w_2, f_b_2, b_norm_2, b_w_in_2, b_w_out_2, final_norm_2,
):
    x = first_block(
        x, meta_tokens, norm_in_g, w_in, mu_shift, w0, w_lora_up, a0, a_lora_up, k_k, k_a, r_k,
        lnx_g, lnx_b, conv_w, w_out, norm_f_g,
    )
    return second_block(
        x, a_norm_2, a_w_in_2, a_rel_bias_2, a_w_out_2, kv_norm_2, kv_w_2, f_w_2, f_b_2,
        b_norm_2, b_w_in_2, b_w_out_2, final_norm_2,
    )


_drawn_inputs = setup_inputs


def setup_inputs(seed=0):
    import zlib

    import numpy as np

    out = dict(_drawn_inputs(seed))
    spreads = {}
    factors = {'w_lora_up': 3.716,
     'a0': 4.935,
     'k_k': 4.909,
     'k_a': 3.715,
     'lnx_g': 3.934,
     'lnx_b': 8.0,
     'a_norm_2': 8.0,
     'a_rel_bias_2': 8.0,
     'kv_norm_2': 8.0,
     'f_w_2': 3.023,
     'b_norm_2': 8.0,
     'final_norm_2': 2.725}
    for name, (base, spread) in spreads.items():
        noise = np.random.default_rng([zlib.crc32(name.encode()), seed]).standard_normal(out[name].shape)
        drawn = base * np.exp(spread * noise) if base else spread * noise
        out[name] = __import__('jax').numpy.asarray(drawn.astype(out[name].dtype))
    for name, factor in factors.items():
        out[name] = (out[name] * factor).astype(out[name].dtype)
    return out
```

```python
from contextlib import ExitStack

import numpy as np

import concourse.bass as bass
from concourse import mybir

F32 = mybir.dt.float32
F32R = mybir.dt.float32r
ALU = mybir.AluOpType
ACT = mybir.ActivationFunctionType
AX_X = mybir.AxisListType.X

P = 128
D = 2048
KT = D // P
SEQ = 256
META = 16
L = SEQ + META
CH = 1024
CT = CH // P
HEADS = 16
HD = 64
LORA = 64
C = 32
NCH = -(-L // C)
LP = NCH * C
TC = 3
TT = TC * C
NT = NCH // TC
RW_COLS = 4 * CH + 2 * LORA
NEG_INF = -1e30

AH = 32
DI = AH * P
GROUPS = 4
GH = AH // GROUPS
N_REL = 513

HALF = 8 * P
RAW = 4
SPL = 4
AHEAD = 3

MU_K, MU_R, MU_V, MU_G, W0, A0, KK, KA, RK, CW0, CW1, CW2, LG, LB = range(14)
NPRM = 14
G_IN, G_F, G_A, G_KV, G_B, G_OUT = range(6)

U_LORA = 0
U_IN = 1
PER_TILE = 8
U_WOUT = U_IN + CT * PER_TILE
PER_GROUP = 4 * GH + GH
U_A = U_WOUT + KT
U_B = U_A + GROUPS * PER_GROUP
U_END = U_B + GROUPS * PER_GROUP


class Chain:

    def __init__(self, eng, sem):
        self.eng, self.sem, self.n, self.dyn, self.began = eng, sem, 0, [], []

    def value(self):
        v = self.n
        for reg, per in self.dyn:
            v = reg * per + v
        return v

    def __call__(self, ins):
        ins.then_inc(self.sem, 1)
        self.n += 1

    def settle(self):
        self.eng.wait_ge(self.sem, self.value())

    def link(self, ins):
        self(ins)
        self.settle()

    def enter(self, reg, per):
        self.dyn.append((reg, per))
        self.began.append(self.n)

    def leave(self, count):
        reg, per = self.dyn.pop()
        began = self.began.pop()
        assert self.n - began == per, f"chain: {self.n - began} steps per round, {per} stated"
        self.n = began + count * per


class At:

    def __init__(self, u, loops=()):
        self.u, self.loops = u, tuple(loops)

    def __add__(self, k):
        return At(self.u + k, self.loops)

    def count(self, value, per_unit=1, per=1):
        v = value
        for reg, units in self.loops:
            v = reg * (units * per_unit // per) + v
        return v

    def bank(self):
        return self.u % 2

    def evacuated(self):
        return self.count(self.u // 2 + 1, 1, 2)


def wait(eng, sem, value):
    if isinstance(value, int) and value <= 0:
        return
    eng.wait_ge(sem, value)


def fused_blocks(nc, A, stop=99, dbg=None):
    with ExitStack() as top:
        _build(nc, A, top, stop, dbg or {})


def _build(nc, A, top, stop, dbg):
    def sbuf(stack, name, shape, dt=F32):
        return stack.enter_context(nc.sbuf_tensor(name, shape, dt))

    def sem(name):
        return top.enter_context(nc.semaphore(name))

    psum = [top.enter_context(nc.psum_tensor(f"bank{i}", [P, 512], F32)) for i in range(8)]
    GB = psum[0:2]

    raw_in = [sem(f"raw_in{i}") for i in range(RAW)]
    hi_ready = sem("hi_ready")
    lo_ready = sem("lo_ready")
    half_used = sem("half_used")
    taken = [sem("taken0"), sem("taken1")]
    stored = sem("stored")
    act_seq, dve_seq, pool_seq = sem("act_seq"), sem("dve_seq"), sem("pool_seq")
    chains = {}

    def chain(eng, name):
        s = {"act": act_seq, "dve": dve_seq, "pool": pool_seq}[name]
        if name not in chains:
            chains[name] = Chain(eng, s)
        chains[name].eng = eng
        return chains[name]

    ident = sbuf(top, "ident", [P, P])
    ones = sbuf(top, "ones", [P, P])
    gain = sbuf(top, "gain", [P, KT, 6])
    eps = sbuf(top, "eps", [P, 2])
    rms_small = sbuf(top, "rms_small", [P, L])
    rms_inv = sbuf(top, "rms_inv", [P, L])
    mix = sbuf(top, "mix", [P, 2 * CT, SEQ])
    gs = mix[:, 0:CT]
    yb = mix[:, CT:2 * CT]

    class Stream:
        def __init__(self, stack, tag):
            self.raw = [sbuf(stack, f"raw{tag}{i}", [P, 2 * HALF]) for i in range(RAW)]
            self.hi = [sbuf(stack, f"hi{tag}{i}", [P, HALF], F32R) for i in range(SPL)]
            self.lo = [sbuf(stack, f"lo{tag}{i}", [P, HALF], F32R) for i in range(SPL)]

        def load(self, sp, at, halves):
            wait(sp, lo_ready, at.count(2 * (at.u - RAW) + 2, 2))
            slot = at.u % RAW
            for h in range(2):
                dst = self.raw[slot][:, h * HALF:(h + 1) * HALF].rearrange("p (k n) -> p k n", n=P)
                sp.dma_start(dst, halves(h)).then_inc(raw_in[slot], 16)

        def load_columns(self, sp, at, w, cols):
            self.load(sp, at, lambda h: w[:, 8 * h:8 * h + 8, cols])

        def landed(self, eng, at):
            eng.wait_ge(raw_in[at.u % RAW], at.count(32 * (at.u // RAW + 1), 32, RAW))

        def split_hi(self, act, at, h):
            if h == 0:
                self.landed(act, at)
            wait(act, half_used, at.count(2 * at.u + h - SPL + 1, 2))
            nc.scalar.activation(self.hi[(2 * at.u + h) % SPL][:], self.raw[at.u % RAW][:, h * HALF:(h + 1) * HALF],
                                 ACT.Copy).then_inc(hi_ready, 1)

        def split_lo(self, dve, at, h):
            dve.wait_ge(hi_ready, at.count(2 * at.u + h + 1, 2))
            b = (2 * at.u + h) % SPL
            nc.vector.tensor_tensor(self.lo[b][:], self.raw[at.u % RAW][:, h * HALF:(h + 1) * HALF],
                                    self.hi[b][:].bitcast(F32), ALU.subtract).then_inc(lo_ready, 1)

        def product(self, pe, at, h, out, rhs_hi, rhs_lo, start, stop, tiles=range(8), before=None):
            b = (2 * at.u + h) % SPL
            if start and tiles[0] == 0:
                wait(pe, taken[at.bank()], at.count((at.u - 2) // 2 + 1, 1, 2))
            pe.wait_ge(lo_ready, at.count(2 * at.u + h + 1, 2))
            for k in tiles:
                if before and k in before:
                    before[k]()
                w = slice(k * P, (k + 1) * P)
                nc.tensor.matmul(out, self.hi[b][:, w], rhs_hi(k), start=start and k == 0, stop=False)
                nc.tensor.matmul(out, self.hi[b][:, w], rhs_lo(k), start=False, stop=False)
                last = nc.tensor.matmul(out, self.lo[b][:, w], rhs_hi(k), start=False, stop=stop and k == 7)
            if k == 7:
                last.then_inc(half_used, 1)

        def unit(self, pe, at, width, xh, xl, before=({}, {})):
            for h in range(2):
                self.product(pe, at, h, GB[at.bank()][:, 0:width], lambda k: xh[:, 8 * h + k, 0:width],
                             lambda k: xl[:, 8 * h + k, 0:width], start=h == 0, stop=h == 1, before=before[h])

    def computed(eng, at):
        eng.wait_ge(half_used, at.count(2 * at.u + 2, 2))

    const_ready, gain_in, x_in, prm_in = sem("const_ready"), sem("gain_in"), sem("x_in"), sem("prm_in")
    rms_sums, rms_sq, rms_bcast, rms_root, rms_done = (
        sem("rms_sums"), sem("rms_sq"), sem("rms_bcast"), sem("rms_root"), sem("rms_done"))
    xhi_ready, xlo_ready = sem("xhi_ready"), sem("xlo_ready")

    first = ExitStack()
    kr = sbuf(first, "kr", [P, CT, 2, LP])
    bk = sbuf(first, "bk", [P, CT, 2, LP])
    vv = sbuf(first, "vv", [P, CT, LP])
    bon = sbuf(first, "bon", [P, CT, SEQ])
    pc = sbuf(first, "pc", [P, CT, NCH])
    prm = sbuf(first, "prm_sb", [P, CT, NPRM])
    blk = sbuf(first, "blk", [P, P])
    mask = sbuf(first, "mask", [TT, 4, TT])

    rms_n = [0]

    class Rms:

        def __init__(self, x, sq, width):
            rms_n[0] += 1
            self.n, self.x, self.sq, self.w = rms_n[0], x, sq, width

        def act_square(self):
            nc.scalar.activation(self.sq, self.x, ACT.Square).then_inc(rms_sq, 1)

        def dve_sum(self, dve):
            dve.wait_ge(rms_sq, self.n)
            nc.vector.tensor_reduce(rms_small[:, 0:self.w], self.sq.rearrange("p k t -> p t k"), AX_X,
                                    ALU.add).then_inc(rms_sums, 1)

        def pe_bcast(self, pe, bank):
            pe.wait_ge(rms_sums, self.n)
            nc.tensor.matmul(bank[:, 0:self.w], ones[:], rms_small[:, 0:self.w], start=True,
                             stop=True).then_inc(rms_bcast, 1)

        def act_root(self, act, bank):
            act.wait_ge(rms_bcast, self.n)
            nc.scalar.activation(rms_inv[:, 0:self.w], bank[:, 0:self.w], ACT.Sqrt, bias=eps[:, 0:1],
                                 scale=1.0 / D).then_inc(rms_root, 1)

        def dve_inverse(self, dve, ch):
            dve.wait_ge(rms_root, self.n)
            ch.link(nc.vector.reciprocal(rms_inv[:, 0:self.w], rms_inv[:, 0:self.w]))

    xh = xl = None
    p01 = ExitStack()
    xh = sbuf(p01, "xh", [P, KT, L], F32R)
    xl = sbuf(p01, "xl", [P, KT, L], F32R)
    with ExitStack() as ph:
        x0 = sbuf(ph, "x0", [P, KT, L])
        sq0 = sbuf(ph, "sq0", [P, KT, L])
        rms = Rms(x0[:], sq0[:], L)
        with nc.Block() as block:
            @block.sync
            def _(sp):
                sp.dma_start(gain[:], A["gain"]).then_inc(gain_in, 16)
                sp.dma_start(x0[:], A["xt"]).then_inc(x_in, 16)
                sp.dma_start(prm[:], A["prm"]).then_inc(prm_in, 16)

            @block.gpsimd
            def _(pool):
                ch = chain(pool, "pool")
                g = nc.gpsimd
                ch(g.memset(ones[:], 1.0))
                ch(g.memset(ident[:], 0.0))
                ch(g.memset(eps[:, 0:1], 1e-6))
                ch(g.memset(eps[:, 1:2], 64e-5))
                ch(g.memset(blk[:], 0.0))
                ch(g.memset(mask[:, 0], -1.0))
                ch.link(g.memset(mask[:, 1:4], 1.0))
                ch.link(g.affine_select(out=ident[:], in_=ident[:], compare_op=ALU.not_equal, fill=1.0, base=0,
                                   pattern=[[-1, P]], channel_multiplier=1))
                ch.link(g.memset(blk[0:64, 0:64], 1.0))
                ch.link(g.memset(blk[64:128, 64:128], 1.0))
                for kind in range(4):
                    v = mask[:, kind].rearrange("p (c t) -> p c t", c=TC)
                    ch.link(g.affine_select(out=v, in_=v, compare_op=ALU.is_ge, fill=0.0, base=kind % 2 - 1,
                                            pattern=[[C, TC], [1, C]], channel_multiplier=-1))
                    ch.link(g.affine_select(out=v, in_=v, compare_op=ALU.is_ge, fill=0.0, base=0,
                                            pattern=[[-C, TC], [0, C]], channel_multiplier=1))
                ch.settle()

            @block.scalar
            def _(act):
                act.wait_ge(x_in, 16)
                rms.act_square()
                rms.act_root(act, psum[2])
                act.wait_ge(rms_done, 1)
                for half in range(2):
                    s = slice(half * KT // 2, (half + 1) * KT // 2)
                    act.wait_ge(rms_done, half + 1)
                    nc.scalar.activation(xh[:, s], x0[:, s], ACT.Copy).then_inc(xhi_ready, 1)

            @block.tensor
            def _(pe):
                pe.wait_ge(pool_seq, 7)
                rms.pe_bcast(pe, psum[2])

            @block.vector
            def _(dve):
                ch = chain(dve, "dve")
                ch(nc.vector.memset(vv[:, :, L:LP], 0.0))
                rms.dve_sum(dve)
                rms.dve_inverse(dve, ch)
                dve.wait_ge(gain_in, 16)
                for k in range(KT):
                    ins = nc.vector.scalar_tensor_tensor(x0[:, k], x0[:, k], gain[:, k, G_IN:G_IN + 1],
                                                         rms_inv[:, 0:L], ALU.mult, ALU.mult)
                    if k % 8 == 7:
                        ins.then_inc(rms_done, 1)
                for half in range(2):
                    s = slice(half * KT // 2, (half + 1) * KT // 2)
                    dve.wait_ge(xhi_ready, half + 1)
                    nc.vector.tensor_tensor(xl[:, s], x0[:, s], xh[:, s].bitcast(F32),
                                            ALU.subtract).then_inc(xlo_ready, 1)

    shifted = {k: sem(f"shifted_{k}") for k in "lkrvg"}
    lmu_in, lora_ready = sem("lmu_in"), sem("lora_ready")
    lora_copied, prm_copied = sem("lora_copied"), sem("prm_copied")
    z_ready, z_used, cum_ready, exps_ready = sem("z_ready"), sem("z_used"), sem("cum_ready"), sem("exps_ready")
    ksq_ready, n2_ready, n2_held, norm_ready = sem("ksq_ready"), sem("n2_ready"), sem("n2_held"), sem("norm_ready")
    rkm_ready, bonus_ready, gexp_ready, cg_ready = (
        sem("rkm_ready"), sem("bonus_ready"), sem("gexp_ready"), sem("cg_ready"))
    first_consts = sem("first_consts")
    FIRST_CHAIN = 30

    with ExitStack() as ph:
        st = Stream(ph, "a")
        lora = sbuf(ph, "lora_sb", [P, CH])
        lmu = sbuf(ph, "lmu_sb", [P, 1])
        low = sbuf(ph, "low", [P, L])
        lora_i = sbuf(ph, "lora_i", [P, P])
        pi = sbuf(ph, "pi", [P, NPRM + 2])
        pre = {k: sbuf(ph, f"pre_{k}", [P, L + 1]) for k in "lkrvg"}
        names = "dd kx rx ez ea cum pex ec enc eex ksq nrm kkn km tk"
        t = {n: sbuf(ph, f"t_{n}", [P, LP]) for n in names.split()}
        lw = sbuf(ph, "lw", [P, LP])
        reset = sbuf(ph, "reset", [P, LP])
        eg = sbuf(ph, "eg", [P, L])
        cv = sbuf(ph, "cv", [P, SEQ])
        t["av"], t["gx"], t["kb"] = t["ea"], t["rx"], t["ez"]
        pC, uu = t["ksq"][:, 0:L], t["cum"][:, 0:L]
        pgc, egc = pre["l"][:, 0:SEQ], eg[:, 0:SEQ]
        order = [1, 0, 2, 3, 5, 6, 4, 7]
        w_in = A["w_in"].rearrange("(k p) n -> p k n", p=P)

        def col(kind):
            return kind * CH if kind < 4 else RW_COLS + (kind - 4) * CH

        def rounds(eng, body, ch=None, per=0):
            body(0, At(U_IN))
            n0 = ch.n if ch else 0
            with eng.Fori(1, CT - 1) as i:
                if ch:
                    ch.n = n0 - per
                    ch.enter(i, per)
                body(i, At(U_IN, [(i, PER_TILE)]))
                if ch:
                    ch.leave(CT - 1)
            body(CT - 1, At(U_IN + (CT - 1) * PER_TILE), last=True)

        def split_ahead(step, at, h, last):
            j = 2 * at.u + h + AHEAD
            if not (last and j >= 2 * U_WOUT):
                step(At(j // 2, at.loops), j % 2)

        with nc.Block() as block:
            @block.sync
            def _(sp):
                st.load_columns(sp, At(U_LORA), w_in, slice(4 * CH, 4 * CH + P))
                sp.dma_start(lmu[:], A["lmu"]).then_inc(lmu_in, 16)
                sp.dma_start(lora[:], A["lora"]).then_inc(lmu_in, 16)

                def body(i, at, last=False):
                    for n, kind in enumerate(order):
                        cols = (slice(col(kind) + i * P, col(kind) + (i + 1) * P) if isinstance(i, int)
                                else bass.ds((i + col(kind) // P) * P, P))
                        st.load_columns(sp, at + n, w_in, cols)
                rounds(sp, body)

            @block.tensor
            def _(pe):
                pe.wait_ge(xlo_ready, 2)
                st.unit(pe, At(U_LORA), L, xh, xl)
                pe.wait_ge(lora_ready, 2)

                def body(i, at, last=False):
                    pe.wait_ge(lora_copied, i + 1)
                    wait(pe, z_used, 2 * i)
                    for e in range(2):
                        r = slice(64 * e, 64 * e + 64)
                        mm = nc.tensor.matmul(psum[2 + e][:, 0:L], lora_i[r, :], low[r, :], start=True, stop=True)
                    mm.then_inc(z_ready, 1)
                    for n in range(PER_TILE):
                        st.unit(pe, at + n, L, xh, xl)
                        if n == 1:
                            pe.wait_ge(ksq_ready, i + 1)
                            nc.tensor.matmul(psum[4][:, 0:L], blk[:], t["ksq"][:, 0:L], start=True,
                                             stop=True).then_inc(n2_ready, 1)
                        if n == 2:
                            pe.wait_ge(rkm_ready, i + 1)
                            nc.tensor.matmul(psum[5][:, 0:L], blk[:], t["tk"][:, 0:L], start=True,
                                             stop=True).then_inc(bonus_ready, 1)
                rounds(pe, body)

            @block.scalar
            def _(act):
                ch = chain(act, "act")
                a = nc.scalar
                for j in range(AHEAD):
                    st.split_hi(act, At(j // 2), j % 2)
                for h in range(2):
                    split_ahead(lambda q, hh: st.split_hi(act, q, hh), At(U_LORA), h, False)
                computed(act, At(U_LORA))
                act.wait_ge(first_consts, 1)
                a.activation(pre["l"][:, 1:L + 1], GB[0][:, 0:L], ACT.Copy).then_inc(taken[0], 1)
                act.wait_ge(shifted["l"], 1)
                a.activation(low[0:64, :], pre["l"][0:64, 0:L], ACT.Tanh).then_inc(lora_ready, 1)
                a.activation(low[64:128, :], pre["l"][64:128, 0:L], ACT.Copy).then_inc(lora_ready, 1)

                def body(i, at, last=False):
                    src = lora[:, i * P:(i + 1) * P] if isinstance(i, int) else lora[:, bass.ds(i * P, P)]
                    wait(act, z_ready, i)
                    if isinstance(i, int) and i == 0:
                        act.wait_ge(lmu_in, 32)
                    a.activation(lora_i[:], src, ACT.Copy).then_inc(lora_copied, 1)
                    for n in range(PER_TILE):
                        q = at + n
                        for h in range(2):
                            split_ahead(lambda r, hh: st.split_hi(act, r, hh), q, h, last)
                            if n == 0 and h == 0:
                                act.wait_ge(prm_copied, 2 * i + 2)
                                act.wait_ge(z_ready, i + 1)
                                a.activation(t["ez"][:, 0:L], psum[2][:, 0:L], ACT.Exp, bias=pi[:, NPRM:NPRM + 1],
                                             scale=-1.0).then_inc(z_used, 1)
                                a.activation(t["ea"][:, 0:L], psum[3][:, 0:L], ACT.Exp,
                                             bias=pi[:, NPRM + 1:NPRM + 2], scale=-1.0).then_inc(z_used, 1)
                        b = GB[q.bank()]
                        if n < 4:
                            computed(act, q)
                            a.activation(pre["krvg"[n]][:, 1:L + 1], b[:, 0:L], ACT.Copy).then_inc(taken[q.bank()], 1)
                        if n == 0:
                            act.wait_ge(shifted["k"], i + 1)
                            a.activation(t["ksq"][:, 0:L], t["kx"][:, 0:L], ACT.Square,
                                         scale=pi[:, KK:KK + 1]).then_inc(ksq_ready, 1)
                            act.wait_ge(cum_ready, 2 * i + 2)
                            a.activation(t["ec"][:], t["cum"][:], ACT.Exp).then_inc(exps_ready, 1)
                            a.activation(t["enc"][:], t["cum"][:], ACT.Exp, scale=-1.0).then_inc(exps_ready, 1)
                            a.activation(t["eex"][:], t["pex"][:], ACT.Exp).then_inc(exps_ready, 1)
                        if n == 2:
                            act.wait_ge(n2_held, i + 1)
                            a.activation(t["nrm"][:, 0:L], t["nrm"][:, 0:L], ACT.Sqrt).then_inc(norm_ready, 1)
                        if n == 3:
                            act.wait_ge(shifted["g"], i + 1)
                            a.activation(eg[:], t["gx"][:, 0:L], ACT.Exp, scale=-1.0).then_inc(gexp_ready, 1)
                        if n == 4:
                            computed(act, q)
                            a.activation(pC, b[:, 0:L], ACT.Copy).then_inc(taken[q.bank()], 1)
                        if n == 7:
                            computed(act, q)
                            a.activation(pgc, b[:, META:L], ACT.Copy).then_inc(cg_ready, 1)
                            a.activation(egc, b[:, META:L], ACT.Exp, scale=-1.0).then_inc(taken[q.bank()], 1)
                rounds(act, body)

            @block.vector
            def _(dve):
                ch = chain(dve, "dve")
                v = nc.vector
                tt, ts, stt = v.tensor_tensor, v.tensor_scalar, v.scalar_tensor_tensor
                ch(v.memset(reset[:], 1.0))
                ch(v.memset(lw[:], 0.0))
                for n in ("kx", "rx", "kkn", "ez", "km"):
                    ch(v.memset(t[n][:], 0.0))
                for k in "krvg":
                    ch(v.memset(pre[k][:, 0:1], 0.0))
                ch.settle()
                ch(v.memset(reset[:].rearrange("p (c t) -> p c t", t=C)[:, :, 0], 0.0))
                v.memset(pre["l"][:, 0:1], 0.0).then_inc(first_consts, 1)

                for j in range(AHEAD):
                    st.split_lo(dve, At(j // 2), j % 2)
                for h in range(2):
                    split_ahead(lambda q, hh: st.split_lo(dve, q, hh), At(U_LORA), h, False)

                def shift(k, mu, dst, step, seen):
                    seen()
                    ch.link(tt(t["dd"][:, 0:L], pre[k][:, 0:L], pre[k][:, 1:L + 1], ALU.subtract))
                    stt(dst, t["dd"][:, 0:L], mu, pre[k][:, 1:L + 1], ALU.mult, ALU.add).then_inc(shifted[k], 1)

                dve.wait_ge(taken[0], 1)
                dve.wait_ge(first_consts, 1)
                dve.wait_ge(lmu_in, 32)
                ch.link(tt(t["dd"][:, 0:L], pre["l"][:, 0:L], pre["l"][:, 1:L + 1], ALU.subtract))
                ch.link(stt(t["tk"][:, 0:L], t["dd"][:, 0:L], lmu[:, 0:1], pre["l"][:, 1:L + 1], ALU.mult, ALU.add))
                v.tensor_copy(pre["l"][:, 0:L], t["tk"][:, 0:L]).then_inc(shifted["l"], 1)

                def body(i, at, last=False):
                    one = slice(i, i + 1) if isinstance(i, int) else bass.ds(i, 1)

                    def tile(x):
                        return x[:, one]
                    if isinstance(i, int) and i == 0:
                        dve.wait_ge(prm_in, 16)
                    wait(dve, norm_ready, i)
                    v.tensor_copy(pi[:, 0:NPRM], prm[:, one, :].rearrange("p a n -> p (a n)")).then_inc(prm_copied, 1)
                    dve.wait_ge(prm_copied, 2 * i + 1)
                    ts(pi[:, NPRM:NPRM + 2], pi[:, W0:W0 + 2], -1.0, None, ALU.mult).then_inc(prm_copied, 1)

                    def p(n):
                        return pi[:, n:n + 1]
                    for n in range(PER_TILE):
                        q = at + n
                        for h in range(2):
                            split_ahead(lambda r, hh: st.split_lo(dve, r, hh), q, h, last)
                        b = GB[q.bank()]

                        def seen():
                            dve.wait_ge(taken[q.bank()], q.evacuated())
                        if n == 0:
                            dve.wait_ge(z_used, 2 * i + 2)
                            ch(ts(t["ez"][:, 0:L], t["ez"][:, 0:L], 1.0, None, ALU.add))
                            ch.link(ts(t["ea"][:, 0:L], t["ea"][:, 0:L], 1.0, None, ALU.add))
                            ch(v.reciprocal(t["ez"][:, 0:L], t["ez"][:, 0:L]))
                            ch.link(v.reciprocal(t["av"][:, 0:L], t["ea"][:, 0:L]))
                            ch.link(ts(lw[:, 0:L], t["ez"][:, 0:L], -float(np.exp(-0.5)), None, ALU.mult))
                            v.tensor_tensor_scan(t["cum"][:], reset[:], lw[:], 0.0, ALU.mult,
                                                 ALU.add).then_inc(cum_ready, 1)
                            dve.wait_ge(cum_ready, 2 * i + 1)
                            tt(t["pex"][:], t["cum"][:], lw[:], ALU.subtract).then_inc(cum_ready, 1)
                            shift("k", p(MU_K), t["kx"][:, 0:L], i, seen)
                            ch.link(ts(t["tk"][:, 0:L], t["av"][:, 0:L], -1.0, p(KA), ALU.add, ALU.mult))
                            dve.wait_ge(shifted["k"], i + 1)
                            ch.link(stt(t["km"][:, 0:L], t["tk"][:, 0:L], 1.0, t["kx"][:, 0:L], ALU.add, ALU.mult))
                        if n == 1:
                            shift("r", p(MU_R), t["rx"][:, 0:L], i, seen)
                            dve.wait_ge(shifted["r"], i + 1)
                            stt(t["tk"][:, 0:L], t["rx"][:, 0:L], p(RK), t["km"][:, 0:L], ALU.mult,
                                ALU.mult).then_inc(rkm_ready, 1)
                            dve.wait_ge(exps_ready, 3 * i + 3)
                            ch(tt(kr[:, one, 1, :].rearrange("p a t -> p (a t)"), t["rx"][:], t["ec"][:], ALU.mult))
                            ch(tt(bk[:, one, 1, :].rearrange("p a t -> p (a t)"), t["km"][:], t["enc"][:], ALU.mult))
                            ch(v.tensor_copy(pc[:, one, :].rearrange("p a c -> p (a c)"),
                                             t["ec"][:].rearrange("p (c t) -> p c t", t=C)[:, :, C - 1]))
                        if n == 2:
                            shift("v", p(MU_V), vv[:, one, 0:L].rearrange("p a t -> p (a t)"), i, seen)
                            dve.wait_ge(n2_ready, i + 1)
                            ts(t["nrm"][:, 0:L], psum[4][:, 0:L], 1e-24, None, ALU.max).then_inc(n2_held, 1)
                        if n == 3:
                            shift("g", p(MU_G), t["gx"][:, 0:L], i, seen)
                            dve.wait_ge(norm_ready, i + 1)
                            ch.link(v.reciprocal(t["nrm"][:, 0:L], t["nrm"][:, 0:L]))
                            ch.link(stt(t["kkn"][:, 0:L], t["kx"][:, 0:L], p(KK), t["nrm"][:, 0:L], ALU.mult, ALU.mult))
                            ch(tt(kr[:, one, 0, :].rearrange("p a t -> p (a t)"), t["kkn"][:], t["eex"][:], ALU.mult))
                            ch.link(tt(t["kb"][:, 0:L], t["kkn"][:, 0:L], t["av"][:, 0:L], ALU.mult))
                            ch(tt(bk[:, one, 0, :].rearrange("p a t -> p (a t)"), t["kb"][:], t["enc"][:], ALU.mult))
                            dve.wait_ge(bonus_ready, i + 1)
                            dve.wait_ge(shifted["v"], i + 1)
                            ch(tt(bon[:, one, :].rearrange("p a t -> p (a t)"), psum[5][:, META:L],
                                  vv[:, one, META:L].rearrange("p a t -> p (a t)"), ALU.mult))
                        if n == 4:
                            dve.wait_ge(gexp_ready, i + 1)
                            ch.link(ts(eg[:], eg[:], 1.0, None, ALU.add))
                            ch.link(v.reciprocal(eg[:], eg[:]))
                            ch(tt(gs[:, one, :].rearrange("p a t -> p (a t)"), eg[:, META:L], t["gx"][:, META:L],
                                  ALU.mult))
                        if n == 5:
                            computed(dve, q)
                            dve.wait_ge(taken[(q.u - 1) % 2], (q + -1).evacuated())
                            tt(uu, b[:, 0:L], pC, ALU.mult).then_inc(taken[q.bank()], 1)
                            seen()
                            ch.link(ts(cv[:], uu[:, META - 2:L - 2], p(CW0), None, ALU.mult))
                            ch.link(stt(cv[:], uu[:, META - 1:L - 1], p(CW1), cv[:], ALU.mult, ALU.add))
                            ch.link(stt(cv[:], uu[:, META:L], p(CW2), cv[:], ALU.mult, ALU.add))
                        if n == 6:
                            computed(dve, q)
                            tt(cv[:], b[:, META:L], cv[:], ALU.mult).then_inc(taken[q.bank()], 1)
                        if n == 7:
                            seen()
                            ch.link(ts(egc, egc, 1.0, None, ALU.add))
                            ch.link(v.reciprocal(egc, egc))
                            dve.wait_ge(cg_ready, i + 1)
                            ch.link(tt(egc, egc, pgc, ALU.mult))
                            dve.wait_ge(taken[(q.u - 1) % 2], (q + -1).evacuated())
                            ch(tt(yb[:, one, :].rearrange("p a t -> p (a t)"), egc, cv[:], ALU.mult))
                rounds(dve, body, ch, FIRST_CHAIN)
    p01.close()
    if dbg:
        with nc.Block() as block:
            @block.sync
            def _(sp):
                n = 0
                for name, s in (("kr", kr), ("bk", bk), ("vv", vv), ("gs", gs), ("bon", bon), ("pc", pc), ("yb", yb)):
                    if name in dbg:
                        sp.dma_start(dbg[name], s[:]).then_inc(stored, 16)
                        n += 16
                sp.wait_ge(stored, n)
    if stop <= 1:
        first.close()
        return

    pair_ready, pair_taken = sem("pair_ready"), sem("pair_taken")
    aab_out = [sem(f"aab_out{i}") for i in range(NT)]
    sys_in, sys_out = sem("sys_in"), sem("sys_out")
    aab_d = nc.dram_tensor("aab_scratch", [NCH, HEADS, C, C], F32, kind="Internal").ap()
    inv_d = nc.dram_tensor("inv_scratch", [NCH, HEADS, C, C], F32, kind="Internal").ap()
    NA = P // HEADS

    p2 = ExitStack()
    ark = sbuf(p2, "ark", [TT, NT, HEADS, 3, TT])
    with ExitStack() as ph:
        aab = [sbuf(ph, f"aab{i}", [TT, HEADS, TT]) for i in range(2)]
        sa = [sbuf(ph, "sa0", [P, C, C]), sbuf(ph, "sa1", [HEADS, C, C])]
        sx = [sbuf(ph, "sx0", [P, C, C]), sbuf(ph, "sx1", [HEADS, C, C])]
        prod = sbuf(ph, "prod", [P, C, C])
        rows = [P, HEADS]
        real = [C, L - NA * C]

        with nc.Block() as block:
            @block.tensor
            def _(pe):
                for n in range(NT * CT):
                    i, p = divmod(n, CT)
                    wait(pe, pair_taken, n - 1)
                    for e in range(2):
                        for kind in range(2):
                            r = slice(64 * e, 64 * e + 64)
                            mm = nc.tensor.matmul(psum[2 * (n % 2) + e][0:TT, kind * 2 * TT:(kind + 1) * 2 * TT],
                                                  bk[r, p, kind, TT * i:TT * i + TT],
                                                  kr[r, p, :, TT * i:TT * i + TT], start=True, stop=True)
                    mm.then_inc(pair_ready, 1)

            @block.vector
            def _(dve):
                ch = chain(dve, "dve")
                tt = nc.vector.tensor_tensor
                for s in range(2):
                    ch.link(nc.vector.memset(sx[s][:], 0.0))
                    ch(nc.vector.memset(sx[s][:].rearrange("p a b -> p (a b)")[:, 0:C * C:C + 1], -1.0))
                for n in range(NT * CT):
                    i, p = divmod(n, CT)
                    if p == 0 and i >= 2:
                        dve.wait_ge(aab_out[i - 2], 16 * TC)
                    dve.wait_ge(pair_ready, n + 1)
                    for e in range(2):
                        b = psum[2 * (n % 2) + e][0:TT, 0:4 * TT].rearrange("p (k t) -> p k t", k=4)
                        ch(tt(aab[i % 2][:, 2 * p + e], b[:, 0], mask[:, 0], ALU.mult))
                        ins = tt(ark[:, i, 2 * p + e], b[:, 1:4], mask[:, 1:4], ALU.mult)
                        if e == 0:
                            ch(ins)
                        else:
                            ins.then_inc(pair_taken, 1)
                for s in range(2):
                    dve.wait_ge(sys_in, 16 * (s + 1))
                    x, a, r = sx[s], sa[s], rows[s]
                    for t_ in range(1, real[s]):
                        at = a[0:r, 0:t_, t_].rearrange("p (o s) -> p o s", o=1).broadcast_to([r, t_, t_])
                        ch.link(tt(prod[0:r, 0:t_, 0:t_], x[0:r, 0:t_, 0:t_], at, ALU.mult))
                        ch.link(nc.vector.tensor_reduce(x[0:r, 0:t_, t_], prod[0:r, 0:t_, 0:t_], AX_X, ALU.add))
                    nc.vector.tensor_copy(x[0:1, 0:1, 0:1], x[0:1, 0:1, 0:1]).then_inc(sys_out, 1)

            @block.sync
            def _(sp):
                for i in range(NT):
                    sp.wait_ge(pair_taken, CT * (i + 1))
                    for c in range(TC):
                        w = slice(C * c, C * c + C)
                        sp.dma_start(aab_d[TC * i + c].rearrange("h s t -> s h t"),
                                     aab[i % 2][w, :, w]).then_inc(aab_out[i], 16)
                for i in range(NT):
                    sp.wait_ge(aab_out[i], 16 * TC)
                sp.dma_start(sa[0][:], aab_d[0:NA].rearrange("c h s t -> (c h) s t")).then_inc(sys_in, 16)
                sp.wait_ge(sys_in, 16)
                sp.dma_start(sa[1][:], aab_d[NA]).then_inc(sys_in, 16)
                sp.wait_ge(sys_out, 1)
                sp.dma_start(inv_d[0:NA].rearrange("c h s t -> (c h) s t"), sx[0][:]).then_inc(stored, 16)
                sp.wait_ge(sys_out, 2)
                sp.dma_start(inv_d[NA], sx[1][:]).then_inc(stored, 16)
                sp.wait_ge(stored, 32)

    zeroed, inv_in, tm_ready, tm_taken = sem("zeroed"), sem("inv_in"), sem("tm_ready"), sem("tm_taken")
    wn_ready, wn_taken, rt_ready = sem("wn_ready"), sem("wn_taken"), sem("rt_ready")
    z_sum, z_taken, u0_sum, u0_taken = sem("z_sum"), sem("z_taken"), sem("u0_sum"), sem("u0_taken")
    bkp_ready, bkt_ready, bks_ready, v_stacked = sem("bkp_ready"), sem("bkt_ready"), sem("bks_ready"), sem("v_stacked")
    uy_sum, u_ready, y_taken, u_kept, sp_ready = (
        sem("uy_sum"), sem("u_ready"), sem("y_taken"), sem("u_kept"), sem("sp_ready"))
    st_sum, st_ready, out_sum, out_taken = sem("st_sum"), sem("st_ready"), sem("out_sum"), sem("out_taken")
    mean_sum, var_sum, sq_ready, root_ready, cent_ready = (
        sem("mean_sum"), sem("var_sum"), sem("sq_ready"), sem("root_ready"), sem("cent_ready"))

    yT = sbuf(p2, "yT", [P, CT, LP])
    with ExitStack() as ph:
        inv = sbuf(ph, "inv", [TT, HEADS, TT])
        ktm, vtm, utm, ytm = (sbuf(ph, n, [TT, CH]) for n in ("ktm", "vtm", "utm", "ytm"))
        zz, u0 = sbuf(ph, "zz", [TT, CH]), sbuf(ph, "u0", [TT, CH])
        wr = sbuf(ph, "wr", [P, CT, TC, 2 * C])
        bkp = [sbuf(ph, f"bkp{i}", [P, CT, 2 * C]) for i in range(2)]
        bks = [sbuf(ph, f"bks{i}", [2 * C, CH]) for i in range(2)]
        uv = [sbuf(ph, f"uv{i}", [2 * C, CH]) for i in range(2)]
        S = sbuf(ph, "S", [P, CT, P])
        Sp = sbuf(ph, "Sp", [P, CT, HD])
        sq = [sbuf(ph, f"ysq{i}", [P, SEQ]) for i in range(2)]
        root = [sbuf(ph, f"yroot{i}", [P, SEQ]) for i in range(2)]
        out_part, y_done = sem("out_part"), sem("y_done")

        with nc.Block() as block:
            @block.sync
            def _(sp):
                sp.wait_ge(zeroed, 1)
                for i in range(NT):
                    wait(sp, out_sum, i)
                    for c in range(TC):
                        w = slice(C * c, C * c + C)
                        sp.dma_start(inv[w, :, w], inv_d[TC * i + c].rearrange("h s t -> s h t")).then_inc(inv_in, 16)

            @block.gpsimd
            def _(pool):
                g = nc.gpsimd
                g.memset(inv[:], 0.0).then_inc(zeroed, 1)
                g.memset(S[:], 0.0).then_inc(zeroed, 1)
                for i in range(NT):
                    wait(pool, uy_sum, 2 * TC * i)
                    g.tensor_copy(wr[:, :, :, C:2 * C],
                                  kr[:, :, 1, TT * i:TT * i + TT].rearrange("p a (c t) -> p a c t", c=TC)).then_inc(rt_ready, 1)
                    for c in range(TC):
                        m = TC * i + c
                        wait(pool, bkt_ready, 2 * (m - 1))
                        g.tensor_tensor(bkp[m % 2][:].rearrange("p a (k t) -> p a k t", k=2), bk[:, :, :, C * m:C * m + C],
                                        pc[:, :, m:m + 1].rearrange("p a (o q) -> p a o q", o=1).broadcast_to([P, CT, 2, C]),
                                        ALU.mult).then_inc(bkp_ready, 1)

            @block.tensor
            def _(pe):
                tr, mmul = nc.tensor.transpose, nc.tensor.matmul
                for i in range(NT):
                    w = slice(TT * i, TT * i + TT)
                    wait(pe, out_taken, CT * i)
                    for q in range(4):
                        for p in range(4):
                            src = kr[:, 4 * (q % 2) + p, 0, w] if q < 2 else vv[:, 4 * (q % 2) + p, w]
                            last = tr(psum[q][0:TT, P * p:P * p + P], src, ident[:])
                        last.then_inc(tm_ready, 1)
                    pe.wait_ge(inv_in, 16 * TC * (i + 1))
                    for q in range(4):
                        pe.wait_ge(tm_taken, 4 * i + 1 + q // 2)
                        for j in range(2):
                            p = 2 * q + j
                            last = mmul(psum[4 + q][:, 2 * TT * j:2 * TT * j + 2 * TT], ktm[:, P * p:P * p + P],
                                        inv[:, 2 * p:2 * p + 2, :], start=True, stop=True)
                        last.then_inc(wn_ready, 1)
                    pe.wait_ge(tm_taken, 4 * i + 4)
                    for q in range(2):
                        for h in range(8 * q, 8 * q + 8):
                            last = mmul(psum[q][0:TT, HD * (h % 8):HD * (h % 8) + HD], ark[:, i, h, 1, :],
                                        vtm[:, HD * h:HD * h + HD], start=True, stop=True)
                        last.then_inc(z_sum, 1)
                    for q in range(2):
                        pe.wait_ge(z_taken, 2 * i + q + 1)
                        for h in range(8 * q, 8 * q + 8):
                            last = mmul(psum[2 + q][0:TT, HD * (h % 8):HD * (h % 8) + HD], inv[:, h, :],
                                        zz[:, HD * h:HD * h + HD], start=True, stop=True)
                        last.then_inc(u0_sum, 1)
                    for c in range(TC):
                        m = TC * i + c
                        if m < NCH - 1:
                            pe.wait_ge(bkp_ready, m + 1)
                            if c == 0:
                                pe.wait_ge(wn_taken, 8 * (i + 1))
                            else:
                                pe.wait_ge(bks_ready, 2 * m)
                            for q in range(2):
                                for p in range(4):
                                    last = tr(psum[6 + q][0:2 * C, P * p:P * p + P], bkp[m % 2][:, 4 * q + p, :], ident[:])
                                last.then_inc(bkt_ready, 1)
                        pe.wait_ge(rt_ready, i + 1)
                        pe.wait_ge(zeroed, 2)
                        pe.wait_ge(wn_taken, 8 * (i + 1))
                        if c == 0:
                            pe.wait_ge(z_taken, 2 * i + 2)
                        for q in range(2):
                            wait(pe, st_ready, 4 * m - 2 + 2 * q)
                            wait(pe, y_taken, 2 * m - 1 + q)
                            wait(pe, u_ready, 2 * m - 1 + q)
                            for p in range(4 * q, 4 * q + 4):
                                last = mmul(psum[q][0:2 * C, P * (p % 4):P * (p % 4) + P], wr[:, p, c, :], S[:, p, :],
                                            start=True, stop=True)
                            last.then_inc(uy_sum, 1)
                        if m < NCH - 1:
                            pe.wait_ge(v_stacked, m + 1)
                            for q in range(2):
                                pe.wait_ge(bks_ready, 2 * m + q + 1)
                                pe.wait_ge(u_ready, 2 * m + q + 1)
                                for p in range(4 * q, 4 * q + 4):
                                    last = mmul(psum[4 + q][:, P * (p % 4):P * (p % 4) + P], bks[m % 2][:, P * p:P * p + P],
                                                uv[m % 2][:, P * p:P * p + P], start=True, stop=True)
                                last.then_inc(st_sum, 1)
                    pe.wait_ge(u_kept, TC * (i + 1))
                    pe.wait_ge(y_taken, 2 * TC * (i + 1))
                    if i < NT - 1:
                        pe.wait_ge(st_ready, 4 * TC * (i + 1))
                    pe.wait_ge(u0_taken, 2 * (i + 1))
                    two = ident[0:TT, 0:TT].rearrange("p (o t) -> p o t", o=1).broadcast_to([TT, 2, TT])
                    for q in range(4):
                        for j in range(2):
                            p = 2 * q + j
                            o = psum[[2, 3, 4, 5][q]][:, 2 * TT * j:2 * TT * j + 2 * TT]
                            pw = slice(P * p, P * p + P)
                            mmul(o, utm[:, pw], ark[:, i, 2 * p:2 * p + 2, 0, :], start=True, stop=False)
                            mmul(o, vtm[:, pw], ark[:, i, 2 * p:2 * p + 2, 2, :], start=False, stop=False)
                            last = mmul(o, ytm[:, pw], two, start=False, stop=True)
                        if q < 3:
                            last.then_inc(out_part, 1)
                    last.then_inc(out_sum, 1)
                pe.wait_ge(out_taken, CT * NT)
                for p in range(CT):
                    wait(pe, cent_ready, p - 1)
                    mmul(psum[p % 2][:, 0:SEQ], blk[:], yT[:, p, META:L], start=True, stop=True).then_inc(mean_sum, 1)
                    pe.wait_ge(sq_ready, p + 1)
                    wait(pe, root_ready, p - 1)
                    mmul(psum[2 + p % 2][:, 0:SEQ], blk[:], sq[p % 2][:], start=True, stop=True).then_inc(var_sum, 1)

            @block.scalar
            def _(act):
                cp = lambda o, i: nc.scalar.activation(o, i, ACT.Copy)
                for i in range(NT):
                    wait(act, out_sum, i)
                    for q in range(4):
                        act.wait_ge(tm_ready, 4 * i + q + 1)
                        cp((ktm if q < 2 else vtm)[:, 512 * (q % 2):512 * (q % 2) + 512], psum[q][0:TT, :]).then_inc(tm_taken, 1)
                    for q in range(4):
                        act.wait_ge(wn_ready, 4 * i + q + 1)
                        for e in range(2):
                            r = slice(64 * e, 64 * e + 64)
                            src = psum[4 + q][r, 0:4 * TT].rearrange("p (j e c t) -> p j e c t", j=2, e=2, t=C)[:, :, e]
                            for j in range(2):
                                ins = cp(wr[r, 2 * q + j, :, 0:C], src[:, j])
                                if j == 1:
                                    ins.then_inc(wn_taken, 1)
                    for c in range(TC):
                        m = TC * i + c
                        if m < NCH - 1:
                            act.wait_ge(tm_taken, 4 * i + 4)
                            wait(act, st_sum, 2 * (m - 1))
                            cp(uv[m % 2][C:2 * C, :], vtm[C * c:C * c + C, :]).then_inc(v_stacked, 1)
                            for q in range(2):
                                act.wait_ge(bkt_ready, 2 * m + q + 1)
                                cp(bks[m % 2][:, 512 * q:512 * q + 512], psum[6 + q][0:2 * C, :]).then_inc(bks_ready, 1)
                        for q in range(2):
                            act.wait_ge(uy_sum, 2 * m + q + 1)
                            cp(ytm[C * c:C * c + C, 512 * q:512 * q + 512], psum[q][C:2 * C, :]).then_inc(y_taken, 1)
                        act.wait_ge(u_ready, 2 * m + 2)
                        cp(utm[C * c:C * c + C, :], uv[m % 2][0:C, :]).then_inc(u_kept, 1)
                    for q in range(4):
                        if q < 3:
                            act.wait_ge(out_part, 3 * i + q + 1)
                        else:
                            act.wait_ge(out_sum, i + 1)
                        src = psum[[2, 3, 4, 5][q]][:, 0:4 * TT].rearrange("p (j e t) -> p j e t", j=2, e=2)
                        for e in range(2):
                            r = slice(64 * e, 64 * e + 64)
                            cp(yT[r, 2 * q:2 * q + 2, TT * i:TT * i + TT], src[r, :, e]).then_inc(out_taken, 1)
                for p in range(CT):
                    act.wait_ge(cent_ready, p + 1)
                    wait(act, var_sum, p - 1)
                    nc.scalar.activation(sq[p % 2][:], yT[:, p, META:L], ACT.Square).then_inc(sq_ready, 1)
                    act.wait_ge(var_sum, p + 1)
                    if p >= 2:
                        act.wait_ge(y_done, p - 1)
                    nc.scalar.activation(root[p % 2][:], psum[2 + p % 2][:, 0:SEQ], ACT.Sqrt, bias=eps[:, 1:2],
                                         scale=1.0 / HD).then_inc(root_ready, 1)

            @block.vector
            def _(dve):
                ch = chain(dve, "dve")
                v = nc.vector
                tt = v.tensor_tensor
                for i in range(NT):
                    for q in range(2):
                        dve.wait_ge(z_sum, 2 * i + q + 1)
                        v.tensor_copy(zz[:, 512 * q:512 * q + 512], psum[q][0:TT, :]).then_inc(z_taken, 1)
                    for q in range(2):
                        dve.wait_ge(u0_sum, 2 * i + q + 1)
                        v.tensor_copy(u0[:, 512 * q:512 * q + 512], psum[2 + q][0:TT, :]).then_inc(u0_taken, 1)
                    dve.wait_ge(zeroed, 2)
                    for c in range(TC):
                        m = TC * i + c
                        if m < NCH - 1:
                            wait(dve, st_ready, 4 * m)
                            for e in range(2):
                                r = slice(64 * e, 64 * e + 64)
                                tt(Sp[r], S[r, :, r], pc[r, :, m:m + 1].broadcast_to([64, CT, HD]), ALU.mult).then_inc(sp_ready, 1)
                        dve.wait_ge(u0_taken, 2 * (i + 1))
                        wait(dve, u_kept, m - 1)
                        for q in range(2):
                            w = slice(512 * q, 512 * q + 512)
                            dve.wait_ge(uy_sum, 2 * m + q + 1)
                            tt(uv[m % 2][0:C, w], psum[q][0:C, :], u0[C * c:C * c + C, w], ALU.add).then_inc(u_ready, 1)
                        if m < NCH - 1:
                            dve.wait_ge(sp_ready, 2 * m + 2)
                            for q in range(2):
                                dve.wait_ge(st_sum, 2 * m + q + 1)
                                for e in range(2):
                                    r = slice(64 * e, 64 * e + 64)
                                    tt(S[r, 4 * q:4 * q + 4, r], psum[4 + q][r, :].rearrange("p (a b) -> p a b", b=P)[:, :, r],
                                       Sp[r, 4 * q:4 * q + 4, :], ALU.add).then_inc(st_ready, 1)
                dve.wait_ge(out_taken, CT * NT)
                for p in range(CT):
                    y = yT[:, p, META:L]
                    dve.wait_ge(mean_sum, p + 1)
                    v.scalar_tensor_tensor(y, psum[p % 2][:, 0:SEQ], -1.0 / HD, y, ALU.mult, ALU.add).then_inc(cent_ready, 1)
                    dve.wait_ge(root_ready, p + 1)
                    ch.link(v.reciprocal(root[p % 2][:], root[p % 2][:]))
                    ch.link(tt(root[p % 2][:], root[p % 2][:], y, ALU.mult))
                    ch.link(v.tensor_scalar(root[p % 2][:], root[p % 2][:], prm[:, p, LG:LG + 1], prm[:, p, LB:LB + 1],
                                            ALU.mult, ALU.add))
                    ch.link(tt(root[p % 2][:], root[p % 2][:], bon[:, p], ALU.add))
                    tt(gs[:, p], root[p % 2][:], gs[:, p], ALU.mult).then_inc(y_done, 1)
    if dbg:
        with nc.Block() as block:
            @block.sync
            def _(sp):
                n = 0
                for name, s_ in (("ya", gs), ("yT", yT)):
                    if name in dbg:
                        sp.dma_start(dbg[name], s_[:]).then_inc(gain_in, 16)
                        n += 16
                sp.wait_ge(gain_in, 16 + n)
    p2.close()
    first.close()
    if stop <= 2:
        return

    x1_in, normed_out = sem("x1_in"), sem("normed_out")
    sc_sum, sc_taken, max_ready, exp_ready, p_ready = (
        sem("sc_sum"), sem("sc_taken"), sem("max_ready"), sem("exp_ready"), sem("p_ready"))
    tr_ready, pt_taken, vt_taken, o_sum, g_copied = (
        sem("tr_ready"), sem("pt_taken"), sem("vt_taken"), sem("o_sum"), sem("g_copied"))
    vt_sum = sem("vt_sum")
    og_ready, oh_ready, ol_ready = sem("og_ready"), sem("oh_ready"), sem("ol_ready")
    table_in, table_ready, masked = sem("table_in"), sem("table_ready"), sem("masked")
    f_in, f_sum, f_abs, f_exp, f_one, f_ln, f_done, f_out = (
        sem("f_in"), sem("f_sum"), sem("f_abs"), sem("f_exp"), sem("f_one"), sem("f_ln"), sem("f_done"), sem("f_out"))
    nf_d = nc.dram_tensor("nf_scratch", [AH, SEQ], F32, kind="Internal").ap()
    SCALE = float(P) ** -0.5
    PER_HEAD = 4
    HEAD_CHAIN = 7

    ph = top.enter_context(ExitStack())
    st = Stream(ph, "b")
    x1 = sbuf(ph, "x1", [P, KT, SEQ])
    xhi = [sbuf(ph, f"xhi{i}", [P, KT, SEQ], F32R) for i in range(2)]
    xlo = [sbuf(ph, f"xlo{i}", [P, KT, SEQ], F32R) for i in range(2)]
    oh = sbuf(ph, "oh", [P, GH, SEQ], F32R)
    ol = sbuf(ph, "ol", [P, GH, SEQ], F32R)
    qT, kT, vT, gT, eg, og = (sbuf(ph, n, [P, SEQ]) for n in ("qT", "kT", "vT", "gT", "egT", "og"))
    vtm = sbuf(ph, "vtm_b", [P, SEQ])
    W3 = 3 * P
    sc, pr, pT = (sbuf(ph, n, [P, W3]) for n in ("sc", "pr", "pT"))
    parts = [slice(0, P), slice(P, W3)]
    table = sbuf(ph, "table", [P, W3])
    causal = sbuf(ph, "causal", [P, P])
    hidden = sbuf(ph, "hidden", [64, 64])
    nfq = sbuf(ph, "nfq", [P, 2])
    stat = sbuf(ph, "stat", [P, 6])
    fw = sbuf(ph, "fw", [P, KT, AH])
    fz = sbuf(ph, "fz", [AH, 4, SEQ])
    fb = sbuf(ph, "fb", [AH, 1])
    f_ones = sbuf(ph, "f_ones", [AH, SEQ])
    SC, PT, VT, OT, FZ, P2 = psum[2:8]

    w_out = A["w_out"].rearrange("(k p) n -> p k n", p=P)
    w_layer = [[A["a_w_in"]] * 4, [A["b_w_in"], A["kv_w"], A["kv_w"], A["b_w_in"]]]
    w_block = [[0, AH, 2 * AH, 3 * AH], [0, 0, AH, AH]]
    w_proj = [A["a_w_out"], A["b_w_out"]]
    rel = A["rel"]
    rms_f, rms_a, rms_kv, rms_o = (Rms(x1[:], mix[:], SEQ) for _ in range(4))
    GR = [GROUPS, GROUPS - 1]

    def place(layer, g, h=None, n=0):
        base = [U_A, U_B][layer] + n
        loops = []
        for reg, per in ((g, PER_GROUP), (h, PER_HEAD)):
            if isinstance(reg, int):
                base += reg * per
            elif reg is not None:
                loops.append((reg, per))
        return At(base, loops)

    def head_no(layer, g, h):
        return g * GH + h + AH * layer

    def layers(eng, layer, head, project, ch=None):
        def group(g):
            if ch:
                ch.n0 = ch.n
            with eng.Fori(0, GH) as h:
                if ch:
                    ch.enter(h, HEAD_CHAIN)
                head(g, h)
                if ch:
                    ch.leave(GH)
            project(g)
        with eng.Fori(0, GR[layer]) as g:
            if ch:
                ch.enter(g, GH * HEAD_CHAIN)
            group(g)
            if ch:
                ch.leave(GR[layer])
        if GR[layer] < GROUPS:
            group(GR[layer])

    def ahead(step, at, h):
        j = 2 * at.u + h + AHEAD
        if at.loops or j < 2 * U_END:
            step(At(j // 2, at.loops), j % 2)

    with nc.Block() as block:
        @block.sync
        def _(sp):
            sp.dma_start(x1[:], A["xt"][:, :, META:L]).then_inc(x1_in, 16)
            with sp.Fori(0, KT // 4) as i:
                for n in range(4):
                    st.load_columns(sp, At(U_WOUT + n, [(i, 4)]), w_out, bass.ds((i * 4 + n) * P, P))
            sp.dma_start(fw[:], A["f_w"].rearrange("(k p) n -> p k n", p=P)).then_inc(f_in, 16)
            sp.dma_start(fb[:], A["f_b"]).then_inc(f_in, 16)
            for layer in range(2):
                def head(g, h):
                    for n in range(4):
                        w = w_layer[layer][n].rearrange("(k p) n -> p k n", p=P)
                        col = (g * GH + h + w_block[layer][n]) * P
                        st.load_columns(sp, place(layer, g, h, n), w, bass.ds(col, P))

                def project(g):
                    w = w_proj[layer].rearrange("(k p) n -> p k n", p=P)
                    for m in range(GH):
                        rows = slice(g * GH, (g + 1) * GH) if isinstance(g, int) else bass.ds(g * GH, GH)
                        st.load(sp, place(layer, g, n=4 * GH + m),
                                lambda half: w[:, rows, P * (2 * m + half):P * (2 * m + half + 1)])
                layers(sp, layer, head, project)
            for half in range(2):
                s = slice(half * KT // 2, (half + 1) * KT // 2)
                sp.wait_ge(rms_done, 11 + half)
                sp.dma_start(A["out"][:, s], mix[:, s]).then_inc(normed_out, 16)
            sp.wait_ge(normed_out, 32)

        @block.gpsimd
        def _(pool):
            g_ = nc.gpsimd
            ch = chain(pool, "pool")
            g_.memset(f_ones[:], 1.0).then_inc(f_in, 1)
            ch(g_.memset(hidden[:], NEG_INF))
            ch.link(g_.memset(causal[:], 0.0))
            ch.link(g_.affine_select(out=causal[:], in_=causal[:], compare_op=ALU.is_ge, fill=NEG_INF, base=0,
                                     pattern=[[-1, P]], channel_multiplier=1))

            for layer in range(2):
                if layer == 1:
                    pool.wait_ge(f_done, 1)
                    pool.dma_start(nf_d, fz[:, 3]).then_inc(f_out, 16)
                    pool.wait_ge(f_out, 16)

                def head(g, h):
                    n = head_no(layer, g, h)
                    pool.wait_ge(sc_taken, n + 1)
                    if layer == 0:
                        row = rel[bass.ds(n, 1), 1:1 + SEQ]
                        src = bass.AP(tensor=row.tensor, offset=row.offset + (N_REL // 2 + P - SEQ), ap=[[1, P], [1, SEQ]])
                        pool.dma_start(table[:, 0:SEQ], src).then_inc(table_in, 16)
                        pool.wait_ge(table_in, n * 16 + 16)
                        g_.tensor_tensor(table[0:64, 0:64], table[0:64, 0:64], hidden[:], ALU.add).then_inc(table_ready, 1)
                    else:
                        m = n - AH
                        row = nf_d[bass.ds(m, 1), :]
                        pool.dma_start(table[:, 0:P], row[:, 0:P].broadcast_to([P, P])).then_inc(table_in, 16)
                        pool.dma_start(table[:, P:W3], row.broadcast_to([P, SEQ])).then_inc(table_in, 16)
                        pool.dma_start(nfq[:], row.rearrange("o (q p) -> p (o q)", p=P),
                                       allow_slow_non_contiguous=True).then_inc(table_in, 16)
                        pool.wait_ge(table_in, m * 48 + (16 * AH + 48))
                        v = table[:].rearrange("p (b k) -> p b k", k=P)[:, 0:3:2]
                        g_.tensor_tensor(v, v, causal[:].rearrange("p (o k) -> p o k", o=1).broadcast_to([P, 2, P]),
                                         ALU.add).then_inc(masked, 1)
                layers(pool, layer, head, lambda g: None)

        @block.tensor
        def _(pe):
            pe.wait_ge(xlo_ready, 4)
            with pe.Fori(0, KT // 4) as i:
                for n in range(4):
                    st.unit(pe, At(U_WOUT + n, [(i, 4)]), SEQ, xhi[1], xlo[1])
            rms_f.pe_bcast(pe, FZ)
            rms_a.pe_bcast(pe, FZ)
            for layer in range(2):
                if layer == 0:
                    pe.wait_ge(xlo_ready, 6)
                    src = [0, 0, 0, 0]
                else:
                    rms_kv.pe_bcast(pe, FZ)
                    pe.wait_ge(rms_done, 10)
                    pe.wait_ge(f_in, 33)
                    pe.wait_ge(rms_root, rms_kv.n)
                    for k in range(KT):
                        mm = nc.tensor.matmul(FZ[0:AH, 0:SEQ], fw[:, k], mix[:, k], start=k == 0, stop=k == KT - 1)
                    mm.then_inc(f_sum, 1)
                    pe.wait_ge(xlo_ready, 10)
                    src = [1, 0, 0, 1]

                def head(g, h):
                    n = head_no(layer, g, h)
                    q, k, v, gg = (place(layer, g, h, m) for m in range(4))

                    def scores():
                        pe.wait_ge(taken[q.bank()], q.evacuated())
                        pe.wait_ge(taken[k.bank()], k.evacuated())
                        nc.tensor.matmul(SC[:, 0:P], qT[:, 0:P], kT[:, 0:P], start=True, stop=True)
                        nc.tensor.matmul(SC[:, P:W3], qT[:, P:SEQ], kT[:], start=True, stop=True).then_inc(sc_sum, 1)

                    def turn_values():
                        pe.wait_ge(taken[v.bank()], v.evacuated())
                        for m in range(2):
                            last = nc.tensor.transpose(VT[:, P * m:P * m + P], vT[:, P * m:P * m + P], ident[:])
                        last.then_inc(vt_sum, 1)

                    def turn_probs():
                        pe.wait_ge(p_ready, n * 2 + 2)
                        for m in range(3):
                            last = nc.tensor.transpose(PT[:, P * m:P * m + P], pr[:, P * m:P * m + P], ident[:])
                        last.then_inc(tr_ready, 1)
                    none = ({}, {})
                    for m, (at, before) in enumerate(((q, none), (k, none), (v, ({4: scores}, {})),
                                                      (gg, ({3: turn_values}, {3: turn_probs})))):
                        st.unit(pe, at, SEQ, xhi[src[m]], xlo[src[m]], before)
                    pe.wait_ge(pt_taken, n + 1)
                    pe.wait_ge(vt_taken, n + 1)
                    pe.wait_ge(og_ready, n + 1)
                    nc.tensor.matmul(OT[:, 0:SEQ], vtm[:, 0:P], pT[:, 0:SEQ], start=True, stop=False)
                    nc.tensor.matmul(OT[:, P:SEQ], vtm[:, P:SEQ], pT[:, SEQ:W3], start=False, stop=True).then_inc(o_sum, 1)

                def project(g):
                    def product(at, half, tiles):
                        out = GB[at.bank()][:, SEQ * half:SEQ * half + SEQ]
                        if half == 1 and len(tiles) < 8:
                            out = P2[:, 0:SEQ]
                        st.product(pe, at, half, out, lambda k: oh[:, k], lambda k: ol[:, k], start=True, stop=True, tiles=tiles)
                    for m in range(GH):
                        at = place(layer, g, n=4 * GH + m)
                        if m == 0:
                            pe.wait_ge(ol_ready, head_no(layer, g, GH - 1))
                            for half in range(2):
                                product(at, half, range(0, 7))
                            pe.wait_ge(ol_ready, head_no(layer, g, GH))
                            for half in range(2):
                                product(at, half, range(7, 8))
                        else:
                            for half in range(2):
                                product(at, half, range(8))
                layers(pe, layer, head, project)
            rms_o.pe_bcast(pe, FZ)

        @block.scalar
        def _(act):
            a = nc.scalar.activation

            def split_hi(at, h):
                st.split_hi(act, at, h)

            def hi_of_x(pair, n):
                for half in range(2):
                    s = slice(half * KT // 2, (half + 1) * KT // 2)
                    act.wait_ge(rms_done, n + half + 1)
                    a(xhi[pair][:, s], mix[:, s], ACT.Copy).then_inc(xhi_ready, 1)
            for half in range(2):
                s = slice(half * KT // 2, (half + 1) * KT // 2)
                a(xhi[1][:, s], mix[:, s], ACT.Copy).then_inc(xhi_ready, 1)
            for j in range(2 * U_WOUT, 2 * U_WOUT + AHEAD):
                split_hi(At(j // 2), j % 2)
            with act.Fori(0, KT // 4) as i:
                for n in range(4):
                    for h in range(2):
                        ahead(split_hi, At(U_WOUT + n, [(i, 4)]), h)
            act.wait_ge(taken[(U_A - 1) % 2], (U_A - 1) // 2 + 1)
            act.wait_ge(taken[U_A % 2], (U_A - 2) // 2 + 1)
            act.wait_ge(xlo_ready, 4)
            rms_f.act_square()
            rms_f.act_root(act, FZ)
            act.wait_ge(rms_done, 4)
            rms_a.act_square()
            rms_a.act_root(act, FZ)
            hi_of_x(0, 4)
            for layer in range(2):
                if layer == 1:
                    act.wait_ge(taken[(U_B - 1) % 2], (U_B - 1) // 2 + 1)
                    act.wait_ge(taken[U_B % 2], (U_B - 2) // 2 + 1)
                    rms_kv.act_square()
                    rms_kv.act_root(act, FZ)
                    hi_of_x(1, 6)
                    hi_of_x(0, 8)
                    act.wait_ge(f_abs, 1)
                    a(fz[:, 2], fz[:, 2], ACT.Exp, scale=-1.0).then_inc(f_exp, 1)
                    act.wait_ge(f_one, 1)
                    a(fz[:, 2], fz[:, 2], ACT.Ln).then_inc(f_ln, 1)

                def head(g, h):
                    n = head_no(layer, g, h)
                    q, k, v, gg = (place(layer, g, h, m) for m in range(4))
                    for at, dst, scale in ((q, qT, SCALE), (k, kT, 1.0), (v, vT, 1.0)):
                        ahead(split_hi, at, 0)
                        ahead(split_hi, at, 1)
                        if dst is vT:
                            act.wait_ge(max_ready, n + 1)
                            for m in range(2):
                                a(pr[:, parts[m]], sc[:, parts[m]], ACT.Exp, bias=stat[:, 2 + m:3 + m],
                                  accum_out=stat[:, 4 + m:5 + m]).then_inc(exp_ready, 1)
                        computed(act, at)
                        a(dst[:], GB[at.bank()][:, 0:SEQ], ACT.Copy, scale=scale).then_inc(taken[at.bank()], 1)
                    ahead(split_hi, gg, 0)
                    act.wait_ge(vt_sum, n + 1)
                    a(vtm[:], VT[:, 0:SEQ], ACT.Copy).then_inc(vt_taken, 1)
                    ahead(split_hi, gg, 1)
                    act.wait_ge(tr_ready, n + 1)
                    a(pT[:], PT[:, 0:W3], ACT.Copy).then_inc(pt_taken, 1)
                    computed(act, gg)
                    b = GB[gg.bank()][:, 0:SEQ]
                    a(gT[:], b, ACT.Copy).then_inc(g_copied, 1)
                    a(eg[:], b, ACT.Exp, scale=-1.0).then_inc(taken[gg.bank()], 1)
                    act.wait_ge(og_ready, n + 2)
                    dst = oh[:, bass.ds(h, 1), :].rearrange("p a t -> p (a t)")
                    a(dst, og[:], ACT.Copy).then_inc(oh_ready, 1)

                def project(g):
                    for m in range(GH):
                        for hh in range(2):
                            ahead(split_hi, place(layer, g, n=4 * GH + m), hh)
                layers(act, layer, head, project)
            act.wait_ge(taken[(U_END - 1) % 2], (U_END - 1) // 2 + 1)
            act.wait_ge(taken[U_END % 2], (U_END - 2) // 2 + 1)
            rms_o.act_square()
            rms_o.act_root(act, FZ)

        @block.vector
        def _(dve):
            ch = chain(dve, "dve")
            v_ = nc.vector
            tt, ts, stt = v_.tensor_tensor, v_.tensor_scalar, v_.scalar_tensor_tensor

            def split_lo(at, h):
                st.split_lo(dve, at, h)

            def apply_gain(col, dst):
                for k in range(KT):
                    ins = stt(dst[:, k], x1[:, k], gain[:, k, col:col + 1], rms_inv[:, 0:SEQ], ALU.mult, ALU.mult)
                    if k % 8 == 7:
                        ins.then_inc(rms_done, 1)

            def lo_of_x(pair, n):
                for half in range(2):
                    s = slice(half * KT // 2, (half + 1) * KT // 2)
                    dve.wait_ge(xhi_ready, n + half + 1)
                    tt(xlo[pair][:, s], mix[:, s], xhi[pair][:, s].bitcast(F32), ALU.subtract).then_inc(xlo_ready, 1)
            v_.memset(stat[:, 0:1], 0.0).then_inc(sc_taken, 1)
            v_.memset(stat[:, 1:2], 0.0).then_inc(og_ready, 1)
            lo_of_x(1, 2)
            for j in range(2 * U_WOUT, 2 * U_WOUT + AHEAD):
                split_lo(At(j // 2), j % 2)
            dve.wait_ge(x1_in, 16)
            with dve.Fori(0, KT // 4) as i:
                for n in range(4):
                    at = At(U_WOUT + n, [(i, 4)])
                    for h in range(2):
                        ahead(split_lo, at, h)
                    computed(dve, at)
                    xs = x1[:, bass.ds(i * 4 + n, 1), :].rearrange("p a t -> p (a t)")
                    tt(xs, GB[at.bank()][:, 0:SEQ], xs, ALU.add).then_inc(taken[at.bank()], 1)
            rms_f.dve_sum(dve)
            rms_f.dve_inverse(dve, ch)
            apply_gain(G_F, x1)
            rms_a.dve_sum(dve)
            rms_a.dve_inverse(dve, ch)
            apply_gain(G_A, mix)
            lo_of_x(0, 4)
            for layer in range(2):
                if layer == 1:
                    rms_kv.dve_sum(dve)
                    rms_kv.dve_inverse(dve, ch)
                    apply_gain(G_B, mix)
                    lo_of_x(1, 6)
                    dve.wait_ge(xlo_ready, 8)
                    apply_gain(G_KV, mix)
                    lo_of_x(0, 8)
                    dve.wait_ge(f_sum, 1)
                    dve.wait_ge(f_in, 33)
                    ch.link(ts(fz[:, 0], FZ[0:AH, 0:SEQ], fb[:, 0:1], None, ALU.add))
                    ch.link(ts(fz[:, 1], fz[:, 0], -1.0, None, ALU.mult))
                    tt(fz[:, 2], fz[:, 0], fz[:, 1], ALU.max).then_inc(f_abs, 1)
                    dve.wait_ge(f_exp, 1)
                    ts(fz[:, 2], fz[:, 2], 1.0, None, ALU.add).then_inc(f_one, 1)
                    dve.wait_ge(f_ln, 1)
                    ch.link(stt(fz[:, 0], fz[:, 1], 0.0, fz[:, 2], ALU.max, ALU.add))
                    v_.tensor_tensor_scan(fz[:, 3], f_ones[:], fz[:, 0], 0.0, ALU.mult, ALU.add).then_inc(f_done, 1)

                def head(g, h):
                    n = head_no(layer, g, h)
                    q, k, v, gg = (place(layer, g, h, m) for m in range(4))
                    for at in (q, k, v):
                        ahead(split_lo, at, 0)
                        if at is not v:
                            ahead(split_lo, at, 1)
                    dve.wait_ge(sc_sum, n + 1)
                    if layer == 0:
                        dve.wait_ge(table_ready, n + 1)
                        ch(tt(sc[:, parts[0]], SC[:, parts[0]], table[:, 0:P][:, ::-1], ALU.add))
                        tt(sc[:, parts[1]], SC[:, parts[1]], table[:, 0:SEQ][:, ::-1], ALU.add).then_inc(sc_taken, 1)
                        dve.wait_ge(sc_taken, n + 2)
                    else:
                        dve.wait_ge(masked, n - AH + 1)
                        for m in range(2):
                            ins = stt(sc[:, parts[m]], table[:, parts[m]], nfq[:, m:m + 1], SC[:, parts[m]],
                                      ALU.subtract, ALU.add)
                            ch(ins) if m == 0 else ins.then_inc(sc_taken, 1)
                        dve.wait_ge(sc_taken, n + 2)
                    ch(v_.tensor_reduce(stat[:, 0:1], sc[:, parts[0]], AX_X, ALU.max))
                    ch.link(v_.tensor_reduce(stat[:, 1:2], sc[:, parts[1]], AX_X, ALU.max))
                    ts(stat[:, 2:4], stat[:, 0:2], -1.0, None, ALU.mult).then_inc(max_ready, 1)
                    ahead(split_lo, v, 1)
                    dve.wait_ge(exp_ready, n * 2 + 2)
                    ch.link(v_.reciprocal(stat[:, 4:6], stat[:, 4:6]))
                    for m in range(2):
                        ts(pr[:, parts[m]], pr[:, parts[m]], stat[:, 4 + m:5 + m], None, ALU.mult).then_inc(p_ready, 1)
                    ahead(split_lo, gg, 0)
                    ahead(split_lo, gg, 1)
                    dve.wait_ge(taken[gg.bank()], gg.evacuated())
                    ch.link(ts(eg[:], eg[:], 1.0, None, ALU.add))
                    ch.link(v_.reciprocal(eg[:], eg[:]))
                    dve.wait_ge(g_copied, n + 1)
                    ch.link(tt(eg[:], eg[:], gT[:], ALU.mult))
                    dve.wait_ge(o_sum, n + 1)
                    tt(og[:], OT[:, 0:SEQ], eg[:], ALU.mult).then_inc(og_ready, 1)
                    dve.wait_ge(oh_ready, n + 1)
                    one = bass.ds(h, 1)
                    tt(ol[:, one, :].rearrange("p a t -> p (a t)"), og[:],
                       oh[:, one, :].rearrange("p a t -> p (a t)").bitcast(F32), ALU.subtract).then_inc(ol_ready, 1)

                def project(g):
                    for m in range(GH):
                        at = place(layer, g, n=4 * GH + m)
                        for hh in range(2):
                            ahead(split_lo, at, hh)
                        computed(dve, at)
                        if m == 0:
                            tt(x1[:, 1], P2[:, 0:SEQ], x1[:, 1], ALU.add)
                            tt(x1[:, 0], GB[at.bank()][:, 0:SEQ], x1[:, 0], ALU.add).then_inc(taken[at.bank()], 1)
                        else:
                            xs = x1[:, 2 * m:2 * m + 2].rearrange("p a t -> p (a t)")
                            tt(xs, GB[at.bank()][:], xs, ALU.add).then_inc(taken[at.bank()], 1)
                layers(dve, layer, head, project, ch)
            rms_o.dve_sum(dve)
            rms_o.dve_inverse(dve, ch)
            apply_gain(G_OUT, mix)


_SPEC = ["xt", "prm", "gain", "lora", "lmu", "w_in", "w_out", "a_w_in", "rel", "a_w_out", "kv_w", "f_w", "f_b",
         "b_w_in", "b_w_out"]


def _layout(i):
    import numpy as _np

    f = _np.ascontiguousarray
    x = _np.concatenate([i["meta_tokens"], i["x"][0]], 0).T

    def tiles(v):
        return _np.reshape(v, (-1, 128)).T
    mu = i["mu_shift"][0]
    conv = i["conv_w"][0]
    per_channel = [mu[1024:2048], mu[0:1024], mu[2048:3072], mu[3072:4096], i["w0"][0], i["a0"][0], i["k_k"][0],
                   i["k_a"][0], i["r_k"][0], conv[0], conv[1], conv[2], i["lnx_g"][0], i["lnx_b"][0]]
    gains = [i[n] for n in ("norm_in_g", "norm_f_g", "a_norm_2", "kv_norm_2", "b_norm_2", "final_norm_2")]
    return {
        "xt": f(x.reshape(16, 128, 272).transpose(1, 0, 2)),
        "prm": f(_np.stack([tiles(v) for v in per_channel], -1)),
        "gain": f(_np.stack([tiles(v) for v in gains], -1)),
        "lora": f(_np.concatenate([i["w_lora_up"][0], i["a_lora_up"][0]], 0)),
        "lmu": f(mu[4096:4224].reshape(128, 1)),
        "w_in": i["w_in"][0], "w_out": i["w_out"][0], "a_w_in": i["a_w_in_2"][0], "rel": i["a_rel_bias_2"][0],
        "a_w_out": i["a_w_out_2"][0], "kv_w": i["kv_w_2"], "f_w": i["f_w_2"], "f_b": i["f_b_2"].reshape(32, 1),
        "b_w_in": i["b_w_in_2"][0], "b_w_out": i["b_w_out_2"][0],
    }


def kernel(**inputs):
    import numpy as _np
    import concourse.bacc as _bacc
    from concourse import mybir as _mybir
    from concourse.bass_utils import run_bass_kernel_spmd as _run

    nc = _bacc.Bacc("TRN2", target_bir_lowering=False, num_devices=1)
    laid = _layout({k: _np.asarray(v) for k, v in inputs.items()})
    arrays, aps = {}, {}
    for name in _SPEC:
        a = _np.ascontiguousarray(laid[name])
        arrays[f"in_{name}_dram"] = a
        aps[name] = nc.dram_tensor(f"in_{name}_dram", a.shape, _mybir.dt.from_np(a.dtype), kind="ExternalInput").ap()
    aps["out"] = nc.dram_tensor("out_dram", (128, 16, 256), _mybir.dt.float32, kind="ExternalOutput").ap()
    fused_blocks(nc, aps)
    r = _run(nc, [arrays], core_ids=[0])
    y = r.results[0]["out_dram"]
    return _np.ascontiguousarray(_np.reshape(_np.transpose(y, (2, 1, 0)), (1, 256, 2048)))
```

```python
from contextlib import ExitStack

import numpy as np

import concourse.bass as bass
from concourse import mybir

F32 = mybir.dt.float32
F32R = mybir.dt.float32r
ALU = mybir.AluOpType
ACT = mybir.ActivationFunctionType
AX_X = mybir.AxisListType.X

P = 128
D = 2048
KT = D // P
SEQ = 256
META = 16
L = SEQ + META
CH = 1024
CT = CH // P
HEADS = 16
HD = 64
LORA = 64
C = 32
NCH = -(-L // C)
LP = NCH * C
TC = 3
TT = TC * C
NT = NCH // TC
RW_COLS = 4 * CH + 2 * LORA
NEG_INF = -1e30

AH = 32
DI = AH * P
GROUPS = 4
GH = AH // GROUPS
N_REL = 513

HALF = 8 * P
RAW = 4
SPL = 4
AHEAD = 3

MU_K, MU_R, MU_V, MU_G, W0, A0, KK, KA, RK, CW0, CW1, CW2, LG, LB = range(14)
NPRM = 14
G_IN, G_F, G_A, G_KV, G_B, G_OUT = range(6)

U_LORA = 0
U_IN = 1
PER_TILE = 8
U_WOUT = U_IN + CT * PER_TILE
PER_GROUP = 4 * GH + GH
U_A = U_WOUT + KT
U_B = U_A + GROUPS * PER_GROUP
U_END = U_B + GROUPS * PER_GROUP


class Chain:

    def __init__(self, eng, sem):
        self.eng, self.sem, self.n, self.dyn, self.began = eng, sem, 0, [], []

    def value(self):
        v = self.n
        for reg, per in self.dyn:
            v = reg * per + v
        return v

    def __call__(self, ins):
        ins.then_inc(self.sem, 1)
        self.n += 1

    def settle(self):
        self.eng.wait_ge(self.sem, self.value())

    def link(self, ins):
        self(ins)
        self.settle()

    def enter(self, reg, per):
        self.dyn.append((reg, per))
        self.began.append(self.n)

    def leave(self, count):
        reg, per = self.dyn.pop()
        began = self.began.pop()
        assert self.n - began == per, f"chain: {self.n - began} steps per round, {per} stated"
        self.n = began + count * per


class At:

    def __init__(self, u, loops=()):
        self.u, self.loops = u, tuple(loops)

    def __add__(self, k):
        return At(self.u + k, self.loops)

    def count(self, value, per_unit=1, per=1):
        v = value
        for reg, units in self.loops:
            v = reg * (units * per_unit // per) + v
        return v

    def bank(self):
        return self.u % 2

    def evacuated(self):
        return self.count(self.u // 2 + 1, 1, 2)


def wait(eng, sem, value):
    if isinstance(value, int) and value <= 0:
        return
    eng.wait_ge(sem, value)


def fused_blocks(nc, A, stop=99, dbg=None):
    with ExitStack() as top:
        _build(nc, A, top, stop, dbg or {})


def _build(nc, A, top, stop, dbg):
    def sbuf(stack, name, shape, dt=F32):
        return stack.enter_context(nc.sbuf_tensor(name, shape, dt))

    def sem(name):
        return top.enter_context(nc.semaphore(name))

    psum = [top.enter_context(nc.psum_tensor(f"bank{i}", [P, 512], F32)) for i in range(8)]
    GB = psum[0:2]

    raw_in = [sem(f"raw_in{i}") for i in range(RAW)]
    hi_ready = sem("hi_ready")
    lo_ready = sem("lo_ready")
    half_used = sem("half_used")
    taken = [sem("taken0"), sem("taken1")]
    stored = sem("stored")
    act_seq, dve_seq, pool_seq = sem("act_seq"), sem("dve_seq"), sem("pool_seq")
    chains = {}

    def chain(eng, name):
        s = {"act": act_seq, "dve": dve_seq, "pool": pool_seq}[name]
        if name not in chains:
            chains[name] = Chain(eng, s)
        chains[name].eng = eng
        return chains[name]

    ident = sbuf(top, "ident", [P, P])
    ones = sbuf(top, "ones", [P, P])
    gain = sbuf(top, "gain", [P, KT, 6])
    eps = sbuf(top, "eps", [P, 2])
    rms_inv = sbuf(top, "rms_inv", [P, L])
    mix = sbuf(top, "mix", [P, 2 * CT, SEQ])
    gs = mix[:, 0:CT]
    yb = mix[:, CT:2 * CT]

    class Stream:
        def __init__(self, stack, tag):
            self.raw = [sbuf(stack, f"raw{tag}{i}", [P, 2 * HALF]) for i in range(RAW)]
            self.hi = [sbuf(stack, f"hi{tag}{i}", [P, HALF], F32R) for i in range(SPL)]
            self.lo = [sbuf(stack, f"lo{tag}{i}", [P, HALF], F32R) for i in range(SPL)]

        def load(self, sp, at, halves):
            wait(sp, lo_ready, at.count(2 * (at.u - RAW) + 2, 2))
            slot = at.u % RAW
            for h in range(2):
                dst = self.raw[slot][:, h * HALF:(h + 1) * HALF].rearrange("p (k n) -> p k n", n=P)
                sp.dma_start(dst, halves(h)).then_inc(raw_in[slot], 16)

        def load_columns(self, sp, at, w, cols):
            self.load(sp, at, lambda h: w[:, 8 * h:8 * h + 8, cols])

        def landed(self, eng, at):
            eng.wait_ge(raw_in[at.u % RAW], at.count(32 * (at.u // RAW + 1), 32, RAW))

        def split_hi(self, act, at, h):
            if h == 0:
                self.landed(act, at)
            wait(act, half_used, at.count(2 * at.u + h - SPL + 1, 2))
            nc.scalar.activation(self.hi[(2 * at.u + h) % SPL][:], self.raw[at.u % RAW][:, h * HALF:(h + 1) * HALF],
                                 ACT.Copy).then_inc(hi_ready, 1)

        def split_lo(self, dve, at, h):
            dve.wait_ge(hi_ready, at.count(2 * at.u + h + 1, 2))
            b = (2 * at.u + h) % SPL
            nc.vector.tensor_tensor(self.lo[b][:], self.raw[at.u % RAW][:, h * HALF:(h + 1) * HALF],
                                    self.hi[b][:].bitcast(F32), ALU.subtract).then_inc(lo_ready, 1)

        def product(self, pe, at, h, out, rhs_hi, rhs_lo, start, stop, tiles=range(8), before=None):
            b = (2 * at.u + h) % SPL
            if start and tiles[0] == 0:
                wait(pe, taken[at.bank()], at.count((at.u - 2) // 2 + 1, 1, 2))
            pe.wait_ge(lo_ready, at.count(2 * at.u + h + 1, 2))
            for k in tiles:
                if before and k in before:
                    before[k]()
                w = slice(k * P, (k + 1) * P)
                nc.tensor.matmul(out, self.hi[b][:, w], rhs_hi(k), start=start and k == 0, stop=False)
                nc.tensor.matmul(out, self.hi[b][:, w], rhs_lo(k), start=False, stop=False)
                last = nc.tensor.matmul(out, self.lo[b][:, w], rhs_hi(k), start=False, stop=stop and k == 7)
            if k == 7:
                last.then_inc(half_used, 1)

        def unit(self, pe, at, width, xh, xl, before=({}, {})):
            for h in range(2):
                self.product(pe, at, h, GB[at.bank()][:, 0:width], lambda k: xh[:, 8 * h + k, 0:width],
                             lambda k: xl[:, 8 * h + k, 0:width], start=h == 0, stop=h == 1, before=before[h])

    def computed(eng, at):
        eng.wait_ge(half_used, at.count(2 * at.u + 2, 2))

    gain_in, prm_in = sem("gain_in"), sem("prm_in")
    x_in = [sem(f"x_in{c}") for c in range(4)]
    rms_sq, rms_bcast, rms_root, rms_done = sem("rms_sq"), sem("rms_bcast"), sem("rms_root"), sem("rms_done")
    xg_ready = sem("xg_ready")
    xhi_ready, xlo_ready = sem("xhi_ready"), sem("xlo_ready")

    first = ExitStack()
    kr = sbuf(first, "kr", [P, CT, 2, LP])
    bk = sbuf(first, "bk", [P, CT, 2, LP])
    vv = sbuf(first, "vv", [P, CT, LP])
    bon = sbuf(first, "bon", [P, CT, SEQ])
    pc = sbuf(first, "pc", [P, CT, NCH])
    prm = sbuf(first, "prm_sb", [P, CT, NPRM])
    blk = sbuf(first, "blk", [P, P])
    mask = sbuf(first, "mask", [TT, 4, TT])

    xh = xl = None
    p01 = ExitStack()
    xh = sbuf(p01, "xh", [P, KT, L], F32R)
    xl = sbuf(p01, "xl", [P, KT, L], F32R)
    x0 = kr[:].rearrange("p a b t -> p (a b t)")[:, 0:KT * L].rearrange("p (k t) -> p k t", k=KT)
    sq0 = bk[:].rearrange("p a b t -> p (a b t)")[:, 0:KT * L].rearrange("p (k t) -> p k t", k=KT)
    XC = 4
    chunks = [slice(c * KT // XC, (c + 1) * KT // XC) for c in range(XC)]

    def setup_loads(sp):
        sp.dma_start(gain[:], A["gain"]).then_inc(gain_in, 16)
        for c in range(XC):
            sp.dma_start(x0[:, chunks[c]], A["xt"][:, chunks[c]]).then_inc(x_in[c], 16)

    def setup_pool(pool):
        ch = chain(pool, "pool")
        g = nc.gpsimd
        ch(g.memset(ones[:], 1.0))
        ch(g.memset(eps[:, 0:1], 1e-6))
        ch(g.memset(eps[:, 1:2], 64e-5))
        ch(g.memset(ident[:], 0.0))
        ch(g.memset(blk[:], 0.0))
        ch(g.memset(mask[:, 0], -1.0))
        ch.link(g.memset(mask[:, 1:4], 1.0))
        pool.wait_ge(gain_in, 16)
        for c in range(XC):
            pool.wait_ge(rms_sq, c + 1)
            g.tensor_tensor(x0[:, chunks[c]], x0[:, chunks[c]],
                            gain[:, chunks[c], G_IN:G_IN + 1].broadcast_to([P, KT // XC, L]),
                            ALU.mult).then_inc(xg_ready, 1)
            pool.wait_ge(xg_ready, c + 1)
        ch.link(g.affine_select(out=ident[:], in_=ident[:], compare_op=ALU.not_equal, fill=1.0, base=0,
                                pattern=[[-1, P]], channel_multiplier=1))
        ch.link(g.memset(blk[0:64, 0:64], 1.0))
        ch.link(g.memset(blk[64:128, 64:128], 1.0))
        for kind in range(4):
            v = mask[:, kind].rearrange("p (c t) -> p c t", c=TC)
            ch.link(g.affine_select(out=v, in_=v, compare_op=ALU.is_ge, fill=0.0, base=kind % 2 - 1,
                                    pattern=[[C, TC], [1, C]], channel_multiplier=-1))
            ch.link(g.affine_select(out=v, in_=v, compare_op=ALU.is_ge, fill=0.0, base=0,
                                    pattern=[[-C, TC], [0, C]], channel_multiplier=1))

    def setup_squares(act):
        for c in range(XC):
            act.wait_ge(x_in[c], 16)
            nc.scalar.activation(sq0[:, chunks[c]], x0[:, chunks[c]], ACT.Square).then_inc(rms_sq, 1)

    def setup_root(act):
        act.wait_ge(pool_seq, 7)
        act.wait_ge(rms_bcast, 1)
        nc.scalar.activation(rms_inv[:], psum[2][:, 0:L], ACT.Sqrt, bias=eps[:, 0:1], scale=1.0 / D).then_inc(rms_root, 1)

    def setup_hi(act, c):
        act.wait_ge(rms_done, c + 1)
        nc.scalar.activation(xh[:, chunks[c]], x0[:, chunks[c]], ACT.Copy).then_inc(xhi_ready, 1)

    def setup_sums(pe):
        pe.wait_ge(pool_seq, 7)
        for k in range(KT):
            pe.wait_ge(rms_sq, k // (KT // XC) + 1)
            mm = nc.tensor.matmul(psum[2][:, 0:L], ones[:], sq0[:, k], start=k == 0, stop=k == KT - 1)
        mm.then_inc(rms_bcast, 1)

    def setup_inverse(dve, ch):
        ch(nc.vector.memset(vv[:, :, L:LP], 0.0))
        dve.wait_ge(rms_root, 1)
        ch.link(nc.vector.reciprocal(rms_inv[:], rms_inv[:]))

    def setup_scale(dve, c):
        dve.wait_ge(xg_ready, c + 1)
        nc.vector.tensor_tensor(x0[:, chunks[c]], x0[:, chunks[c]],
                                rms_inv[:].rearrange("p (o t) -> p o t", o=1).broadcast_to([P, KT // XC, L]),
                                ALU.mult).then_inc(rms_done, 1)

    def setup_lo(dve, c):
        dve.wait_ge(xhi_ready, c + 1)
        nc.vector.tensor_tensor(xl[:, chunks[c]], x0[:, chunks[c]], xh[:, chunks[c]].bitcast(F32),
                                ALU.subtract).then_inc(xlo_ready, 1)

    shifted = {k: sem(f"shifted_{k}") for k in "lkrvg"}
    lmu_in, lora_ready = sem("lmu_in"), sem("lora_ready")
    lora_copied, prm_copied = sem("lora_copied"), sem("prm_copied")
    z_ready, z_used, cum_ready, exps_ready = sem("z_ready"), sem("z_used"), sem("cum_ready"), sem("exps_ready")
    ksq_ready, n2_ready, n2_held, norm_ready = sem("ksq_ready"), sem("n2_ready"), sem("n2_held"), sem("norm_ready")
    rkm_ready, bonus_ready, gexp_ready, cg_ready = (
        sem("rkm_ready"), sem("bonus_ready"), sem("gexp_ready"), sem("cg_ready"))
    first_consts = sem("first_consts")
    FIRST_CHAIN = 30

    with ExitStack() as ph:
        st = Stream(ph, "a")
        lora = sbuf(ph, "lora_sb", [P, CH])
        lmu = sbuf(ph, "lmu_sb", [P, 1])
        low = sbuf(ph, "low", [P, L])
        lora_i = sbuf(ph, "lora_i", [P, P])
        pi = sbuf(ph, "pi", [P, NPRM + 2])
        pre = {k: sbuf(ph, f"pre_{k}", [P, L + 1]) for k in "lkrvg"}
        names = "dd kx rx ez ea cum pex ec enc eex ksq nrm kkn km tk"
        t = {n: sbuf(ph, f"t_{n}", [P, LP]) for n in names.split()}
        lw = sbuf(ph, "lw", [P, LP])
        reset = sbuf(ph, "reset", [P, LP])
        eg = sbuf(ph, "eg", [P, L])
        cv = sbuf(ph, "cv", [P, SEQ])
        t["av"], t["gx"], t["kb"] = t["ea"], t["rx"], t["ez"]
        pC, uu = t["ksq"][:, 0:L], t["cum"][:, 0:L]
        pgc, egc = pre["l"][:, 0:SEQ], eg[:, 0:SEQ]
        order = [1, 0, 2, 3, 5, 6, 4, 7]
        w_in = A["w_in"].rearrange("(k p) n -> p k n", p=P)

        def col(kind):
            return kind * CH if kind < 4 else RW_COLS + (kind - 4) * CH

        def rounds(eng, body, ch=None, per=0):
            body(0, At(U_IN))
            n0 = ch.n if ch else 0
            with eng.Fori(1, CT - 1) as i:
                if ch:
                    ch.n = n0 - per
                    ch.enter(i, per)
                body(i, At(U_IN, [(i, PER_TILE)]))
                if ch:
                    ch.leave(CT - 1)
            body(CT - 1, At(U_IN + (CT - 1) * PER_TILE), last=True)

        def split_ahead(step, at, h, last):
            j = 2 * at.u + h + AHEAD
            if not (last and j >= 2 * U_WOUT):
                step(At(j // 2, at.loops), j % 2)

        with nc.Block() as block:
            @block.sync
            def _(sp):
                setup_loads(sp)
                st.load_columns(sp, At(U_LORA), w_in, slice(4 * CH, 4 * CH + P))
                sp.dma_start(prm[:], A["prm"]).then_inc(prm_in, 16)
                sp.dma_start(lmu[:], A["lmu"]).then_inc(lmu_in, 16)
                sp.dma_start(lora[:], A["lora"]).then_inc(lmu_in, 16)

                def body(i, at, last=False):
                    for n, kind in enumerate(order):
                        cols = (slice(col(kind) + i * P, col(kind) + (i + 1) * P) if isinstance(i, int)
                                else bass.ds((i + col(kind) // P) * P, P))
                        st.load_columns(sp, at + n, w_in, cols)
                rounds(sp, body)

            @block.tensor
            def _(pe):
                setup_sums(pe)
                x_chunk = {4 * j: (lambda n: lambda: pe.wait_ge(xlo_ready, n))(j + 1) for j in range(2)}
                x_rest = {4 * j: (lambda n: lambda: pe.wait_ge(xlo_ready, n))(j + 3) for j in range(2)}
                st.unit(pe, At(U_LORA), L, xh, xl, (x_chunk, x_rest))
                pe.wait_ge(lora_ready, 2)
                pe.wait_ge(pool_seq, 10)

                def body(i, at, last=False):
                    def gates():
                        pe.wait_ge(lora_copied, i + 1)
                        wait(pe, z_used, 2 * i)
                        for e in range(2):
                            r = slice(64 * e, 64 * e + 64)
                            mm = nc.tensor.matmul(psum[2 + e][:, 0:L], lora_i[r, :], low[r, :], start=True, stop=True)
                        mm.then_inc(z_ready, 1)

                    def key_norm():
                        pe.wait_ge(ksq_ready, i + 1)
                        nc.tensor.matmul(psum[4][:, 0:L], blk[:], t["ksq"][:, 0:L], start=True,
                                         stop=True).then_inc(n2_ready, 1)

                    def bonus():
                        pe.wait_ge(rkm_ready, i + 1)
                        nc.tensor.matmul(psum[5][:, 0:L], blk[:], t["tk"][:, 0:L], start=True,
                                         stop=True).then_inc(bonus_ready, 1)
                    before = {0: ({4: gates}, {}), 2: ({4: key_norm}, {}), 3: ({4: bonus}, {})}
                    for n in range(PER_TILE):
                        st.unit(pe, at + n, L, xh, xl, before.get(n, ({}, {})))
                rounds(pe, body)

            @block.gpsimd
            def _(pool):
                setup_pool(pool)

            @block.scalar
            def _(act):
                ch = chain(act, "act")
                a = nc.scalar
                setup_squares(act)
                st.split_hi(act, At(0), 0)
                setup_root(act)
                st.split_hi(act, At(0), 1)
                for c in range(XC):
                    setup_hi(act, c)
                for j in range(2, AHEAD):
                    st.split_hi(act, At(j // 2), j % 2)
                for h in range(2):
                    split_ahead(lambda q, hh: st.split_hi(act, q, hh), At(U_LORA), h, False)
                computed(act, At(U_LORA))
                act.wait_ge(first_consts, 1)
                a.activation(pre["l"][:, 1:L + 1], GB[0][:, 0:L], ACT.Copy).then_inc(taken[0], 1)
                act.wait_ge(shifted["l"], 1)
                a.activation(low[0:64, :], pre["l"][0:64, 0:L], ACT.Tanh).then_inc(lora_ready, 1)
                a.activation(low[64:128, :], pre["l"][64:128, 0:L], ACT.Copy).then_inc(lora_ready, 1)

                def body(i, at, last=False):
                    src = lora[:, i * P:(i + 1) * P] if isinstance(i, int) else lora[:, bass.ds(i * P, P)]
                    wait(act, z_ready, i)
                    if isinstance(i, int) and i == 0:
                        act.wait_ge(lmu_in, 32)
                    a.activation(lora_i[:], src, ACT.Copy).then_inc(lora_copied, 1)
                    for n in range(PER_TILE):
                        q = at + n
                        for h in range(2):
                            split_ahead(lambda r, hh: st.split_hi(act, r, hh), q, h, last)
                            if n == 0 and h == 0:
                                act.wait_ge(prm_copied, 2 * i + 2)
                                act.wait_ge(z_ready, i + 1)
                                a.activation(t["ez"][:, 0:L], psum[2][:, 0:L], ACT.Exp, bias=pi[:, NPRM:NPRM + 1],
                                             scale=-1.0).then_inc(z_used, 1)
                                a.activation(t["ea"][:, 0:L], psum[3][:, 0:L], ACT.Exp,
                                             bias=pi[:, NPRM + 1:NPRM + 2], scale=-1.0).then_inc(z_used, 1)
                        b = GB[q.bank()]
                        if n < 4:
                            computed(act, q)
                            a.activation(pre["krvg"[n]][:, 1:L + 1], b[:, 0:L], ACT.Copy).then_inc(taken[q.bank()], 1)
                        if n == 0:
                            act.wait_ge(shifted["k"], i + 1)
                            a.activation(t["ksq"][:, 0:L], t["kx"][:, 0:L], ACT.Square,
                                         scale=pi[:, KK:KK + 1]).then_inc(ksq_ready, 1)
                            act.wait_ge(cum_ready, 2 * i + 2)
                            a.activation(t["ec"][:], t["cum"][:], ACT.Exp).then_inc(exps_ready, 1)
                            a.activation(t["enc"][:], t["cum"][:], ACT.Exp, scale=-1.0).then_inc(exps_ready, 1)
                            a.activation(t["eex"][:], t["pex"][:], ACT.Exp).then_inc(exps_ready, 1)
                        if n == 2:
                            act.wait_ge(n2_held, i + 1)
                            a.activation(t["nrm"][:, 0:L], t["nrm"][:, 0:L], ACT.Sqrt).then_inc(norm_ready, 1)
                        if n == 3:
                            act.wait_ge(shifted["g"], i + 1)
                            a.activation(eg[:], t["gx"][:, 0:L], ACT.Exp, scale=-1.0).then_inc(gexp_ready, 1)
                        if n == 4:
                            computed(act, q)
                            a.activation(pC, b[:, 0:L], ACT.Copy).then_inc(taken[q.bank()], 1)
                        if n == 7:
                            computed(act, q)
                            a.activation(pgc, b[:, META:L], ACT.Copy).then_inc(cg_ready, 1)
                            a.activation(egc, b[:, META:L], ACT.Exp, scale=-1.0).then_inc(taken[q.bank()], 1)
                rounds(act, body)

            @block.vector
            def _(dve):
                ch = chain(dve, "dve")
                v = nc.vector
                tt, ts, stt = v.tensor_tensor, v.tensor_scalar, v.scalar_tensor_tensor
                ch(v.memset(reset[:], 1.0))
                ch(v.memset(lw[:], 0.0))
                for n in ("kx", "rx", "kkn", "ez", "km"):
                    ch(v.memset(t[n][:], 0.0))
                for k in "krvg":
                    ch(v.memset(pre[k][:, 0:1], 0.0))
                ch.settle()
                ch(v.memset(reset[:].rearrange("p (c t) -> p c t", t=C)[:, :, 0], 0.0))
                v.memset(pre["l"][:, 0:1], 0.0).then_inc(first_consts, 1)

                st.split_lo(dve, At(0), 0)
                setup_inverse(dve, ch)
                setup_scale(dve, 0)
                setup_scale(dve, 1)
                setup_lo(dve, 0)
                setup_scale(dve, 2)
                setup_lo(dve, 1)
                st.split_lo(dve, At(0), 1)
                setup_scale(dve, 3)
                setup_lo(dve, 2)
                setup_lo(dve, 3)
                for j in range(2, AHEAD):
                    st.split_lo(dve, At(j // 2), j % 2)
                for h in range(2):
                    split_ahead(lambda q, hh: st.split_lo(dve, q, hh), At(U_LORA), h, False)

                def shift(k, mu, dst, step, seen):
                    seen()
                    ch.link(tt(t["dd"][:, 0:L], pre[k][:, 0:L], pre[k][:, 1:L + 1], ALU.subtract))
                    stt(dst, t["dd"][:, 0:L], mu, pre[k][:, 1:L + 1], ALU.mult, ALU.add).then_inc(shifted[k], 1)

                dve.wait_ge(taken[0], 1)
                dve.wait_ge(first_consts, 1)
                dve.wait_ge(lmu_in, 32)
                ch.link(tt(t["dd"][:, 0:L], pre["l"][:, 0:L], pre["l"][:, 1:L + 1], ALU.subtract))
                ch.link(stt(t["tk"][:, 0:L], t["dd"][:, 0:L], lmu[:, 0:1], pre["l"][:, 1:L + 1], ALU.mult, ALU.add))
                v.tensor_copy(pre["l"][:, 0:L], t["tk"][:, 0:L]).then_inc(shifted["l"], 1)

                def body(i, at, last=False):
                    one = slice(i, i + 1) if isinstance(i, int) else bass.ds(i, 1)

                    def tile(x):
                        return x[:, one]
                    if isinstance(i, int) and i == 0:
                        dve.wait_ge(prm_in, 16)
                    wait(dve, norm_ready, i)
                    v.tensor_copy(pi[:, 0:NPRM], prm[:, one, :].rearrange("p a n -> p (a n)")).then_inc(prm_copied, 1)
                    dve.wait_ge(prm_copied, 2 * i + 1)
                    ts(pi[:, NPRM:NPRM + 2], pi[:, W0:W0 + 2], -1.0, None, ALU.mult).then_inc(prm_copied, 1)

                    def p(n):
                        return pi[:, n:n + 1]
                    for n in range(PER_TILE):
                        q = at + n
                        for h in range(2):
                            split_ahead(lambda r, hh: st.split_lo(dve, r, hh), q, h, last)
                        b = GB[q.bank()]

                        def seen():
                            dve.wait_ge(taken[q.bank()], q.evacuated())
                        if n == 0:
                            dve.wait_ge(z_used, 2 * i + 2)
                            ch(ts(t["ez"][:, 0:L], t["ez"][:, 0:L], 1.0, None, ALU.add))
                            ch.link(ts(t["ea"][:, 0:L], t["ea"][:, 0:L], 1.0, None, ALU.add))
                            ch(v.reciprocal(t["ez"][:, 0:L], t["ez"][:, 0:L]))
                            ch.link(v.reciprocal(t["av"][:, 0:L], t["ea"][:, 0:L]))
                            ch.link(ts(lw[:, 0:L], t["ez"][:, 0:L], -float(np.exp(-0.5)), None, ALU.mult))
                            v.tensor_tensor_scan(t["cum"][:], reset[:], lw[:], 0.0, ALU.mult,
                                                 ALU.add).then_inc(cum_ready, 1)
                            dve.wait_ge(cum_ready, 2 * i + 1)
                            tt(t["pex"][:], t["cum"][:], lw[:], ALU.subtract).then_inc(cum_ready, 1)
                            shift("k", p(MU_K), t["kx"][:, 0:L], i, seen)
                            ch.link(ts(t["tk"][:, 0:L], t["av"][:, 0:L], -1.0, p(KA), ALU.add, ALU.mult))
                            dve.wait_ge(shifted["k"], i + 1)
                            ch.link(stt(t["km"][:, 0:L], t["tk"][:, 0:L], 1.0, t["kx"][:, 0:L], ALU.add, ALU.mult))
                        if n == 1:
                            shift("r", p(MU_R), t["rx"][:, 0:L], i, seen)
                            dve.wait_ge(shifted["r"], i + 1)
                            stt(t["tk"][:, 0:L], t["rx"][:, 0:L], p(RK), t["km"][:, 0:L], ALU.mult,
                                ALU.mult).then_inc(rkm_ready, 1)
                            dve.wait_ge(exps_ready, 3 * i + 3)
                            ch(tt(kr[:, one, 1, :].rearrange("p a t -> p (a t)"), t["rx"][:], t["ec"][:], ALU.mult))
                            ch(tt(bk[:, one, 1, :].rearrange("p a t -> p (a t)"), t["km"][:], t["enc"][:], ALU.mult))
                            ch(v.tensor_copy(pc[:, one, :].rearrange("p a c -> p (a c)"),
                                             t["ec"][:].rearrange("p (c t) -> p c t", t=C)[:, :, C - 1]))
                        if n == 2:
                            shift("v", p(MU_V), vv[:, one, 0:L].rearrange("p a t -> p (a t)"), i, seen)
                            dve.wait_ge(n2_ready, i + 1)
                            ts(t["nrm"][:, 0:L], psum[4][:, 0:L], 1e-24, None, ALU.max).then_inc(n2_held, 1)
                        if n == 3:
                            shift("g", p(MU_G), t["gx"][:, 0:L], i, seen)
                            dve.wait_ge(norm_ready, i + 1)
                            ch.link(v.reciprocal(t["nrm"][:, 0:L], t["nrm"][:, 0:L]))
                            ch.link(stt(t["kkn"][:, 0:L], t["kx"][:, 0:L], p(KK), t["nrm"][:, 0:L], ALU.mult, ALU.mult))
                            ch(tt(kr[:, one, 0, :].rearrange("p a t -> p (a t)"), t["kkn"][:], t["eex"][:], ALU.mult))
                            ch.link(tt(t["kb"][:, 0:L], t["kkn"][:, 0:L], t["av"][:, 0:L], ALU.mult))
                            ch(tt(bk[:, one, 0, :].rearrange("p a t -> p (a t)"), t["kb"][:], t["enc"][:], ALU.mult))
                            dve.wait_ge(bonus_ready, i + 1)
                            dve.wait_ge(shifted["v"], i + 1)
                            ch(tt(bon[:, one, :].rearrange("p a t -> p (a t)"), psum[5][:, META:L],
                                  vv[:, one, META:L].rearrange("p a t -> p (a t)"), ALU.mult))
                        if n == 4:
                            dve.wait_ge(gexp_ready, i + 1)
                            ch.link(ts(eg[:], eg[:], 1.0, None, ALU.add))
                            ch.link(v.reciprocal(eg[:], eg[:]))
                            ch(tt(gs[:, one, :].rearrange("p a t -> p (a t)"), eg[:, META:L], t["gx"][:, META:L],
                                  ALU.mult))
                        if n == 5:
                            computed(dve, q)
                            dve.wait_ge(taken[(q.u - 1) % 2], (q + -1).evacuated())
                            tt(uu, b[:, 0:L], pC, ALU.mult).then_inc(taken[q.bank()], 1)
                            seen()
                            ch.link(ts(cv[:], uu[:, META - 2:L - 2], p(CW0), None, ALU.mult))
                            ch.link(stt(cv[:], uu[:, META - 1:L - 1], p(CW1), cv[:], ALU.mult, ALU.add))
                            ch.link(stt(cv[:], uu[:, META:L], p(CW2), cv[:], ALU.mult, ALU.add))
                        if n == 6:
                            computed(dve, q)
                            tt(cv[:], b[:, META:L], cv[:], ALU.mult).then_inc(taken[q.bank()], 1)
                        if n == 7:
                            seen()
                            ch.link(ts(egc, egc, 1.0, None, ALU.add))
                            ch.link(v.reciprocal(egc, egc))
                            dve.wait_ge(cg_ready, i + 1)
                            ch.link(tt(egc, egc, pgc, ALU.mult))
                            dve.wait_ge(taken[(q.u - 1) % 2], (q + -1).evacuated())
                            ch(tt(yb[:, one, :].rearrange("p a t -> p (a t)"), egc, cv[:], ALU.mult))
                rounds(dve, body, ch, FIRST_CHAIN)
    p01.close()
    if dbg:
        with nc.Block() as block:
            @block.sync
            def _(sp):
                n = 0
                for name, s in (("kr", kr), ("bk", bk), ("vv", vv), ("gs", gs), ("bon", bon), ("pc", pc), ("yb", yb)):
                    if name in dbg:
                        sp.dma_start(dbg[name], s[:]).then_inc(stored, 16)
                        n += 16
                sp.wait_ge(stored, n)
    if stop <= 1:
        first.close()
        return

    pair_ready, pair_taken = sem("pair_ready"), sem("pair_taken")
    spread_zeroed, spread_ready = sem("spread_zeroed"), sem("spread_ready")
    aab_out = [sem(f"aab_out{i}") for i in range(NT)]
    sys_in, sys_out, sys_zeroed = sem("sys_in"), [sem("sys_out0"), sem("sys_out1")], sem("sys_zeroed")
    aab_d = nc.dram_tensor("aab_scratch", [NCH, HEADS, C, C], F32, kind="Internal").ap()
    inv_d = nc.dram_tensor("inv_scratch", [NCH, HEADS, C, C], F32, kind="Internal").ap()
    H2 = C // 2
    NA = P // HEADS

    p2 = ExitStack()
    ark = sbuf(p2, "ark", [TT, NT, HEADS, 3, TT])
    with ExitStack() as ph:
        aab = [sbuf(ph, f"aab{i}", [TT, HEADS, TT]) for i in range(2)]
        sa, sx = sbuf(ph, "sa", [P, C + 1 + H2, C]), sbuf(ph, "sx", [P, C + 1 + H2, C])
        sx_last = sbuf(ph, "sx_last", [HEADS, C, C])
        prod = sbuf(ph, "prod", [P, 3, H2, H2])
        mid = sbuf(ph, "mid", [P, H2, H2])
        spread = sbuf(ph, "spread", [P, 2, 2, 2, TT])
        cube = sbuf(ph, "cube", [P, H2, H2, H2])
        last_block = slice(C + 1, C + 1 + H2)
        assert L - NA * C == H2

        def blocks(x, offset, *dims):
            v = x[:]
            return bass.AP(tensor=v.tensor, offset=v.offset + offset,
                           ap=[list(v.ap[0]), [H2 * C + H2, 3], *[list(d) for d in dims]])

        with nc.Block() as block:
            @block.tensor
            def _(pe):
                for n in range(NT * CT):
                    i, p = divmod(n, CT)
                    wait(pe, pair_taken, n - 1)
                    pe.wait_ge(spread_ready, n + 1)
                    for kind in range(2):
                        mm = nc.tensor.matmul(psum[2 * (n % 2) + kind][0:TT, 0:4 * TT], bk[:, p, kind, TT * i:TT * i + TT],
                                              spread[:, n % 2].rearrange("p e k t -> p (e k t)"), start=True, stop=True)
                    mm.then_inc(pair_ready, 1)

            @block.scalar
            def _(act):
                act.wait_ge(spread_zeroed, 1)
                for n in range(NT * CT):
                    i, p = divmod(n, CT)
                    wait(act, pair_ready, n - 1)
                    for e in range(2):
                        r = slice(64 * e, 64 * e + 64)
                        ins = nc.scalar.activation(spread[r, n % 2, e], kr[r, p, :, TT * i:TT * i + TT], ACT.Copy)
                    ins.then_inc(spread_ready, 1)

            @block.gpsimd
            def _(pool):
                nc.gpsimd.memset(spread[:], 0.0).then_inc(spread_zeroed, 1)

            @block.vector
            def _(dve):
                ch = chain(dve, "dve")
                tt = nc.vector.tensor_tensor
                nc.vector.memset(sa[:, C:], 0.0).then_inc(sys_zeroed, 1)
                ch(nc.vector.memset(sx[:], 0.0))
                ch.link(nc.vector.memset(sx_last[:], 0.0))
                ch(nc.vector.memset(blocks(sx, 0, (C + 1, H2)), -1.0))
                ch(nc.vector.memset(sx_last[:].rearrange("p a b -> p (a b)")[:, 0:C * C:C + 1], -1.0))
                for n in range(NT * CT):
                    i, p = divmod(n, CT)
                    if p == 0 and i >= 2:
                        dve.wait_ge(aab_out[i - 2], 16 * TC)
                    dve.wait_ge(pair_ready, n + 1)
                    sums = [psum[2 * (n % 2) + kind][0:TT, 0:4 * TT].rearrange("p (e k t) -> p e k t", e=2, k=2)
                            for kind in range(2)]
                    pair = slice(2 * p, 2 * p + 2)
                    ch(tt(aab[i % 2][:, pair], sums[0][:, :, 0], mask[:, 0:1].broadcast_to([TT, 2, TT]), ALU.mult))
                    ch(tt(ark[:, i, pair, 0], sums[0][:, :, 1], mask[:, 1:2].broadcast_to([TT, 2, TT]), ALU.mult))
                    tt(ark[:, i, pair, 1:3], sums[1], mask[:, 2:4].rearrange("p (o k) t -> p o k t", o=1)
                       .broadcast_to([TT, 2, 2, TT]), ALU.mult).then_inc(pair_taken, 1)
                dve.wait_ge(sys_in, 32)
                for n in range(1, H2):
                    ch.link(tt(prod[:, :, 0:n, 0:n], blocks(sx, 0, (C, n), (1, n)), blocks(sa, n, (0, n), (C, n)), ALU.mult))
                    ch.link(nc.vector.tensor_reduce(blocks(sx, n, (C, n)), prod[:, :, 0:n, 0:n], AX_X, ALU.add))
                nc.vector.tensor_copy(sx_last[:, 0:H2, 0:H2], sx[0:HEADS, last_block, 0:H2]).then_inc(sys_out[1], 1)
                lo, hi = slice(0, H2), slice(H2, C)
                for left, right, out in ((sx[:, lo, lo], sa[:, lo, hi], mid[:]), (mid[:], sx[:, hi, hi], mid[:])):
                    lhs = left.rearrange("p i (o s) -> p i o s", o=1).broadcast_to([P, H2, H2, H2])
                    rhs = right.rearrange("p s (o j) -> p o j s", o=1).broadcast_to([P, H2, H2, H2])
                    ch.link(tt(cube[:], lhs, rhs, ALU.mult))
                    ch.link(nc.vector.tensor_reduce(out, cube[:], AX_X, ALU.add))
                nc.vector.tensor_scalar(sx[:, lo, hi], mid[:], -1.0, None, ALU.mult).then_inc(sys_out[0], 1)

            @block.sync
            def _(sp):
                for i in range(NT):
                    sp.wait_ge(pair_taken, CT * (i + 1))
                    for c in range(TC):
                        w = slice(C * c, C * c + C)
                        sp.dma_start(aab_d[TC * i + c].rearrange("h s t -> s h t"),
                                     aab[i % 2][w, :, w]).then_inc(aab_out[i], 16)
                for i in range(NT):
                    sp.wait_ge(aab_out[i], 16 * TC)
                sp.dma_start(sa[:, 0:C], aab_d[0:NA].rearrange("c h s t -> (c h) s t")).then_inc(sys_in, 16)
                sp.wait_ge(sys_zeroed, 1)
                sp.dma_start(sa[0:HEADS, last_block, 0:H2], aab_d[NA, :, 0:H2, 0:H2]).then_inc(sys_in, 16)
                sp.wait_ge(sys_out[1], 1)
                sp.dma_start(inv_d[NA], sx_last[:]).then_inc(stored, 16)
                sp.wait_ge(sys_out[0], 1)
                sp.dma_start(inv_d[0:NA].rearrange("c h s t -> (c h) s t"), sx[:, 0:C]).then_inc(stored, 16)
                sp.wait_ge(stored, 32)

    zeroed, inv_in, tm_ready, tm_taken = sem("zeroed"), sem("inv_in"), sem("tm_ready"), sem("tm_taken")
    wn_ready, wn_taken, rt_ready = sem("wn_ready"), sem("wn_taken"), sem("rt_ready")
    z_sum, z_taken, u0_sum, u0_taken = sem("z_sum"), sem("z_taken"), sem("u0_sum"), sem("u0_taken")
    bkp_ready, bkt_ready, bks_ready, v_stacked = sem("bkp_ready"), sem("bkt_ready"), sem("bks_ready"), sem("v_stacked")
    uy_sum, u_ready, y_taken, u_kept, sp_ready = (
        sem("uy_sum"), sem("u_ready"), sem("y_taken"), sem("u_kept"), sem("sp_ready"))
    st_sum, st_ready, out_sum, out_taken = sem("st_sum"), sem("st_ready"), sem("out_sum"), sem("out_taken")
    mean_sum, var_sum, sq_ready, root_ready, cent_ready = (
        sem("mean_sum"), sem("var_sum"), sem("sq_ready"), sem("root_ready"), sem("cent_ready"))

    yT = sbuf(p2, "yT", [P, CT, LP])
    with ExitStack() as ph:
        inv = sbuf(ph, "inv", [TT, HEADS, TT])
        ktm, vtm, utm, ytm = (sbuf(ph, n, [TT, CH]) for n in ("ktm", "vtm", "utm", "ytm"))
        zz, u0 = sbuf(ph, "zz", [TT, CH]), sbuf(ph, "u0", [TT, CH])
        wr = sbuf(ph, "wr", [P, CT, TC, 2 * C])
        bkp = [sbuf(ph, f"bkp{i}", [P, CT, 2 * C]) for i in range(2)]
        bks = [sbuf(ph, f"bks{i}", [2 * C, CH]) for i in range(2)]
        uv = [sbuf(ph, f"uv{i}", [2 * C, CH]) for i in range(2)]
        S = sbuf(ph, "S", [P, CT, P])
        Sp = sbuf(ph, "Sp", [P, CT, HD])
        sqy = kr[:, :, 1, 0:SEQ]
        root = sbuf(ph, "yroot", [HEADS, SEQ])
        sel = sbuf(ph, "sel", [P, CT, HEADS])
        selT = sbuf(ph, "selT", [HEADS, CT, 2, HD])
        inv_sum, sel_ready, folded = sem("inv_sum"), sem("sel_ready"), sem("folded")
        out_part, y_done = sem("out_part"), sem("y_done")

        with nc.Block() as block:
            @block.sync
            def _(sp):
                sp.wait_ge(zeroed, 1)
                for i in range(NT):
                    wait(sp, out_sum, i)
                    for c in range(TC):
                        w = slice(C * c, C * c + C)
                        sp.dma_start(inv[w, :, w], inv_d[TC * i + c].rearrange("h s t -> s h t")).then_inc(inv_in, 16)

            @block.gpsimd
            def _(pool):
                g = nc.gpsimd
                g.memset(inv[:], 0.0).then_inc(zeroed, 1)
                g.memset(S[:], 0.0).then_inc(zeroed, 1)
                for i in range(NT):
                    wait(pool, uy_sum, 2 * TC * i)
                    g.tensor_copy(wr[:, :, :, C:2 * C],
                                  kr[:, :, 1, TT * i:TT * i + TT].rearrange("p a (c t) -> p a c t", c=TC)).then_inc(rt_ready, 1)
                    for c in range(TC):
                        m = TC * i + c
                        wait(pool, bkt_ready, 2 * (m - 1))
                        g.tensor_tensor(bkp[m % 2][:].rearrange("p a (k t) -> p a k t", k=2), bk[:, :, :, C * m:C * m + C],
                                        pc[:, :, m:m + 1].rearrange("p a (o q) -> p a o q", o=1).broadcast_to([P, CT, 2, C]),
                                        ALU.mult).then_inc(bkp_ready, 1)
                    if i == 0:
                        g.memset(sel[:], 0.0).then_inc(sel_ready, 1)
                        g.memset(selT[:], 0.0).then_inc(sel_ready, 1)
                        pool.wait_ge(sel_ready, 2)
                        for e in range(2):
                            v = sel[64 * e:64 * e + 64]
                            g.affine_select(out=v, in_=v, compare_op=ALU.not_equal, fill=1.0, base=e,
                                            pattern=[[2, CT], [-1, HEADS]], channel_multiplier=0).then_inc(sel_ready, 1)
                        pool.wait_ge(sel_ready, 4)
                        g.affine_select(out=selT[:], in_=selT[:], compare_op=ALU.not_equal, fill=1.0, base=0,
                                        pattern=[[-2, CT], [-1, 2], [0, HD]], channel_multiplier=1).then_inc(sel_ready, 1)
                        pool.wait_ge(sel_ready, 5)
                ch = chain(pool, "pool")
                pool.wait_ge(bkp_ready, NCH)
                for p in range(CT):
                    ch.link(g.tensor_scalar(bon[:, p], bon[:, p], prm[:, p, LB:LB + 1], None, ALU.add))
                g.tensor_tensor(bon[:], bon[:], gs, ALU.mult).then_inc(folded, 1)
                pool.wait_ge(folded, 1)
                for p in range(CT):
                    ins = g.tensor_scalar(gs[:, p], gs[:, p], prm[:, p, LG:LG + 1], None, ALU.mult)
                    ins.then_inc(folded, 1) if p == CT - 1 else ch.link(ins)

            @block.tensor
            def _(pe):
                tr, mmul = nc.tensor.transpose, nc.tensor.matmul
                for i in range(NT):
                    w = slice(TT * i, TT * i + TT)
                    wait(pe, out_taken, CT * i)
                    for q in range(4):
                        for p in range(4):
                            src = kr[:, 4 * (q % 2) + p, 0, w] if q < 2 else vv[:, 4 * (q % 2) + p, w]
                            last = tr(psum[q][0:TT, P * p:P * p + P], src, ident[:])
                        last.then_inc(tm_ready, 1)
                    pe.wait_ge(inv_in, 16 * TC * (i + 1))
                    for q in range(4):
                        pe.wait_ge(tm_taken, 4 * i + 1 + q // 2)
                        for j in range(2):
                            p = 2 * q + j
                            last = mmul(psum[4 + q][:, 2 * TT * j:2 * TT * j + 2 * TT], ktm[:, P * p:P * p + P],
                                        inv[:, 2 * p:2 * p + 2, :], start=True, stop=True)
                        last.then_inc(wn_ready, 1)
                    pe.wait_ge(tm_taken, 4 * i + 4)
                    for q in range(2):
                        for h in range(8 * q, 8 * q + 8):
                            last = mmul(psum[q][0:TT, HD * (h % 8):HD * (h % 8) + HD], ark[:, i, h, 1, :],
                                        vtm[:, HD * h:HD * h + HD], start=True, stop=True)
                        last.then_inc(z_sum, 1)
                    for q in range(2):
                        pe.wait_ge(z_taken, 2 * i + q + 1)
                        for h in range(8 * q, 8 * q + 8):
                            last = mmul(psum[2 + q][0:TT, HD * (h % 8):HD * (h % 8) + HD], inv[:, h, :],
                                        zz[:, HD * h:HD * h + HD], start=True, stop=True)
                        last.then_inc(u0_sum, 1)
                    for c in range(TC):
                        m = TC * i + c
                        if m < NCH - 1:
                            pe.wait_ge(bkp_ready, m + 1)
                            if c == 0:
                                pe.wait_ge(wn_taken, 8 * (i + 1))
                            else:
                                pe.wait_ge(bks_ready, 2 * m)
                            for q in range(2):
                                for p in range(4):
                                    last = tr(psum[6 + q][0:2 * C, P * p:P * p + P], bkp[m % 2][:, 4 * q + p, :], ident[:])
                                last.then_inc(bkt_ready, 1)
                        pe.wait_ge(rt_ready, i + 1)
                        pe.wait_ge(zeroed, 2)
                        pe.wait_ge(wn_taken, 8 * (i + 1))
                        if c == 0:
                            pe.wait_ge(z_taken, 2 * i + 2)
                        for q in range(2):
                            wait(pe, st_ready, 4 * m - 2 + 2 * q)
                            wait(pe, y_taken, 2 * m - 1 + q)
                            wait(pe, u_ready, 2 * m - 1 + q)
                            for p in range(4 * q, 4 * q + 4):
                                last = mmul(psum[q][0:2 * C, P * (p % 4):P * (p % 4) + P], wr[:, p, c, :], S[:, p, :],
                                            start=True, stop=True)
                            last.then_inc(uy_sum, 1)
                        if m < NCH - 1:
                            pe.wait_ge(v_stacked, m + 1)
                            for q in range(2):
                                pe.wait_ge(bks_ready, 2 * m + q + 1)
                                pe.wait_ge(u_ready, 2 * m + q + 1)
                                for p in range(4 * q, 4 * q + 4):
                                    last = mmul(psum[4 + q][:, P * (p % 4):P * (p % 4) + P], bks[m % 2][:, P * p:P * p + P],
                                                uv[m % 2][:, P * p:P * p + P], start=True, stop=True)
                                last.then_inc(st_sum, 1)
                    pe.wait_ge(u_kept, TC * (i + 1))
                    pe.wait_ge(y_taken, 2 * TC * (i + 1))
                    if i < NT - 1:
                        pe.wait_ge(st_ready, 4 * TC * (i + 1))
                    pe.wait_ge(u0_taken, 2 * (i + 1))
                    two = ident[0:TT, 0:TT].rearrange("p (o t) -> p o t", o=1).broadcast_to([TT, 2, TT])
                    for q in range(4):
                        for j in range(2):
                            p = 2 * q + j
                            o = psum[[2, 3, 4, 5][q]][:, 2 * TT * j:2 * TT * j + 2 * TT]
                            pw = slice(P * p, P * p + P)
                            mmul(o, utm[:, pw], ark[:, i, 2 * p:2 * p + 2, 0, :], start=True, stop=False)
                            mmul(o, vtm[:, pw], ark[:, i, 2 * p:2 * p + 2, 2, :], start=False, stop=False)
                            last = mmul(o, ytm[:, pw], two, start=False, stop=True)
                        if q < 3:
                            last.then_inc(out_part, 1)
                    last.then_inc(out_sum, 1)
                pe.wait_ge(out_taken, CT * NT)
                for p in range(CT):
                    mm = mmul(psum[p // 2][:, SEQ * (p % 2):SEQ * (p % 2) + SEQ], blk[:], yT[:, p, META:L],
                              start=True, stop=True)
                    if p % 2:
                        mm.then_inc(mean_sum, 1)
                pe.wait_ge(sel_ready, 5)
                for p in range(CT):
                    pe.wait_ge(sq_ready, p // 2 + 1)
                    mm = mmul(psum[4][0:HEADS, 0:SEQ], sel[:, p, :], sqy[:, p], start=p == 0, stop=p == CT - 1)
                mm.then_inc(var_sum, 1)
                pe.wait_ge(root_ready, 2)
                for p in range(CT):
                    mm = mmul(psum[p // 2][:, SEQ * (p % 2):SEQ * (p % 2) + SEQ],
                              selT[:, p].rearrange("h e c -> h (e c)"), root[:], start=True, stop=True)
                    if p % 2:
                        mm.then_inc(inv_sum, 1)

            @block.scalar
            def _(act):
                cp = lambda o, i: nc.scalar.activation(o, i, ACT.Copy)
                for i in range(NT):
                    wait(act, out_sum, i)
                    for q in range(4):
                        act.wait_ge(tm_ready, 4 * i + q + 1)
                        cp((ktm if q < 2 else vtm)[:, 512 * (q % 2):512 * (q % 2) + 512], psum[q][0:TT, :]).then_inc(tm_taken, 1)
                    for q in range(4):
                        act.wait_ge(wn_ready, 4 * i + q + 1)
                        for e in range(2):
                            r = slice(64 * e, 64 * e + 64)
                            src = psum[4 + q][r, 0:4 * TT].rearrange("p (j e c t) -> p j e c t", j=2, e=2, t=C)[:, :, e]
                            for j in range(2):
                                ins = cp(wr[r, 2 * q + j, :, 0:C], src[:, j])
                                if j == 1:
                                    ins.then_inc(wn_taken, 1)
                    for c in range(TC):
                        m = TC * i + c
                        if m < NCH - 1:
                            act.wait_ge(tm_taken, 4 * i + 4)
                            wait(act, st_sum, 2 * (m - 1))
                            cp(uv[m % 2][C:2 * C, :], vtm[C * c:C * c + C, :]).then_inc(v_stacked, 1)
                            for q in range(2):
                                act.wait_ge(bkt_ready, 2 * m + q + 1)
                                cp(bks[m % 2][:, 512 * q:512 * q + 512], psum[6 + q][0:2 * C, :]).then_inc(bks_ready, 1)
                        for q in range(2):
                            act.wait_ge(uy_sum, 2 * m + q + 1)
                            cp(ytm[C * c:C * c + C, 512 * q:512 * q + 512], psum[q][C:2 * C, :]).then_inc(y_taken, 1)
                        act.wait_ge(u_ready, 2 * m + 2)
                        cp(utm[C * c:C * c + C, :], uv[m % 2][0:C, :]).then_inc(u_kept, 1)
                    for q in range(4):
                        if q < 3:
                            act.wait_ge(out_part, 3 * i + q + 1)
                        else:
                            act.wait_ge(out_sum, i + 1)
                        src = psum[[2, 3, 4, 5][q]][:, 0:4 * TT].rearrange("p (j e t) -> p j e t", j=2, e=2)
                        for e in range(2):
                            r = slice(64 * e, 64 * e + 64)
                            cp(yT[r, 2 * q:2 * q + 2, TT * i:TT * i + TT], src[r, :, e]).then_inc(out_taken, 1)
                for q in range(4):
                    act.wait_ge(cent_ready, q + 1)
                    nc.scalar.activation(sqy[:, 2 * q:2 * q + 2], yT[:, 2 * q:2 * q + 2, META:L],
                                         ACT.Square).then_inc(sq_ready, 1)
                act.wait_ge(var_sum, 1)
                nc.scalar.activation(root[:], psum[4][0:HEADS, 0:SEQ], ACT.Sqrt, bias=eps[0:HEADS, 1:2],
                                     scale=1.0 / HD).then_inc(root_ready, 1)

            @block.vector
            def _(dve):
                ch = chain(dve, "dve")
                v = nc.vector
                tt = v.tensor_tensor
                for i in range(NT):
                    for q in range(2):
                        dve.wait_ge(z_sum, 2 * i + q + 1)
                        v.tensor_copy(zz[:, 512 * q:512 * q + 512], psum[q][0:TT, :]).then_inc(z_taken, 1)
                    for q in range(2):
                        dve.wait_ge(u0_sum, 2 * i + q + 1)
                        v.tensor_copy(u0[:, 512 * q:512 * q + 512], psum[2 + q][0:TT, :]).then_inc(u0_taken, 1)
                    dve.wait_ge(zeroed, 2)
                    for c in range(TC):
                        m = TC * i + c
                        if m < NCH - 1:
                            wait(dve, st_ready, 4 * m)
                            for e in range(2):
                                r = slice(64 * e, 64 * e + 64)
                                tt(Sp[r], S[r, :, r], pc[r, :, m:m + 1].broadcast_to([64, CT, HD]), ALU.mult).then_inc(sp_ready, 1)
                        dve.wait_ge(u0_taken, 2 * (i + 1))
                        wait(dve, u_kept, m - 1)
                        for q in range(2):
                            w = slice(512 * q, 512 * q + 512)
                            dve.wait_ge(uy_sum, 2 * m + q + 1)
                            tt(uv[m % 2][0:C, w], psum[q][0:C, :], u0[C * c:C * c + C, w], ALU.add).then_inc(u_ready, 1)
                        if m < NCH - 1:
                            dve.wait_ge(sp_ready, 2 * m + 2)
                            for q in range(2):
                                dve.wait_ge(st_sum, 2 * m + q + 1)
                                for e in range(2):
                                    r = slice(64 * e, 64 * e + 64)
                                    tt(S[r, 4 * q:4 * q + 4, r], psum[4 + q][r, :].rearrange("p (a b) -> p a b", b=P)[:, :, r],
                                       Sp[r, 4 * q:4 * q + 4, :], ALU.add).then_inc(st_ready, 1)
                dve.wait_ge(out_taken, CT * NT)
                def two(x, q):
                    return x[:, 2 * q:2 * q + 2]

                def bank(q):
                    return psum[q][:].rearrange("p (a t) -> p a t", a=2)
                for q in range(4):
                    y = two(yT, q)[:, :, META:L]
                    dve.wait_ge(mean_sum, q + 1)
                    v.scalar_tensor_tensor(y, bank(q), -1.0 / HD, y, ALU.mult, ALU.add).then_inc(cent_ready, 1)
                dve.wait_ge(folded, 2)
                for q in range(4):
                    y = two(yT, q)[:, :, META:L]
                    dve.wait_ge(sq_ready, q + 1)
                    ch(tt(y, y, two(gs, q), ALU.mult))
                dve.wait_ge(root_ready, 1)
                v.reciprocal(root[:], root[:]).then_inc(root_ready, 1)
                for q in range(4):
                    y = two(yT, q)[:, :, META:L]
                    dve.wait_ge(inv_sum, q + 1)
                    ch.link(tt(y, bank(q), y, ALU.mult))
                    tt(two(gs, q), y, two(bon, q), ALU.add).then_inc(y_done, 1)
    if dbg:
        with nc.Block() as block:
            @block.sync
            def _(sp):
                n = 0
                for name, s_ in (("ya", gs), ("yT", yT)):
                    if name in dbg:
                        sp.dma_start(dbg[name], s_[:]).then_inc(gain_in, 16)
                        n += 16
                sp.wait_ge(gain_in, 16 + n)
    p2.close()
    first.close()
    if stop <= 2:
        return

    x1_in = [sem(f"x1_in{n}") for n in range(4)]
    out_ready, normed_out = sem("out_ready"), sem("normed_out")
    gcol_ready, x_part, sq_part, acc_part, x1_scaled = (
        sem("gcol_ready"), sem("x_part"), sem("sq_part"), sem("acc_part"), sem("x1_scaled"))
    norm_sum, norm_mean, norm_root, norm_inv = sem("norm_sum"), sem("norm_mean"), sem("norm_root"), sem("norm_inv")
    sc_sum, sc_taken, max_ready, exp_ready, p_ready = (
        sem("sc_sum"), sem("sc_taken"), sem("max_ready"), sem("exp_ready"), sem("p_ready"))
    tr_ready, pt_taken, vt_taken, o_sum, g_copied = (
        sem("tr_ready"), sem("pt_taken"), sem("vt_taken"), sem("o_sum"), sem("g_copied"))
    vt_sum = sem("vt_sum")
    og_ready, oh_ready, ol_ready = sem("og_ready"), sem("oh_ready"), sem("ol_ready")
    table_in, table_ready, masked = sem("table_in"), sem("table_ready"), sem("masked")
    f_in, f_sum, f_abs, f_exp, f_one, f_ln, f_done, f_out = (
        sem("f_in"), sem("f_sum"), sem("f_abs"), sem("f_exp"), sem("f_one"), sem("f_ln"), sem("f_done"), sem("f_out"))
    nf_d = nc.dram_tensor("nf_scratch", [AH, SEQ], F32, kind="Internal").ap()
    SCALE = float(P) ** -0.5
    PER_HEAD = 4
    HEAD_CHAIN = 7

    ph = top.enter_context(ExitStack())
    st = Stream(ph, "b")
    x1 = sbuf(ph, "x1", [P, KT, SEQ])
    xhi = [sbuf(ph, f"xhi{i}", [P, KT, SEQ], F32R) for i in range(2)]
    xlo = [sbuf(ph, f"xlo{i}", [P, KT, SEQ], F32R) for i in range(2)]
    oh = sbuf(ph, "oh", [P, GH, SEQ], F32R)
    ol = sbuf(ph, "ol", [P, GH, SEQ], F32R)
    qT, kT, vT, gT, eg, og = (sbuf(ph, n, [P, SEQ]) for n in ("qT", "kT", "vT", "gT", "egT", "og"))
    vtm = sbuf(ph, "vtm_b", [P, SEQ])
    W3 = 3 * P
    sc, pr, pT = (sbuf(ph, n, [P, W3]) for n in ("sc", "pr", "pT"))
    parts = [slice(0, P), slice(P, W3)]
    table = sbuf(ph, "table", [P, W3])
    causal = sbuf(ph, "causal", [P, P])
    hidden = sbuf(ph, "hidden", [64, 64])
    nfq = sbuf(ph, "nfq", [P, 2])
    stat = sbuf(ph, "stat", [P, 6])
    fw = sbuf(ph, "fw", [P, KT, AH])
    fz = sbuf(ph, "fz", [AH, 4, SEQ])
    fb = sbuf(ph, "fb", [AH, 1])
    f_ones = sbuf(ph, "f_ones", [AH, SEQ])
    SC, PT, VT, OT, FZ, P2 = psum[2:8]

    w_out = A["w_out"].rearrange("(k p) n -> p k n", p=P)
    w_layer = [[A["a_w_in"]] * 4, [A["b_w_in"], A["kv_w"], A["kv_w"], A["b_w_in"]]]
    w_block = [[0, AH, 2 * AH, 3 * AH], [0, 0, AH, AH]]
    w_proj = [A["a_w_out"], A["b_w_out"]]
    rel = A["rel"]
    sqs = mix[:, 0:4].rearrange("p (b k) t -> p b (k t)", b=2)
    acc = mix[:, 4:6].rearrange("p k t -> p (k t)")
    xraw = mix[:, 6:8]
    inv_f = mix[:, 8]
    inv = rms_inv[:, 0:SEQ]
    gcol = sbuf(ph, "gcol", [P, 2, 6])
    GR = GROUPS - 1
    XH_W, XH_LA = 6 + KT, 6 + KT + GH
    ACC_0, SQ_W, ACC_W = 2, KT, 2 + KT

    def place(layer, g, h=None, n=0):
        base = [U_A, U_B][layer] + n
        loops = []
        for reg, per in ((g, PER_GROUP), (h, PER_HEAD)):
            if isinstance(reg, int):
                base += reg * per
            elif reg is not None:
                loops.append((reg, per))
        return At(base, loops)

    def head_no(layer, g, h):
        return g * GH + h + AH * layer

    def layers(eng, layer, head, project, ch=None):
        def group(g):
            if ch:
                ch.n0 = ch.n
            with eng.Fori(0, GH) as h:
                if ch:
                    ch.enter(h, HEAD_CHAIN)
                head(g, h)
                if ch:
                    ch.leave(GH)
            project(g)
        with eng.Fori(0, GR) as g:
            if ch:
                ch.enter(g, GH * HEAD_CHAIN)
            group(g)
            if ch:
                ch.leave(GR)
        group(GR)

    def ahead(step, at, h):
        j = 2 * at.u + h + AHEAD
        if at.loops or j < 2 * U_END:
            step(At(j // 2, at.loops), j % 2)

    with nc.Block() as block:
        @block.sync
        def _(sp):
            with sp.Fori(0, KT // 4) as i:
                for n in range(4):
                    st.load_columns(sp, At(U_WOUT + n, [(i, 4)]), w_out, bass.ds((i * 4 + n) * P, P))
                    one = bass.ds(i * 4 + n, 1)
                    sp.dma_start(x1[:, one, :], A["xt"][:, one, META:L]).then_inc(x1_in[n], 16)
            sp.dma_start(fw[:], A["f_w"].rearrange("(k p) n -> p k n", p=P)).then_inc(f_in, 16)
            sp.dma_start(fb[:], A["f_b"]).then_inc(f_in, 16)
            for layer in range(2):
                def head(g, h):
                    for n in range(4):
                        w = w_layer[layer][n].rearrange("(k p) n -> p k n", p=P)
                        col = (g * GH + h + w_block[layer][n]) * P
                        st.load_columns(sp, place(layer, g, h, n), w, bass.ds(col, P))

                def project(g):
                    w = w_proj[layer].rearrange("(k p) n -> p k n", p=P)
                    for m in range(GH):
                        rows = slice(g * GH, (g + 1) * GH) if isinstance(g, int) else bass.ds(g * GH, GH)
                        st.load(sp, place(layer, g, n=4 * GH + m),
                                lambda half: w[:, rows, P * (2 * m + half):P * (2 * m + half + 1)])
                layers(sp, layer, head, project)
            for q in range(4):
                s = slice(q * KT // 4, (q + 1) * KT // 4)
                sp.wait_ge(out_ready, q + 1)
                sp.dma_start(A["out"][:, s], mix[:, s]).then_inc(normed_out, 16)
            sp.wait_ge(normed_out, 64)

        @block.gpsimd
        def _(pool):
            g_ = nc.gpsimd
            ch = chain(pool, "pool")
            g_.memset(f_ones[:], 1.0).then_inc(f_in, 1)
            ch(g_.memset(hidden[:], NEG_INF))
            ch.link(g_.memset(causal[:], 0.0))
            ch.link(g_.affine_select(out=causal[:], in_=causal[:], compare_op=ALU.is_ge, fill=NEG_INF, base=0,
                                     pattern=[[-1, P]], channel_multiplier=1))

            pool.wait_ge(xlo_ready, 6)
            g_.memset(acc[:, 0:SEQ], 0.0).then_inc(acc_part, 1)
            g_.memset(acc[:, SEQ:], 0.0).then_inc(acc_part, 1)

            def accumulate(b, sq_count, acc_count, first=False):
                pool.wait_ge(sq_part, sq_count)
                pool.wait_ge(acc_part, acc_count)
                if first:
                    ins = g_.tensor_copy(acc, sqs[:, b])
                else:
                    ins = g_.tensor_tensor(acc, acc, sqs[:, b], ALU.add)
                ins.then_inc(acc_part, 1)
            with pool.Fori(0, KT // 4) as i:
                for n in range(4):
                    accumulate(n % 2, i * 4 + n + 1, i * 4 + n + ACC_0)
            pool.wait_ge(f_in, 33)
            g_.tensor_tensor(fw[:], fw[:], gain[:, :, G_KV:G_KV + 1].broadcast_to([P, KT, AH]), ALU.mult).then_inc(f_in, 1)
            pool.wait_ge(norm_inv, 2)
            pool.wait_ge(xlo_ready, XH_W)
            g_.tensor_tensor(x1[:], x1[:], inv_f.rearrange("p (o t) -> p o t", o=1).broadcast_to([P, KT, SEQ]),
                             ALU.mult).then_inc(x1_scaled, 1)
            for layer in range(2):
                if layer == 1:
                    pool.wait_ge(f_done, 1)
                    pool.dma_start(nf_d, fz[:, 3]).then_inc(f_out, 16)
                    pool.wait_ge(f_out, 16)

                def head(g, h):
                    n = head_no(layer, g, h)
                    pool.wait_ge(sc_taken, n + 1)
                    if layer == 0:
                        row = rel[bass.ds(n, 1), 1:1 + SEQ]
                        src = bass.AP(tensor=row.tensor, offset=row.offset + (N_REL // 2 + P - SEQ), ap=[[1, P], [1, SEQ]])
                        pool.dma_start(table[:, 0:SEQ], src).then_inc(table_in, 16)
                        pool.wait_ge(table_in, n * 16 + 16)
                        g_.tensor_tensor(table[0:64, 0:64], table[0:64, 0:64], hidden[:], ALU.add).then_inc(table_ready, 1)
                    else:
                        m = n - AH
                        row = nf_d[bass.ds(m, 1), :]
                        pool.dma_start(table[:, 0:P], row[:, 0:P].broadcast_to([P, P])).then_inc(table_in, 16)
                        pool.dma_start(table[:, P:W3], row.broadcast_to([P, SEQ])).then_inc(table_in, 16)
                        pool.dma_start(nfq[:], row.rearrange("o (q p) -> p (o q)", p=P),
                                       allow_slow_non_contiguous=True).then_inc(table_in, 16)
                        pool.wait_ge(table_in, m * 48 + (16 * AH + 48))
                        v = table[:].rearrange("p (b k) -> p b k", k=P)[:, 0:3:2]
                        g_.tensor_tensor(v, v, causal[:].rearrange("p (o k) -> p o k", o=1).broadcast_to([P, 2, P]),
                                         ALU.add).then_inc(masked, 1)

                def project(g):
                    if isinstance(g, int):
                        for m in range(GH):
                            if m == 0:
                                pool.wait_ge(norm_sum, layer + 1)
                            accumulate(m % 2, SQ_W + GH * layer + m + 1, ACC_W + GH * layer + m, first=m == 0)
                layers(pool, layer, head, project)

        @block.tensor
        def _(pe):
            pe.wait_ge(xlo_ready, 6)
            with pe.Fori(0, KT // 4) as i:
                for n in range(4):
                    st.unit(pe, At(U_WOUT + n, [(i, 4)]), SEQ, xhi[1], xlo[1])
            pe.wait_ge(acc_part, ACC_W)
            nc.tensor.matmul(FZ[:], ones[:], acc, start=True, stop=True).then_inc(norm_sum, 1)

            def total(n):
                pe.wait_ge(acc_part, ACC_W + GH * n)
                pe.wait_ge(norm_root, n + 1)
                nc.tensor.matmul(FZ[:, 0:SEQ], ones[:], acc[:, 0:SEQ], start=True, stop=False)
                nc.tensor.matmul(FZ[:, 0:SEQ], ones[:], acc[:, SEQ:], start=False, stop=True).then_inc(norm_sum, 1)
            for layer in range(2):
                if layer == 0:
                    pe.wait_ge(xlo_ready, XH_W)
                    src = [0, 0, 0, 0]
                else:
                    pe.wait_ge(f_in, 34)
                    pe.wait_ge(taken[(U_B - 1) % 2], At(U_B - 1).evacuated())
                    for k in range(KT):
                        mm = nc.tensor.matmul(P2[0:AH, 0:SEQ], fw[:, k], x1[:, k], start=k == 0, stop=k == KT - 1)
                    mm.then_inc(f_sum, 1)
                    total(1)
                    pe.wait_ge(xlo_ready, XH_LA)
                    src = [1, 0, 0, 1]

                def head(g, h):
                    n = head_no(layer, g, h)
                    q, k, v, gg = (place(layer, g, h, m) for m in range(4))

                    def scores():
                        pe.wait_ge(taken[q.bank()], q.evacuated())
                        pe.wait_ge(taken[k.bank()], k.evacuated())
                        nc.tensor.matmul(SC[:, 0:P], qT[:, 0:P], kT[:, 0:P], start=True, stop=True)
                        nc.tensor.matmul(SC[:, P:W3], qT[:, P:SEQ], kT[:], start=True, stop=True).then_inc(sc_sum, 1)

                    def turn_values():
                        pe.wait_ge(taken[v.bank()], v.evacuated())
                        for m in range(2):
                            last = nc.tensor.transpose(VT[:, P * m:P * m + P], vT[:, P * m:P * m + P], ident[:])
                        last.then_inc(vt_sum, 1)

                    def turn_probs():
                        pe.wait_ge(p_ready, n * 2 + 2)
                        for m in range(3):
                            last = nc.tensor.transpose(PT[:, P * m:P * m + P], pr[:, P * m:P * m + P], ident[:])
                        last.then_inc(tr_ready, 1)
                    none = ({}, {})
                    for m, (at, before) in enumerate(((q, none), (k, none), (v, ({4: scores}, {})),
                                                      (gg, ({3: turn_values}, {3: turn_probs})))):
                        st.unit(pe, at, SEQ, xhi[src[m]], xlo[src[m]], before)
                    pe.wait_ge(pt_taken, n + 1)
                    pe.wait_ge(vt_taken, n + 1)
                    pe.wait_ge(og_ready, n + 1)
                    nc.tensor.matmul(OT[:, 0:SEQ], vtm[:, 0:P], pT[:, 0:SEQ], start=True, stop=False)
                    nc.tensor.matmul(OT[:, P:SEQ], vtm[:, P:SEQ], pT[:, SEQ:W3], start=False, stop=True).then_inc(o_sum, 1)

                def project(g):
                    def product(at, half, tiles):
                        out = GB[at.bank()][:, SEQ * half:SEQ * half + SEQ]
                        if half == 1 and len(tiles) < 8:
                            out = P2[:, 0:SEQ]
                        st.product(pe, at, half, out, lambda k: oh[:, k], lambda k: ol[:, k], start=True, stop=True, tiles=tiles)
                    for m in range(GH):
                        at = place(layer, g, n=4 * GH + m)
                        if m == 0:
                            pe.wait_ge(ol_ready, head_no(layer, g, GH - 1))
                            for half in range(2):
                                product(at, half, range(0, 7))
                            pe.wait_ge(ol_ready, head_no(layer, g, GH))
                            for half in range(2):
                                product(at, half, range(7, 8))
                        else:
                            for half in range(2):
                                product(at, half, range(8))
                layers(pe, layer, head, project)
            total(2)

        @block.scalar
        def _(act):
            a = nc.scalar.activation

            def split_hi(at, h):
                st.split_hi(act, at, h)

            for half in range(2):
                s = slice(half * KT // 2, (half + 1) * KT // 2)
                a(xhi[1][:, s], mix[:, s], ACT.Copy).then_inc(xhi_ready, 1)
            for j in range(2 * U_WOUT, 2 * U_WOUT + AHEAD):
                split_hi(At(j // 2), j % 2)
            act.wait_ge(xlo_ready, 6)
            with act.Fori(0, KT // 4) as i:
                for n in range(4):
                    for h in range(2):
                        ahead(split_hi, At(U_WOUT + n, [(i, 4)]), h)
                    b, j = n % 2, i * 4 + n
                    one = bass.ds(j, 1)
                    act.wait_ge(acc_part, j + (ACC_0 - 1))
                    at = At(U_WOUT + n, [(i, 4)])
                    act.wait_ge(taken[at.bank()], at.evacuated())
                    a(sqs[:, b, 0:SEQ], xraw[:, b], ACT.Square)
                    act.wait_ge(x_part, j + 1)
                    x1j = x1[:, one, :].rearrange("p a t -> p (a t)")
                    a(sqs[:, b, SEQ:], x1j, ACT.Square).then_inc(sq_part, 1)
                    a(xhi[0][:, one, :].rearrange("p a t -> p (a t)"), x1j, ACT.Copy,
                      scale=gcol[:, b, G_A:G_A + 1]).then_inc(xhi_ready, 1)
            act.wait_ge(norm_mean, 1)
            a(inv, inv, ACT.Sqrt).then_inc(norm_root, 1)
            a(inv_f, FZ[:, 0:SEQ], ACT.Sqrt, bias=eps[:, 0:1], scale=1.0 / D).then_inc(norm_root, 1)

            def root(n):
                act.wait_ge(norm_sum, n + 1)
                a(inv, FZ[:, 0:SEQ], ACT.Sqrt, bias=eps[:, 0:1], scale=1.0 / D).then_inc(norm_root, 1)
            for layer in range(2):
                if layer == 1:
                    root(1)
                    act.wait_ge(f_abs, 1)
                    a(fz[:, 2], fz[:, 2], ACT.Exp, scale=-1.0).then_inc(f_exp, 1)
                    act.wait_ge(f_one, 1)
                    a(fz[:, 2], fz[:, 2], ACT.Ln).then_inc(f_ln, 1)

                def head(g, h):
                    n = head_no(layer, g, h)
                    q, k, v, gg = (place(layer, g, h, m) for m in range(4))
                    for at in (q, k, v):
                        for hh in range(2):
                            ahead(split_hi, at, hh)
                    act.wait_ge(max_ready, n + 1)
                    for m in range(2):
                        a(pr[:, parts[m]], sc[:, parts[m]], ACT.Exp, bias=stat[:, 2 + m:3 + m],
                          accum_out=stat[:, 4 + m:5 + m]).then_inc(exp_ready, 1)
                    ahead(split_hi, gg, 0)
                    act.wait_ge(vt_sum, n + 1)
                    a(vtm[:], VT[:, 0:SEQ], ACT.Copy).then_inc(vt_taken, 1)
                    ahead(split_hi, gg, 1)
                    act.wait_ge(tr_ready, n + 1)
                    a(pT[:], PT[:, 0:W3], ACT.Copy).then_inc(pt_taken, 1)
                    act.wait_ge(taken[gg.bank()], gg.evacuated())
                    a(eg[:], gT[:], ACT.Exp, scale=-1.0).then_inc(g_copied, 1)
                    act.wait_ge(og_ready, n + 2)
                    dst = oh[:, bass.ds(h, 1), :].rearrange("p a t -> p (a t)")
                    a(dst, og[:], ACT.Copy).then_inc(oh_ready, 1)

                def project(g):
                    for m in range(GH):
                        at = place(layer, g, n=4 * GH + m)
                        for hh in range(2):
                            ahead(split_hi, at, hh)
                        if isinstance(g, int):
                            act.wait_ge(taken[at.bank()], at.evacuated())
                            act.wait_ge(acc_part, ACC_W + GH * layer + m - 1)
                            pair = slice(2 * m, 2 * m + 2)
                            a(sqs[:, m % 2], x1[:, pair].rearrange("p a t -> p (a t)"), ACT.Square).then_inc(sq_part, 1)
                            if layer == 0:
                                for kt in (2 * m, 2 * m + 1):
                                    for to, col in ((1, G_B), (0, G_KV)):
                                        ins = a(xhi[to][:, kt], x1[:, kt], ACT.Copy, scale=gain[:, kt, col:col + 1])
                                ins.then_inc(xhi_ready, 1)
                layers(act, layer, head, project)
            root(2)

        @block.vector
        def _(dve):
            ch = chain(dve, "dve")
            v_ = nc.vector
            tt, ts, stt = v_.tensor_tensor, v_.tensor_scalar, v_.scalar_tensor_tensor

            def split_lo(at, h):
                st.split_lo(dve, at, h)

            v_.memset(stat[:, 0:1], 0.0).then_inc(sc_taken, 1)
            v_.memset(stat[:, 1:2], 0.0).then_inc(og_ready, 1)
            for half in range(2):
                s = slice(half * KT // 2, (half + 1) * KT // 2)
                dve.wait_ge(xhi_ready, 5 + half)
                tt(xlo[1][:, s], mix[:, s], xhi[1][:, s].bitcast(F32), ALU.subtract).then_inc(xlo_ready, 1)
            for j in range(2 * U_WOUT, 2 * U_WOUT + AHEAD):
                split_lo(At(j // 2), j % 2)
            dve.wait_ge(xlo_ready, 6)
            with dve.Fori(0, KT // 4) as i:
                for n in range(4):
                    at = At(U_WOUT + n, [(i, 4)])
                    ahead(split_lo, at, 0)
                    b, j = n % 2, i * 4 + n
                    one = bass.ds(j, 1)
                    x1j = x1[:, one, :].rearrange("p a t -> p (a t)")
                    v_.tensor_copy(gcol[:, b], gain[:, one, :].rearrange("p a n -> p (a n)")).then_inc(gcol_ready, 1)
                    dve.wait_ge(x1_in[n], i * 16 + 16)
                    computed(dve, at)
                    tt(xraw[:, b], GB[at.bank()][:, 0:SEQ], x1j, ALU.add).then_inc(taken[at.bank()], 1)
                    dve.wait_ge(gcol_ready, j + 1)
                    dve.wait_ge(taken[at.bank()], at.evacuated())
                    ts(x1j, xraw[:, b], gcol[:, b, G_F:G_F + 1], None, ALU.mult).then_inc(x_part, 1)
                    ahead(split_lo, at, 1)
                    dve.wait_ge(xhi_ready, j + 7)
                    stt(xlo[0][:, one, :].rearrange("p a t -> p (a t)"), x1j, gcol[:, b, G_A:G_A + 1],
                        xhi[0][:, one, :].rearrange("p a t -> p (a t)").bitcast(F32), ALU.mult,
                        ALU.subtract).then_inc(xlo_ready, 1)
            dve.wait_ge(norm_sum, 1)
            ch.link(ts(inv, FZ[:, 0:SEQ], 1e-6 / D, 1e-12, ALU.mult, ALU.add))
            stt(inv, FZ[:, SEQ:], 1.0 / D, inv, ALU.mult, ALU.add).then_inc(norm_mean, 1)
            dve.wait_ge(norm_root, 1)
            v_.reciprocal(inv, inv).then_inc(norm_inv, 1)
            dve.wait_ge(norm_root, 2)
            v_.reciprocal(inv_f, inv_f).then_inc(norm_inv, 1)
            dve.wait_ge(norm_inv, 1)

            def inverse(n):
                dve.wait_ge(norm_root, n + 2)
                ch.link(v_.reciprocal(inv, inv))
            for layer in range(2):
                if layer == 1:
                    inverse(1)
                    dve.wait_ge(f_sum, 1)
                    dve.wait_ge(f_in, 34)
                    ch.link(tt(fz[:, 0], P2[0:AH, 0:SEQ], inv[0:AH], ALU.mult))
                    ch.link(ts(fz[:, 0], fz[:, 0], fb[:, 0:1], None, ALU.add))
                    ch.link(ts(fz[:, 1], fz[:, 0], -1.0, None, ALU.mult))
                    tt(fz[:, 2], fz[:, 0], fz[:, 1], ALU.max).then_inc(f_abs, 1)
                    dve.wait_ge(f_exp, 1)
                    ts(fz[:, 2], fz[:, 2], 1.0, None, ALU.add).then_inc(f_one, 1)
                    dve.wait_ge(f_ln, 1)
                    ch.link(stt(fz[:, 0], fz[:, 1], 0.0, fz[:, 2], ALU.max, ALU.add))
                    v_.tensor_tensor_scan(fz[:, 3], f_ones[:], fz[:, 0], 0.0, ALU.mult, ALU.add).then_inc(f_done, 1)

                def head(g, h):
                    n = head_no(layer, g, h)
                    q, k, v, gg = (place(layer, g, h, m) for m in range(4))
                    def evacuate(at, dst):
                        computed(dve, at)
                        b = GB[at.bank()][:, 0:SEQ]
                        (stt(dst[:], b, SCALE, inv, ALU.mult, ALU.mult) if dst is qT
                         else tt(dst[:], b, inv, ALU.mult)).then_inc(taken[at.bank()], 1)
                    for at, dst in ((q, qT), (k, kT)):
                        ahead(split_lo, at, 0)
                        ahead(split_lo, at, 1)
                        evacuate(at, dst)
                    ahead(split_lo, v, 0)
                    dve.wait_ge(sc_sum, n + 1)
                    if layer == 0:
                        dve.wait_ge(table_ready, n + 1)
                        ch(tt(sc[:, parts[0]], SC[:, parts[0]], table[:, 0:P][:, ::-1], ALU.add))
                        tt(sc[:, parts[1]], SC[:, parts[1]], table[:, 0:SEQ][:, ::-1], ALU.add).then_inc(sc_taken, 1)
                        dve.wait_ge(sc_taken, n + 2)
                    else:
                        dve.wait_ge(masked, n - AH + 1)
                        for m in range(2):
                            ins = stt(sc[:, parts[m]], table[:, parts[m]], nfq[:, m:m + 1], SC[:, parts[m]],
                                      ALU.subtract, ALU.add)
                            ch(ins) if m == 0 else ins.then_inc(sc_taken, 1)
                        dve.wait_ge(sc_taken, n + 2)
                    ch(v_.tensor_reduce(stat[:, 0:1], sc[:, parts[0]], AX_X, ALU.max))
                    ch.link(v_.tensor_reduce(stat[:, 1:2], sc[:, parts[1]], AX_X, ALU.max))
                    ts(stat[:, 2:4], stat[:, 0:2], -1.0, None, ALU.mult).then_inc(max_ready, 1)
                    ahead(split_lo, v, 1)
                    dve.wait_ge(exp_ready, n * 2 + 2)
                    ch.link(v_.reciprocal(stat[:, 4:6], stat[:, 4:6]))
                    for m in range(2):
                        ts(pr[:, parts[m]], pr[:, parts[m]], stat[:, 4 + m:5 + m], None, ALU.mult).then_inc(p_ready, 1)
                    evacuate(v, vT)
                    ahead(split_lo, gg, 0)
                    ahead(split_lo, gg, 1)
                    evacuate(gg, gT)
                    dve.wait_ge(g_copied, n + 1)
                    ch.link(ts(eg[:], eg[:], 1.0, None, ALU.add))
                    ch.link(v_.reciprocal(eg[:], eg[:]))
                    ch.link(tt(eg[:], eg[:], gT[:], ALU.mult))
                    dve.wait_ge(o_sum, n + 1)
                    tt(og[:], OT[:, 0:SEQ], eg[:], ALU.mult).then_inc(og_ready, 1)
                    dve.wait_ge(oh_ready, n + 1)
                    one = bass.ds(h, 1)
                    tt(ol[:, one, :].rearrange("p a t -> p (a t)"), og[:],
                       oh[:, one, :].rearrange("p a t -> p (a t)").bitcast(F32), ALU.subtract).then_inc(ol_ready, 1)

                def project(g):
                    dve.wait_ge(x1_scaled, 1)
                    for m in range(GH):
                        at = place(layer, g, n=4 * GH + m)
                        for hh in range(2):
                            ahead(split_lo, at, hh)
                        computed(dve, at)
                        if m == 0:
                            tt(x1[:, 1], P2[:, 0:SEQ], x1[:, 1], ALU.add)
                            tt(x1[:, 0], GB[at.bank()][:, 0:SEQ], x1[:, 0], ALU.add).then_inc(taken[at.bank()], 1)
                        else:
                            xs = x1[:, 2 * m:2 * m + 2].rearrange("p a t -> p (a t)")
                            tt(xs, GB[at.bank()][:], xs, ALU.add).then_inc(taken[at.bank()], 1)
                        if isinstance(g, int) and layer == 0:
                            dve.wait_ge(xhi_ready, XH_W + m + 1)
                            for kt in (2 * m, 2 * m + 1):
                                for to, col in ((1, G_B), (0, G_KV)):
                                    ins = stt(xlo[to][:, kt], x1[:, kt], gain[:, kt, col:col + 1],
                                              xhi[to][:, kt].bitcast(F32), ALU.mult, ALU.subtract)
                            ins.then_inc(xlo_ready, 1)
                layers(dve, layer, head, project, ch)
            inverse(2)
            for kt in range(KT):
                ins = stt(mix[:, kt], x1[:, kt], gain[:, kt, G_OUT:G_OUT + 1], inv, ALU.mult, ALU.mult)
                if kt % 4 == 3:
                    ins.then_inc(out_ready, 1)


_SPEC = ["xt", "prm", "gain", "lora", "lmu", "w_in", "w_out", "a_w_in", "rel", "a_w_out", "kv_w", "f_w", "f_b",
         "b_w_in", "b_w_out"]


def _layout(i):
    import numpy as _np

    f = _np.ascontiguousarray
    x = _np.concatenate([i["meta_tokens"], i["x"][0]], 0).T

    def tiles(v):
        return _np.reshape(v, (-1, 128)).T
    mu = i["mu_shift"][0]
    conv = i["conv_w"][0]
    per_channel = [mu[1024:2048], mu[0:1024], mu[2048:3072], mu[3072:4096], i["w0"][0], i["a0"][0], i["k_k"][0],
                   i["k_a"][0], i["r_k"][0], conv[0], conv[1], conv[2], i["lnx_g"][0], i["lnx_b"][0]]
    gains = [i[n] for n in ("norm_in_g", "norm_f_g", "a_norm_2", "kv_norm_2", "b_norm_2", "final_norm_2")]
    return {
        "xt": f(x.reshape(16, 128, 272).transpose(1, 0, 2)),
        "prm": f(_np.stack([tiles(v) for v in per_channel], -1)),
        "gain": f(_np.stack([tiles(v) for v in gains], -1)),
        "lora": f(_np.concatenate([i["w_lora_up"][0], i["a_lora_up"][0]], 0)),
        "lmu": f(mu[4096:4224].reshape(128, 1)),
        "w_in": i["w_in"][0], "w_out": i["w_out"][0], "a_w_in": i["a_w_in_2"][0], "rel": i["a_rel_bias_2"][0],
        "a_w_out": i["a_w_out_2"][0], "kv_w": i["kv_w_2"], "f_w": i["f_w_2"], "f_b": i["f_b_2"].reshape(32, 1),
        "b_w_in": i["b_w_in_2"][0], "b_w_out": i["b_w_out_2"][0],
    }


def kernel(**inputs):
    import numpy as _np
    import concourse.bacc as _bacc
    from concourse import mybir as _mybir
    from concourse.bass_utils import run_bass_kernel_spmd as _run

    nc = _bacc.Bacc("TRN2", target_bir_lowering=False, num_devices=1)
    laid = _layout({k: _np.asarray(v) for k, v in inputs.items()})
    arrays, aps = {}, {}
    for name in _SPEC:
        a = _np.ascontiguousarray(laid[name])
        arrays[f"in_{name}_dram"] = a
        aps[name] = nc.dram_tensor(f"in_{name}_dram", a.shape, _mybir.dt.from_np(a.dtype), kind="ExternalInput").ap()
    aps["out"] = nc.dram_tensor("out_dram", (128, 16, 256), _mybir.dt.float32, kind="ExternalOutput").ap()
    fused_blocks(nc, aps)
    r = _run(nc, [arrays], core_ids=[0])
    y = r.results[0]["out_dram"]
    return _np.ascontiguousarray(_np.reshape(_np.transpose(y, (2, 1, 0)), (1, 256, 2048)))
```

```python
from contextlib import ExitStack

import numpy as np

import concourse.bass as bass
from concourse import mybir

F32 = mybir.dt.float32
F32R = mybir.dt.float32r
ALU = mybir.AluOpType
ACT = mybir.ActivationFunctionType
AX_X = mybir.AxisListType.X

P = 128
D = 2048
KT = D // P
SEQ = 256
META = 16
L = SEQ + META
CH = 1024
CT = CH // P
HEADS = 16
HD = 64
LORA = 64
C = 32
NCH = -(-L // C)
LP = NCH * C
TC = 3
TT = TC * C
NT = NCH // TC
RW_COLS = 4 * CH + 2 * LORA
NEG_INF = -1e30

AH = 32
DI = AH * P
GROUPS = 4
GH = AH // GROUPS
N_REL = 513

HALF = 8 * P
RAW = 4
SPL = 4
AHEAD = 3

MU_K, MU_R, MU_V, MU_G, W0, A0, KK, KA, RK, CW0, CW1, CW2, LG, LB = range(14)
NPRM = 14
G_IN, G_F, G_A, G_KV, G_B, G_OUT = range(6)

U_LORA = 0
U_IN = 1
PER_TILE = 8
U_WOUT = U_IN + CT * PER_TILE
PER_GROUP = 4 * GH + GH
U_A = U_WOUT + KT
U_B = U_A + GROUPS * PER_GROUP
U_END = U_B + GROUPS * PER_GROUP


class Chain:

    def __init__(self, eng, sem):
        self.eng, self.sem, self.n, self.dyn, self.began = eng, sem, 0, [], []

    def value(self):
        v = self.n
        for reg, per in self.dyn:
            v = reg * per + v
        return v

    def __call__(self, ins):
        ins.then_inc(self.sem, 1)
        self.n += 1

    def settle(self):
        self.eng.wait_ge(self.sem, self.value())

    def link(self, ins):
        self(ins)
        self.settle()

    def enter(self, reg, per):
        self.dyn.append((reg, per))
        self.began.append(self.n)

    def leave(self, count):
        reg, per = self.dyn.pop()
        began = self.began.pop()
        assert self.n - began == per, f"chain: {self.n - began} steps per round, {per} stated"
        self.n = began + count * per


class At:

    def __init__(self, u, loops=()):
        self.u, self.loops = u, tuple(loops)

    def __add__(self, k):
        return At(self.u + k, self.loops)

    def count(self, value, per_unit=1, per=1):
        v = value
        for reg, units in self.loops:
            v = reg * (units * per_unit // per) + v
        return v

    def bank(self):
        return self.u % 2

    def evacuated(self):
        return self.count(self.u // 2 + 1, 1, 2)


def wait(eng, sem, value):
    if isinstance(value, int) and value <= 0:
        return
    eng.wait_ge(sem, value)


def fused_blocks(nc, A):
    with ExitStack() as top:
        _build(nc, A, top)


def _build(nc, A, top):
    def sbuf(stack, name, shape, dt=F32):
        return stack.enter_context(nc.sbuf_tensor(name, shape, dt))

    def sem(name):
        return top.enter_context(nc.semaphore(name))

    psum = [top.enter_context(nc.psum_tensor(f"bank{i}", [P, 512], F32)) for i in range(8)]
    GB = psum[0:2]

    raw_in = [sem(f"raw_in{i}") for i in range(RAW)]
    hi_ready = sem("hi_ready")
    lo_ready = sem("lo_ready")
    half_used = sem("half_used")
    taken = [sem("taken0"), sem("taken1")]
    stored = sem("stored")
    act_seq, dve_seq, pool_seq = sem("act_seq"), sem("dve_seq"), sem("pool_seq")
    chains = {}

    def chain(eng, name):
        s = {"act": act_seq, "dve": dve_seq, "pool": pool_seq}[name]
        if name not in chains:
            chains[name] = Chain(eng, s)
        chains[name].eng = eng
        return chains[name]

    ident = sbuf(top, "ident", [P, P])
    ones = sbuf(top, "ones", [P, P])
    gain = sbuf(top, "gain", [P, KT, 6])
    eps = sbuf(top, "eps", [P, 2])
    rms_inv = sbuf(top, "rms_inv", [P, L])
    mix = sbuf(top, "mix", [P, 2 * CT, SEQ])
    gs = mix[:, 0:CT]
    yb = mix[:, CT:2 * CT]

    class Stream:
        def __init__(self, stack, tag):
            self.raw = [sbuf(stack, f"raw{tag}{i}", [P, 2 * HALF]) for i in range(RAW)]
            self.hi = [sbuf(stack, f"hi{tag}{i}", [P, HALF], F32R) for i in range(SPL)]
            self.lo = [sbuf(stack, f"lo{tag}{i}", [P, HALF], F32R) for i in range(SPL)]

        def load(self, sp, at, halves):
            wait(sp, lo_ready, at.count(2 * (at.u - RAW) + 2, 2))
            slot = at.u % RAW
            for h in range(2):
                dst = self.raw[slot][:, h * HALF:(h + 1) * HALF].rearrange("p (k n) -> p k n", n=P)
                sp.dma_start(dst, halves(h)).then_inc(raw_in[slot], 16)

        def load_columns(self, sp, at, w, cols):
            self.load(sp, at, lambda h: w[:, 8 * h:8 * h + 8, cols])

        def landed(self, eng, at):
            eng.wait_ge(raw_in[at.u % RAW], at.count(32 * (at.u // RAW + 1), 32, RAW))

        def split_hi(self, act, at, h):
            if h == 0:
                self.landed(act, at)
            wait(act, half_used, at.count(2 * at.u + h - SPL + 1, 2))
            nc.scalar.activation(self.hi[(2 * at.u + h) % SPL][:], self.raw[at.u % RAW][:, h * HALF:(h + 1) * HALF],
                                 ACT.Copy).then_inc(hi_ready, 1)

        def split_lo(self, dve, at, h):
            dve.wait_ge(hi_ready, at.count(2 * at.u + h + 1, 2))
            b = (2 * at.u + h) % SPL
            nc.vector.tensor_tensor(self.lo[b][:], self.raw[at.u % RAW][:, h * HALF:(h + 1) * HALF],
                                    self.hi[b][:].bitcast(F32), ALU.subtract).then_inc(lo_ready, 1)

        def product(self, pe, at, h, out, rhs_hi, rhs_lo, start, stop, tiles=range(8), before=None):
            b = (2 * at.u + h) % SPL
            if start and tiles[0] == 0:
                wait(pe, taken[at.bank()], at.count((at.u - 2) // 2 + 1, 1, 2))
            pe.wait_ge(lo_ready, at.count(2 * at.u + h + 1, 2))
            for k in tiles:
                if before and k in before:
                    before[k]()
                w = slice(k * P, (k + 1) * P)
                nc.tensor.matmul(out, self.hi[b][:, w], rhs_hi(k), start=start and k == 0, stop=False)
                nc.tensor.matmul(out, self.hi[b][:, w], rhs_lo(k), start=False, stop=False)
                last = nc.tensor.matmul(out, self.lo[b][:, w], rhs_hi(k), start=False, stop=stop and k == 7)
            if k == 7:
                last.then_inc(half_used, 1)

        def unit(self, pe, at, width, xh, xl, before=({}, {}), first=0):
            for h in range(2):
                self.product(pe, at, h, GB[at.bank()][:, first:width], lambda k: xh[:, 8 * h + k, first:width],
                             lambda k: xl[:, 8 * h + k, first:width], start=h == 0, stop=h == 1, before=before[h])

    def computed(eng, at):
        eng.wait_ge(half_used, at.count(2 * at.u + 2, 2))

    gain_in, prm_in = sem("gain_in"), sem("prm_in")
    x_in = [sem(f"x_in{c}") for c in range(4)]
    rms_sq, rms_bcast, rms_root, rms_inverse = sem("rms_sq"), sem("rms_bcast"), sem("rms_root"), sem("rms_inverse")
    x_scaled = [sem(f"x_scaled{c}") for c in range(4)]
    xg_ready = sem("xg_ready")
    xhi_ready, xlo_ready = sem("xhi_ready"), sem("xlo_ready")

    first = ExitStack()
    kr = sbuf(first, "kr", [P, CT, 2, LP])
    bk = sbuf(first, "bk", [P, CT, 2, LP])
    vv = sbuf(first, "vv", [P, CT, LP])
    bon = sbuf(first, "bon", [P, CT, SEQ])
    pc = sbuf(first, "pc", [P, CT, NCH])
    prm = sbuf(first, "prm_sb", [P, CT, NPRM])
    blk = sbuf(first, "blk", [P, P])
    mask = sbuf(first, "mask", [TT, 4, TT])

    p01 = ExitStack()
    xh = sbuf(p01, "xh", [P, KT, L], F32R)
    xl = sbuf(p01, "xl", [P, KT, L], F32R)
    x0 = kr[:].rearrange("p a b t -> p (a b t)")[:, 0:KT * L].rearrange("p (k t) -> p k t", k=KT)
    sq0 = bk[:].rearrange("p a b t -> p (a b t)")[:, 0:KT * L].rearrange("p (k t) -> p k t", k=KT)
    XC = 4
    chunks = [slice(c * KT // XC, (c + 1) * KT // XC) for c in range(XC)]

    def setup_loads(sp):
        sp.dma_start(gain[:], A["gain"]).then_inc(gain_in, 16)
        for c in range(XC):
            sp.dma_start(x0[:, chunks[c]], A["xt"][:, chunks[c]]).then_inc(x_in[c], 16)

    def setup_pool(pool):
        ch = chain(pool, "pool")
        g = nc.gpsimd
        ch(g.memset(ones[:], 1.0))
        ch(g.memset(eps[:, 0:1], 1e-6))
        ch(g.memset(eps[:, 1:2], 64e-5))
        ch(g.memset(ident[:], 0.0))
        ch(g.memset(blk[:], 0.0))
        ch(g.memset(mask[:, 0], -1.0))
        ch.link(g.memset(mask[:, 1:4], 1.0))
        pool.wait_ge(gain_in, 16)
        for c in range(XC):
            pool.wait_ge(rms_sq, c + 1)
            g.tensor_tensor(x0[:, chunks[c]], x0[:, chunks[c]],
                            gain[:, chunks[c], G_IN:G_IN + 1].broadcast_to([P, KT // XC, L]),
                            ALU.mult).then_inc(xg_ready, 1)
            pool.wait_ge(xg_ready, c + 1)
        ch.link(g.affine_select(out=ident[:], in_=ident[:], compare_op=ALU.not_equal, fill=1.0, base=0,
                                pattern=[[-1, P]], channel_multiplier=1))
        ch.link(g.memset(blk[0:64, 0:64], 1.0))
        ch.link(g.memset(blk[64:128, 64:128], 1.0))
        for kind in range(4):
            v = mask[:, kind].rearrange("p (c t) -> p c t", c=TC)
            ch.link(g.affine_select(out=v, in_=v, compare_op=ALU.is_ge, fill=0.0, base=kind % 2 - 1,
                                    pattern=[[C, TC], [1, C]], channel_multiplier=-1))
            ch.link(g.affine_select(out=v, in_=v, compare_op=ALU.is_ge, fill=0.0, base=0,
                                    pattern=[[-C, TC], [0, C]], channel_multiplier=1))

    def setup_squares(act):
        for c in range(XC):
            act.wait_ge(x_in[c], 16)
            nc.scalar.activation(sq0[:, chunks[c]], x0[:, chunks[c]], ACT.Square).then_inc(rms_sq, 1)

    def setup_root(act):
        act.wait_ge(pool_seq, 7)
        act.wait_ge(rms_bcast, 1)
        nc.scalar.activation(rms_inv[:], psum[2][:, 0:L], ACT.Sqrt, bias=eps[:, 0:1], scale=1.0 / D).then_inc(rms_root, 1)

    def setup_hi(act, c):
        act.wait_ge(x_scaled[c], 1)
        nc.scalar.activation(xh[:, chunks[c]], x0[:, chunks[c]], ACT.Copy).then_inc(xhi_ready, 1)

    def setup_sums(pe):
        pe.wait_ge(pool_seq, 7)
        for k in range(KT):
            pe.wait_ge(rms_sq, k // (KT // XC) + 1)
            mm = nc.tensor.matmul(psum[2][:, 0:L], ones[:], sq0[:, k], start=k == 0, stop=k == KT - 1)
        mm.then_inc(rms_bcast, 1)

    def setup_inverse(dve, ch):
        ch(nc.vector.memset(vv[:, :, L:LP], 0.0))
        dve.wait_ge(rms_root, 1)
        nc.vector.reciprocal(rms_inv[:], rms_inv[:]).then_inc(rms_inverse, 1)

    def setup_scale(eng, vec, c):
        eng.wait_ge(rms_inverse, 1)
        eng.wait_ge(xg_ready, c + 1)
        vec.tensor_tensor(x0[:, chunks[c]], x0[:, chunks[c]],
                                rms_inv[:].rearrange("p (o t) -> p o t", o=1).broadcast_to([P, KT // XC, L]),
                                ALU.mult).then_inc(x_scaled[c], 1)

    def setup_lo(dve, c):
        dve.wait_ge(xhi_ready, c + 1)
        nc.vector.tensor_tensor(xl[:, chunks[c]], x0[:, chunks[c]], xh[:, chunks[c]].bitcast(F32),
                                ALU.subtract).then_inc(xlo_ready, 1)

    shifted = {k: sem(f"shifted_{k}") for k in "lkrvg"}
    lmu_in, lora_ready = sem("lmu_in"), sem("lora_ready")
    lora_copied, prm_copied = sem("lora_copied"), sem("prm_copied")
    z_ready, z_used, cum_ready, exps_ready = sem("z_ready"), sem("z_used"), sem("cum_ready"), sem("exps_ready")
    ksq_ready, n2_ready, n2_held, norm_ready = sem("ksq_ready"), sem("n2_ready"), sem("n2_held"), sem("norm_ready")
    rkm_ready, bonus_ready, gexp_ready, cg_ready = (
        sem("rkm_ready"), sem("bonus_ready"), sem("gexp_ready"), sem("cg_ready"))
    first_consts = sem("first_consts")
    kb_ready, rt_made, kap_made = sem("kb_ready"), sem("rt_made"), sem("kap_made")
    FIRST_CHAIN = 24
    FIRST = [0, META - 2, 0, META - 2, META - 2, META - 2, META, META]

    with ExitStack() as ph:
        st = Stream(ph, "a")
        lora = sbuf(ph, "lora_sb", [P, CH])
        lmu = sbuf(ph, "lmu_sb", [P, 1])
        low = sbuf(ph, "low", [P, L])
        lora_i = sbuf(ph, "lora_i", [P, P])
        pi = sbuf(ph, "pi", [P, NPRM + 2])
        pre = {k: sbuf(ph, f"pre_{k}", [P, L + 1]) for k in "lkrvg"}
        names = "dd kx rx ez ea cum pex ec enc eex ksq nrm kkn km tk"
        t = {n: sbuf(ph, f"t_{n}", [P, LP]) for n in names.split()}
        lw = sbuf(ph, "lw", [P, LP])
        reset = sbuf(ph, "reset", [P, LP])
        eg = sbuf(ph, "eg", [P, L])
        cv = sbuf(ph, "cv", [P, SEQ])
        t["av"], t["gx"], t["kb"] = t["ea"], t["rx"], t["ez"]
        pC, uu = t["ksq"][:, 0:SEQ + 2], t["cum"][:, 0:SEQ + 2]
        pgc, egc = pre["l"][:, 0:SEQ], eg[:, 0:SEQ]
        order = [1, 0, 2, 3, 5, 6, 4, 7]
        w_in = A["w_in"].rearrange("(k p) n -> p k n", p=P)

        def col(kind):
            return kind * CH if kind < 4 else RW_COLS + (kind - 4) * CH

        def rounds(eng, body, ch=None, per=0):
            body(0, At(U_IN))
            n0 = ch.n if ch else 0
            with eng.Fori(1, CT - 1) as i:
                if ch:
                    ch.n = n0 - per
                    ch.enter(i, per)
                body(i, At(U_IN, [(i, PER_TILE)]))
                if ch:
                    ch.leave(CT - 1)
            body(CT - 1, At(U_IN + (CT - 1) * PER_TILE), last=True)

        def split_ahead(step, at, h, last):
            j = 2 * at.u + h + AHEAD
            if not (last and j >= 2 * U_WOUT):
                step(At(j // 2, at.loops), j % 2)

        with nc.Block() as block:
            @block.sync
            def _(sp):
                setup_loads(sp)
                st.load_columns(sp, At(U_LORA), w_in, slice(4 * CH, 4 * CH + P))
                sp.dma_start(prm[:], A["prm"]).then_inc(prm_in, 16)
                sp.dma_start(lmu[:], A["lmu"]).then_inc(lmu_in, 16)
                sp.dma_start(lora[:], A["lora"]).then_inc(lmu_in, 16)

                def body(i, at, last=False):
                    for n, kind in enumerate(order):
                        cols = (slice(col(kind) + i * P, col(kind) + (i + 1) * P) if isinstance(i, int)
                                else bass.ds((i + col(kind) // P) * P, P))
                        st.load_columns(sp, at + n, w_in, cols)
                rounds(sp, body)

            @block.tensor
            def _(pe):
                setup_sums(pe)
                x_chunk = {4 * j: (lambda n: lambda: pe.wait_ge(xlo_ready, n))(j + 1) for j in range(2)}
                x_rest = {4 * j: (lambda n: lambda: pe.wait_ge(xlo_ready, n))(j + 3) for j in range(2)}
                st.unit(pe, At(U_LORA), L, xh, xl, (x_chunk, x_rest))

                def body(i, at, last=False):
                    def gates():
                        if isinstance(i, int) and i == 0:
                            pe.wait_ge(lora_ready, 2)
                            pe.wait_ge(pool_seq, 10)
                        pe.wait_ge(lora_copied, i + 1)
                        wait(pe, z_used, 2 * i)
                        for e in range(2):
                            r = slice(64 * e, 64 * e + 64)
                            mm = nc.tensor.matmul(psum[2 + e][:, 0:L], lora_i[r, :], low[r, :], start=True, stop=True)
                        mm.then_inc(z_ready, 1)

                    def key_norm():
                        pe.wait_ge(ksq_ready, i + 1)
                        nc.tensor.matmul(psum[4][:, 0:L], blk[:], t["ksq"][:, 0:L], start=True,
                                         stop=True).then_inc(n2_ready, 1)

                    def bonus():
                        pe.wait_ge(rkm_ready, i + 1)
                        nc.tensor.matmul(psum[5][:, 0:L], blk[:], t["tk"][:, 0:L], start=True,
                                         stop=True).then_inc(bonus_ready, 1)
                    before = {0: ({4: gates}, {}), 2: ({}, {4: key_norm}), 3: ({}, {4: bonus})}
                    for n in range(PER_TILE):
                        st.unit(pe, at + n, L, xh, xl, before.get(n, ({}, {})), FIRST[n])
                rounds(pe, body)

            @block.gpsimd
            def _(pool):
                setup_pool(pool)
                setup_scale(pool, nc.gpsimd, 2)
                pool.wait_ge(x_scaled[2], 1)
                setup_scale(pool, nc.gpsimd, 3)
                pool.wait_ge(x_scaled[3], 1)
                g = nc.gpsimd
                ch = chain(pool, "pool")

                def body(i, at, last=False):
                    one = slice(i, i + 1) if isinstance(i, int) else bass.ds(i, 1)

                    def row(x, *kind):
                        return x[(slice(None), one, *kind)].rearrange("p a t -> p (a t)")
                    pool.wait_ge(rkm_ready, i + 1)
                    pool.wait_ge(exps_ready, 3 * i + 3)
                    ch.link(g.tensor_tensor(row(kr, 1), t["rx"][:], t["ec"][:], ALU.mult))
                    ch.link(g.tensor_tensor(row(bk, 1), t["km"][:], t["enc"][:], ALU.mult))
                    g.tensor_copy(row(pc), t["ec"][:].rearrange("p (c t) -> p c t", t=C)[:, :, C - 1]).then_inc(rt_made, 1)
                    pool.wait_ge(rt_made, i + 1)
                    pool.wait_ge(kb_ready, i + 1)
                    ch.link(g.tensor_tensor(row(kr, 0), t["kkn"][:], t["eex"][:], ALU.mult))
                    g.tensor_tensor(row(bk, 0), t["kb"][:], t["enc"][:], ALU.mult).then_inc(kap_made, 1)
                    pool.wait_ge(kap_made, i + 1)
                rounds(pool, body, ch, 3)

            @block.scalar
            def _(act):
                ch = chain(act, "act")
                a = nc.scalar
                setup_squares(act)
                st.split_hi(act, At(0), 0)
                setup_root(act)
                st.split_hi(act, At(0), 1)
                for c in range(XC):
                    setup_hi(act, c)
                for j in range(2, AHEAD):
                    st.split_hi(act, At(j // 2), j % 2)
                for h in range(2):
                    split_ahead(lambda q, hh: st.split_hi(act, q, hh), At(U_LORA), h, False)
                computed(act, At(U_LORA))
                act.wait_ge(first_consts, 1)
                a.activation(pre["l"][:, 1:L + 1], GB[0][:, 0:L], ACT.Copy).then_inc(taken[0], 1)
                act.wait_ge(shifted["l"], 1)
                a.activation(low[0:64, :], pre["l"][0:64, 0:L], ACT.Tanh).then_inc(lora_ready, 1)
                a.activation(low[64:128, :], pre["l"][64:128, 0:L], ACT.Copy).then_inc(lora_ready, 1)

                def body(i, at, last=False):
                    src = lora[:, i * P:(i + 1) * P] if isinstance(i, int) else lora[:, bass.ds(i * P, P)]
                    wait(act, z_ready, i)
                    if isinstance(i, int) and i == 0:
                        act.wait_ge(lmu_in, 32)
                    a.activation(lora_i[:], src, ACT.Copy).then_inc(lora_copied, 1)
                    for n in range(PER_TILE):
                        q = at + n
                        for h in range(2):
                            split_ahead(lambda r, hh: st.split_hi(act, r, hh), q, h, last)
                            if n == 0 and h == 0:
                                act.wait_ge(prm_copied, 2 * i + 2)
                                act.wait_ge(z_ready, i + 1)
                                a.activation(t["ez"][:, 0:L], psum[2][:, 0:L], ACT.Exp, bias=pi[:, NPRM:NPRM + 1],
                                             scale=-1.0).then_inc(z_used, 1)
                                a.activation(t["ea"][:, 0:L], psum[3][:, 0:L], ACT.Exp,
                                             bias=pi[:, NPRM + 1:NPRM + 2], scale=-1.0).then_inc(z_used, 1)
                            if n == 1 and h == 0:
                                act.wait_ge(shifted["k"], i + 1)
                                a.activation(t["ksq"][:, 0:L], t["kx"][:, 0:L], ACT.Square,
                                             scale=pi[:, KK:KK + 1]).then_inc(ksq_ready, 1)
                                act.wait_ge(cum_ready, 2 * i + 2)
                                a.activation(t["ec"][:], t["cum"][:], ACT.Exp).then_inc(exps_ready, 1)
                                a.activation(t["enc"][:], t["cum"][:], ACT.Exp, scale=-1.0).then_inc(exps_ready, 1)
                                a.activation(t["eex"][:], t["pex"][:], ACT.Exp).then_inc(exps_ready, 1)
                        b = GB[q.bank()]
                        if n < 4:
                            computed(act, q)
                            a.activation(pre["krvg"[n]][:, 1 + FIRST[n]:L + 1], b[:, FIRST[n]:L], ACT.Copy).then_inc(taken[q.bank()], 1)
                        if n == 2:
                            act.wait_ge(n2_held, i + 1)
                            a.activation(t["nrm"][:, 0:L], t["nrm"][:, 0:L], ACT.Sqrt).then_inc(norm_ready, 1)
                        if n == 3:
                            act.wait_ge(shifted["g"], i + 1)
                            a.activation(eg[:, META:L], t["gx"][:, META:L], ACT.Exp, scale=-1.0).then_inc(gexp_ready, 1)
                        if n == 4:
                            computed(act, q)
                            a.activation(pC, b[:, META - 2:L], ACT.Copy).then_inc(taken[q.bank()], 1)
                        if n == 7:
                            computed(act, q)
                            a.activation(pgc, b[:, META:L], ACT.Copy).then_inc(cg_ready, 1)
                            a.activation(egc, b[:, META:L], ACT.Exp, scale=-1.0).then_inc(taken[q.bank()], 1)
                rounds(act, body)

            @block.vector
            def _(dve):
                ch = chain(dve, "dve")
                v = nc.vector
                tt, ts, stt = v.tensor_tensor, v.tensor_scalar, v.scalar_tensor_tensor
                ch(v.memset(reset[:], 1.0))
                ch(v.memset(lw[:], 0.0))
                for n in ("kx", "rx", "kkn", "ez", "km"):
                    ch(v.memset(t[n][:], 0.0))
                for k in "krvg":
                    ch(v.memset(pre[k][:, 0:1], 0.0))
                ch.settle()
                ch(v.memset(reset[:].rearrange("p (c t) -> p c t", t=C)[:, :, 0], 0.0))
                v.memset(pre["l"][:, 0:1], 0.0).then_inc(first_consts, 1)

                st.split_lo(dve, At(0), 0)
                setup_inverse(dve, ch)
                setup_scale(dve, nc.vector, 0)
                setup_scale(dve, nc.vector, 1)
                setup_lo(dve, 0)
                setup_lo(dve, 1)
                st.split_lo(dve, At(0), 1)
                setup_lo(dve, 2)
                setup_lo(dve, 3)
                for j in range(2, AHEAD):
                    st.split_lo(dve, At(j // 2), j % 2)
                for h in range(2):
                    split_ahead(lambda q, hh: st.split_lo(dve, q, hh), At(U_LORA), h, False)

                def shift(k, mu, dst, seen):
                    seen()
                    f = META if k in "rg" else 0
                    ch.link(tt(t["dd"][:, f:L], pre[k][:, f:L], pre[k][:, f + 1:L + 1], ALU.subtract))
                    stt(dst, t["dd"][:, f:L], mu, pre[k][:, f + 1:L + 1], ALU.mult, ALU.add).then_inc(shifted[k], 1)

                dve.wait_ge(taken[0], 1)
                dve.wait_ge(first_consts, 1)
                dve.wait_ge(lmu_in, 32)
                ch.link(tt(t["dd"][:, 0:L], pre["l"][:, 0:L], pre["l"][:, 1:L + 1], ALU.subtract))
                ch.link(stt(t["tk"][:, 0:L], t["dd"][:, 0:L], lmu[:, 0:1], pre["l"][:, 1:L + 1], ALU.mult, ALU.add))
                v.tensor_copy(pre["l"][:, 0:L], t["tk"][:, 0:L]).then_inc(shifted["l"], 1)

                def body(i, at, last=False):
                    one = slice(i, i + 1) if isinstance(i, int) else bass.ds(i, 1)

                    def tile(x):
                        return x[:, one]
                    if isinstance(i, int) and i == 0:
                        dve.wait_ge(prm_in, 16)
                    wait(dve, kap_made, i)
                    wait(dve, norm_ready, i)
                    v.tensor_copy(pi[:, 0:NPRM], prm[:, one, :].rearrange("p a n -> p (a n)")).then_inc(prm_copied, 1)
                    dve.wait_ge(prm_copied, 2 * i + 1)
                    ts(pi[:, NPRM:NPRM + 2], pi[:, W0:W0 + 2], -1.0, None, ALU.mult).then_inc(prm_copied, 1)

                    def p(n):
                        return pi[:, n:n + 1]
                    for n in range(PER_TILE):
                        q = at + n
                        for h in range(2):
                            split_ahead(lambda r, hh: st.split_lo(dve, r, hh), q, h, last)
                            if n == 1 and h == 0:
                                ch.link(v.reciprocal(t["av"][:, 0:L], t["ea"][:, 0:L]))
                                ch.link(ts(t["tk"][:, 0:L], t["av"][:, 0:L], -1.0, p(KA), ALU.add, ALU.mult))
                                dve.wait_ge(shifted["k"], i + 1)
                                ch.link(stt(t["km"][:, 0:L], t["tk"][:, 0:L], 1.0, t["kx"][:, 0:L], ALU.add, ALU.mult))
                        b = GB[q.bank()]

                        def seen():
                            dve.wait_ge(taken[q.bank()], q.evacuated())
                        if n == 0:
                            dve.wait_ge(z_used, 2 * i + 2)
                            ch(ts(t["ea"][:, 0:L], t["ea"][:, 0:L], 1.0, None, ALU.add))
                            ch.link(ts(t["ez"][:, 0:L], t["ez"][:, 0:L], 1.0, None, ALU.add))
                            ch.link(v.reciprocal(t["ez"][:, 0:L], t["ez"][:, 0:L]))
                            ch.link(ts(lw[:, 0:L], t["ez"][:, 0:L], -float(np.exp(-0.5)), None, ALU.mult))
                            v.tensor_tensor_scan(t["cum"][:], reset[:], lw[:], 0.0, ALU.mult,
                                                 ALU.add).then_inc(cum_ready, 1)
                            dve.wait_ge(cum_ready, 2 * i + 1)
                            tt(t["pex"][:], t["cum"][:], lw[:], ALU.subtract).then_inc(cum_ready, 1)
                            shift("k", p(MU_K), t["kx"][:, 0:L], seen)
                        if n == 1:
                            shift("r", p(MU_R), t["rx"][:, META:L], seen)
                            dve.wait_ge(shifted["r"], i + 1)
                            stt(t["tk"][:, 0:L], t["rx"][:, 0:L], p(RK), t["km"][:, 0:L], ALU.mult,
                                ALU.mult).then_inc(rkm_ready, 1)
                        if n == 2:
                            shift("v", p(MU_V), vv[:, one, 0:L].rearrange("p a t -> p (a t)"), seen)
                            dve.wait_ge(n2_ready, i + 1)
                            ts(t["nrm"][:, 0:L], psum[4][:, 0:L], 1e-24, None, ALU.max).then_inc(n2_held, 1)
                        if n == 3:
                            dve.wait_ge(rt_made, i + 1)
                            shift("g", p(MU_G), t["gx"][:, META:L], seen)
                            dve.wait_ge(norm_ready, i + 1)
                            ch.link(v.reciprocal(t["nrm"][:, 0:L], t["nrm"][:, 0:L]))
                            ch.link(stt(t["kkn"][:, 0:L], t["kx"][:, 0:L], p(KK), t["nrm"][:, 0:L], ALU.mult, ALU.mult))
                            tt(t["kb"][:, 0:L], t["kkn"][:, 0:L], t["av"][:, 0:L], ALU.mult).then_inc(kb_ready, 1)
                            dve.wait_ge(bonus_ready, i + 1)
                            dve.wait_ge(shifted["v"], i + 1)
                            ch(tt(bon[:, one, :].rearrange("p a t -> p (a t)"), psum[5][:, META:L],
                                  vv[:, one, META:L].rearrange("p a t -> p (a t)"), ALU.mult))
                        if n == 4:
                            dve.wait_ge(gexp_ready, i + 1)
                            ch.link(ts(eg[:, META:L], eg[:, META:L], 1.0, None, ALU.add))
                            ch.link(v.reciprocal(eg[:, META:L], eg[:, META:L]))
                            ch(tt(gs[:, one, :].rearrange("p a t -> p (a t)"), eg[:, META:L], t["gx"][:, META:L],
                                  ALU.mult))
                        if n == 5:
                            computed(dve, q)
                            dve.wait_ge(taken[(q.u - 1) % 2], (q + -1).evacuated())
                            tt(uu, b[:, META - 2:L], pC, ALU.mult).then_inc(taken[q.bank()], 1)
                            seen()
                            ch.link(ts(cv[:], uu[:, 0:SEQ], p(CW0), None, ALU.mult))
                            ch.link(stt(cv[:], uu[:, 1:SEQ + 1], p(CW1), cv[:], ALU.mult, ALU.add))
                            ch.link(stt(cv[:], uu[:, 2:SEQ + 2], p(CW2), cv[:], ALU.mult, ALU.add))
                        if n == 6:
                            computed(dve, q)
                            tt(cv[:], b[:, META:L], cv[:], ALU.mult).then_inc(taken[q.bank()], 1)
                        if n == 7:
                            seen()
                            ch.link(ts(egc, egc, 1.0, None, ALU.add))
                            ch.link(v.reciprocal(egc, egc))
                            dve.wait_ge(cg_ready, i + 1)
                            ch.link(tt(egc, egc, pgc, ALU.mult))
                            dve.wait_ge(taken[(q.u - 1) % 2], (q + -1).evacuated())
                            ch(tt(yb[:, one, :].rearrange("p a t -> p (a t)"), egc, cv[:], ALU.mult))
                rounds(dve, body, ch, FIRST_CHAIN)
    p01.close()

    pair_ready, aab_taken, ark_taken = sem("pair_ready"), sem("aab_taken"), sem("ark_taken")
    spread_zeroed, spread_ready = sem("spread_zeroed"), sem("spread_ready")
    aab_out = [sem(f"aab_out{i}") for i in range(NT)]
    sys_in, sys_out, sys_zeroed = sem("sys_in"), [sem("sys_out0"), sem("sys_out1")], sem("sys_zeroed")
    aab_d = nc.dram_tensor("aab_scratch", [NCH, HEADS, C, C], F32, kind="Internal").ap()
    inv_d = nc.dram_tensor("inv_scratch", [NCH, HEADS, C, C], F32, kind="Internal").ap()
    H2 = C // 2
    PAIRS = NT * CT
    NA = P // HEADS

    p2 = ExitStack()
    ark = sbuf(p2, "ark", [TT, NT, HEADS, 3, TT])
    with ExitStack() as ph:
        aab = [sbuf(ph, f"aab{i}", [TT, HEADS, TT]) for i in range(2)]
        sa, sx = sbuf(ph, "sa", [P, C + 1 + H2, C]), sbuf(ph, "sx", [P, C + 1 + H2, C])
        sx_last = sbuf(ph, "sx_last", [HEADS, C, C])
        prod = sbuf(ph, "prod", [P, 3, H2, H2])
        mid, mid2 = sbuf(ph, "mid", [P, H2, H2]), sbuf(ph, "mid2", [P, H2, H2])
        SPREAD = 4
        spread = sbuf(ph, "spread", [P, SPREAD, 2, 2, TT])
        assert PAIRS % SPREAD == 0
        cube = sbuf(ph, "cube", [P, H2, H2, H2])
        last_block = slice(C + 1, C + 1 + H2)
        assert L - NA * C == H2

        def blocks(x, offset, *dims):
            v = x[:]
            return bass.AP(tensor=v.tensor, offset=v.offset + offset,
                           ap=[list(v.ap[0]), [H2 * C + H2, 3], *[list(d) for d in dims]])

        with nc.Block() as block:
            @block.tensor
            def _(pe):
                for n in range(PAIRS):
                    i, p = divmod(n, CT)
                    wait(pe, aab_taken, n - 3)
                    pe.wait_ge(spread_ready, n + 1)
                    nc.tensor.matmul(psum[n % 4][0:TT, 0:2 * TT], bk[:, p, 0, TT * i:TT * i + TT],
                                     spread[:, n % SPREAD, :, 0], start=True, stop=True).then_inc(pair_ready, 1)
                for n in range(PAIRS):
                    i, p = divmod(n, CT)
                    wait(pe, ark_taken, n - 1)
                    pe.wait_ge(spread_ready, PAIRS + n + 1)
                    b = psum[4 + 2 * (n % 2):6 + 2 * (n % 2)]
                    nc.tensor.matmul(b[0][0:TT, 0:2 * TT], bk[:, p, 0, TT * i:TT * i + TT],
                                     spread[:, n % SPREAD, :, 1], start=True, stop=True)
                    nc.tensor.matmul(b[1][0:TT, 0:4 * TT], bk[:, p, 1, TT * i:TT * i + TT],
                                     spread[:, n % SPREAD].rearrange("p e k t -> p (e k t)"), start=True,
                                     stop=True).then_inc(pair_ready, 1)

            @block.scalar
            def _(act):
                cp = lambda o, i: nc.scalar.activation(o, i, ACT.Copy)

                def spread_out(n, kinds):
                    i, p = divmod(n % PAIRS, CT)
                    if n < SPREAD:
                        act.wait_ge(spread_zeroed, n + 1)
                    wait(act, pair_ready, n - SPREAD + 1)
                    for e in range(2):
                        r = slice(64 * e, 64 * e + 64)
                        ins = cp(spread[r, n % SPREAD, e, kinds], kr[r, p, kinds, TT * i:TT * i + TT])
                    ins.then_inc(spread_ready, 1)
                for n in range(PAIRS):
                    spread_out(n, slice(0, 1))
                spread_out(PAIRS, slice(0, 2))
                for n in range(PAIRS):
                    i, p = divmod(n, CT)
                    if n < PAIRS - 1:
                        spread_out(PAIRS + n + 1, slice(0, 2))
                    act.wait_ge(pair_ready, PAIRS + n + 1)
                    sums = [psum[4 + 2 * (n % 2) + kind][0:TT, 0:2 * TT * (kind + 1)] for kind in range(2)]
                    pair = slice(2 * p, 2 * p + 2)
                    cp(ark[:, i, pair, 0], sums[0].rearrange("p (e t) -> p e t", e=2))
                    cp(ark[:, i, pair, 1:3], sums[1].rearrange("p (e k t) -> p e k t", e=2, k=2)).then_inc(ark_taken, 1)

            @block.gpsimd
            def _(pool):
                ch = chain(pool, "pool")
                g = nc.gpsimd
                for n in range(SPREAD):
                    g.memset(spread[:, n], 0.0).then_inc(spread_zeroed, 1)
                g.memset(sa[:, C:], 0.0).then_inc(sys_zeroed, 1)
                ch.link(g.memset(sx[:], 0.0))
                ch.link(g.memset(sx_last[:], 0.0))
                ch.link(g.memset(blocks(sx, 0, (C + 1, H2)), -1.0))
                g.memset(sx_last[:].rearrange("p a b -> p (a b)")[:, 0:C * C:C + 1], -1.0).then_inc(sys_zeroed, 1)
                pool.wait_ge(sys_zeroed, 2)
                for n in range(PAIRS):
                    i, p = divmod(n, CT)
                    v = ark[:, i, 2 * p:2 * p + 2]
                    pool.wait_ge(ark_taken, n + 1)
                    ch.link(nc.gpsimd.tensor_tensor(v, v, mask[:, 1:4].rearrange("p (o k) t -> p o k t", o=1)
                                                    .broadcast_to([TT, 2, 3, TT]), ALU.mult))

            @block.vector
            def _(dve):
                ch = chain(dve, "dve")
                tt = nc.vector.tensor_tensor
                for n in range(PAIRS):
                    i, p = divmod(n, CT)
                    if p == 0 and i >= 2:
                        dve.wait_ge(aab_out[i - 2], 16 * TC)
                    dve.wait_ge(pair_ready, n + 1)
                    tt(aab[i % 2][:, 2 * p:2 * p + 2], psum[n % 4][0:TT, 0:2 * TT].rearrange("p (e t) -> p e t", e=2),
                       mask[:, 0:1].broadcast_to([TT, 2, TT]), ALU.mult).then_inc(aab_taken, 1)
                dve.wait_ge(sys_in, 32)
                dve.wait_ge(sys_zeroed, 2)
                for n in range(1, H2):
                    ch.link(tt(prod[:, :, 0:n, 0:n], blocks(sx, 0, (C, n), (1, n)), blocks(sa, n, (0, n), (C, n)), ALU.mult))
                    ch.link(nc.vector.tensor_reduce(blocks(sx, n, (C, n)), prod[:, :, 0:n, 0:n], AX_X, ALU.add))
                nc.vector.tensor_copy(sx_last[:, 0:H2, 0:H2], sx[0:HEADS, last_block, 0:H2]).then_inc(sys_out[1], 1)
                lo, hi = slice(0, H2), slice(H2, C)
                q = H2 // 2
                near, far = slice(0, q), slice(q, H2)
                both = slice(0, H2)
                for left, right, out, parts in (
                        (sx[:, lo, lo], sa[:, lo, hi], mid, ((near, both, both), (far, far, both))),
                        (mid[:], sx[:, hi, hi], mid2, ((both, near, near), (both, both, far)))):
                    for rows, inner, cols in parts:
                        shape = [P] + [len(range(*x.indices(H2))) for x in (rows, cols, inner)]
                        lhs = left[:, rows, inner].rearrange("p i (o s) -> p i o s", o=1).broadcast_to(shape)
                        rhs = right[:, inner, cols].rearrange("p s (o j) -> p o j s", o=1).broadcast_to(shape)
                        ch(tt(cube[:, rows, cols, inner], lhs, rhs, ALU.mult))
                    ch.settle()
                    for rows, inner, cols in parts:
                        ch(nc.vector.tensor_reduce(out[:, rows, cols], cube[:, rows, cols, inner], AX_X, ALU.add))
                    ch.settle()
                nc.vector.tensor_scalar(sx[:, lo, hi], mid2[:], -1.0, None, ALU.mult).then_inc(sys_out[0], 1)

            @block.sync
            def _(sp):
                for i in range(NT):
                    sp.wait_ge(aab_taken, CT * (i + 1))
                    for c in range(TC):
                        w = slice(C * c, C * c + C)
                        sp.dma_start(aab_d[TC * i + c].rearrange("h s t -> s h t"),
                                     aab[i % 2][w, :, w]).then_inc(aab_out[i], 16)
                for i in range(NT):
                    sp.wait_ge(aab_out[i], 16 * TC)
                sp.dma_start(sa[:, 0:C], aab_d[0:NA].rearrange("c h s t -> (c h) s t")).then_inc(sys_in, 16)
                sp.wait_ge(sys_zeroed, 1)
                sp.dma_start(sa[0:HEADS, last_block, 0:H2], aab_d[NA, :, 0:H2, 0:H2]).then_inc(sys_in, 16)
                sp.wait_ge(sys_out[1], 1)
                sp.dma_start(inv_d[NA], sx_last[:]).then_inc(stored, 16)
                sp.wait_ge(sys_out[0], 1)
                sp.dma_start(inv_d[0:NA].rearrange("c h s t -> (c h) s t"), sx[:, 0:C]).then_inc(stored, 16)
                sp.wait_ge(stored, 32)

    zeroed, inv_in, tm_ready, tm_taken = sem("zeroed"), sem("inv_in"), sem("tm_ready"), sem("tm_taken")
    wn_ready, wn_taken, rt_ready = sem("wn_ready"), sem("wn_taken"), sem("rt_ready")
    z_sum, z_taken, u0_sum, u0_taken = sem("z_sum"), sem("z_taken"), sem("u0_sum"), sem("u0_taken")
    bkp_ready, bkt_ready, bks_ready, v_stacked = sem("bkp_ready"), sem("bkt_ready"), sem("bks_ready"), sem("v_stacked")
    uy_sum, u_ready, y_taken, u_kept, sp_ready = (
        sem("uy_sum"), sem("u_ready"), sem("y_taken"), sem("u_kept"), sem("sp_ready"))
    st_sum, st_ready, out_sum, out_taken = sem("st_sum"), sem("st_ready"), sem("out_sum"), sem("out_taken")
    mean_sum, var_sum, sq_ready, root_ready, cent_ready = (
        sem("mean_sum"), sem("var_sum"), sem("sq_ready"), sem("root_ready"), sem("cent_ready"))

    yT = sbuf(p2, "yT", [P, CT, LP])
    with ExitStack() as ph:
        inv = sbuf(ph, "inv", [TT, HEADS, TT])
        ktm, vtm, utm, ytm = (sbuf(ph, n, [TT, CH]) for n in ("ktm", "vtm", "utm", "ytm"))
        zz, u0 = sbuf(ph, "zz", [TT, CH]), sbuf(ph, "u0", [TT, CH])
        wr = sbuf(ph, "wr", [P, CT, TC, 2 * C])
        bkp = [sbuf(ph, f"bkp{i}", [P, CT, 2 * C]) for i in range(2)]
        bks = [sbuf(ph, f"bks{i}", [2 * C, CH]) for i in range(2)]
        uv = [sbuf(ph, f"uv{i}", [2 * C, CH]) for i in range(2)]
        S = sbuf(ph, "S", [P, CT, P])
        Sp = sbuf(ph, "Sp", [P, CT, HD])
        sqy = kr[:, :, 1, 0:SEQ]
        root = sbuf(ph, "yroot", [HEADS, SEQ])
        sel = sbuf(ph, "sel", [P, CT, HEADS])
        selT = sbuf(ph, "selT", [HEADS, CT, 2, HD])
        inv_sum, sel_ready, folded = sem("inv_sum"), sem("sel_ready"), sem("folded")
        out_part = sem("out_part")

        with nc.Block() as block:
            @block.sync
            def _(sp):
                sp.wait_ge(zeroed, 1)
                for i in range(NT):
                    wait(sp, out_sum, i)
                    for c in range(TC):
                        w = slice(C * c, C * c + C)
                        sp.dma_start(inv[w, :, w], inv_d[TC * i + c].rearrange("h s t -> s h t")).then_inc(inv_in, 16)

            @block.gpsimd
            def _(pool):
                g = nc.gpsimd
                g.memset(inv[:], 0.0).then_inc(zeroed, 1)
                g.memset(S[:], 0.0).then_inc(zeroed, 1)
                for i in range(NT):
                    wait(pool, uy_sum, 2 * TC * i)
                    g.tensor_copy(wr[:, :, :, C:2 * C],
                                  kr[:, :, 1, TT * i:TT * i + TT].rearrange("p a (c t) -> p a c t", c=TC)).then_inc(rt_ready, 1)
                    for c in range(TC):
                        m = TC * i + c
                        wait(pool, bkt_ready, 2 * (m - 1))
                        g.tensor_tensor(bkp[m % 2][:].rearrange("p a (k t) -> p a k t", k=2), bk[:, :, :, C * m:C * m + C],
                                        pc[:, :, m:m + 1].rearrange("p a (o q) -> p a o q", o=1).broadcast_to([P, CT, 2, C]),
                                        ALU.mult).then_inc(bkp_ready, 1)
                    if i == 0:
                        g.memset(sel[:], 0.0).then_inc(sel_ready, 1)
                        g.memset(selT[:], 0.0).then_inc(sel_ready, 1)
                        pool.wait_ge(sel_ready, 2)
                        for e in range(2):
                            v = sel[64 * e:64 * e + 64]
                            g.affine_select(out=v, in_=v, compare_op=ALU.not_equal, fill=1.0, base=e,
                                            pattern=[[2, CT], [-1, HEADS]], channel_multiplier=0).then_inc(sel_ready, 1)
                        pool.wait_ge(sel_ready, 4)
                        g.affine_select(out=selT[:], in_=selT[:], compare_op=ALU.not_equal, fill=1.0, base=0,
                                        pattern=[[-2, CT], [-1, 2], [0, HD]], channel_multiplier=1).then_inc(sel_ready, 1)
                        pool.wait_ge(sel_ready, 5)
                ch = chain(pool, "pool")
                pool.wait_ge(bkp_ready, NCH)
                for p in range(CT):
                    ch.link(g.tensor_scalar(bon[:, p], bon[:, p], prm[:, p, LB:LB + 1], None, ALU.add))
                g.tensor_tensor(bon[:], bon[:], gs, ALU.mult).then_inc(folded, 1)
                pool.wait_ge(folded, 1)
                for p in range(CT):
                    ins = g.tensor_scalar(gs[:, p], gs[:, p], prm[:, p, LG:LG + 1], None, ALU.mult)
                    ins.then_inc(folded, 1) if p == CT - 1 else ch.link(ins)

            @block.tensor
            def _(pe):
                tr, mmul = nc.tensor.transpose, nc.tensor.matmul
                for i in range(NT):
                    w = slice(TT * i, TT * i + TT)
                    wait(pe, out_taken, CT * i)
                    for q in range(4):
                        for p in range(4):
                            src = kr[:, 4 * (q % 2) + p, 0, w] if q < 2 else vv[:, 4 * (q % 2) + p, w]
                            last = tr(psum[q][0:TT, P * p:P * p + P], src, ident[:])
                        last.then_inc(tm_ready, 1)
                    pe.wait_ge(inv_in, 16 * TC * (i + 1))
                    for q in range(4):
                        pe.wait_ge(tm_taken, 4 * i + 1 + q // 2)
                        for j in range(2):
                            p = 2 * q + j
                            last = mmul(psum[4 + q][:, 2 * TT * j:2 * TT * j + 2 * TT], ktm[:, P * p:P * p + P],
                                        inv[:, 2 * p:2 * p + 2, :], start=True, stop=True)
                        last.then_inc(wn_ready, 1)
                    pe.wait_ge(tm_taken, 4 * i + 4)
                    for q in range(2):
                        for h in range(8 * q, 8 * q + 8):
                            last = mmul(psum[q][0:TT, HD * (h % 8):HD * (h % 8) + HD], ark[:, i, h, 1, :],
                                        vtm[:, HD * h:HD * h + HD], start=True, stop=True)
                        last.then_inc(z_sum, 1)
                    for q in range(2):
                        pe.wait_ge(z_taken, 2 * i + q + 1)
                        for h in range(8 * q, 8 * q + 8):
                            last = mmul(psum[2 + q][0:TT, HD * (h % 8):HD * (h % 8) + HD], inv[:, h, :],
                                        zz[:, HD * h:HD * h + HD], start=True, stop=True)
                        last.then_inc(u0_sum, 1)
                    for c in range(TC):
                        m = TC * i + c
                        if m < NCH - 1:
                            pe.wait_ge(bkp_ready, m + 1)
                            if c == 0:
                                pe.wait_ge(wn_taken, 8 * (i + 1))
                            else:
                                pe.wait_ge(bks_ready, 2 * m)
                            for q in range(2):
                                for p in range(4):
                                    last = tr(psum[6 + q][0:2 * C, P * p:P * p + P], bkp[m % 2][:, 4 * q + p, :], ident[:])
                                last.then_inc(bkt_ready, 1)
                        pe.wait_ge(rt_ready, i + 1)
                        pe.wait_ge(zeroed, 2)
                        pe.wait_ge(wn_taken, 8 * (i + 1))
                        if c == 0:
                            pe.wait_ge(z_taken, 2 * i + 2)
                        for q in range(2):
                            wait(pe, st_ready, 4 * m - 2 + 2 * q)
                            wait(pe, y_taken, 2 * m - 1 + q)
                            wait(pe, u_ready, 2 * m - 1 + q)
                            for p in range(4 * q, 4 * q + 4):
                                last = mmul(psum[q][0:2 * C, P * (p % 4):P * (p % 4) + P], wr[:, p, c, :], S[:, p, :],
                                            start=True, stop=True)
                            last.then_inc(uy_sum, 1)
                        if m < NCH - 1:
                            pe.wait_ge(v_stacked, m + 1)
                            for q in range(2):
                                pe.wait_ge(bks_ready, 2 * m + q + 1)
                                pe.wait_ge(u_ready, 2 * m + q + 1)
                                for p in range(4 * q, 4 * q + 4):
                                    last = mmul(psum[4 + q][:, P * (p % 4):P * (p % 4) + P], bks[m % 2][:, P * p:P * p + P],
                                                uv[m % 2][:, P * p:P * p + P], start=True, stop=True)
                                last.then_inc(st_sum, 1)
                    pe.wait_ge(u_kept, TC * (i + 1))
                    pe.wait_ge(y_taken, 2 * TC * (i + 1))
                    if i < NT - 1:
                        pe.wait_ge(st_ready, 4 * TC * (i + 1))
                    pe.wait_ge(u0_taken, 2 * (i + 1))
                    two = ident[0:TT, 0:TT].rearrange("p (o t) -> p o t", o=1).broadcast_to([TT, 2, TT])
                    for q in range(4):
                        for j in range(2):
                            p = 2 * q + j
                            o = psum[[2, 3, 4, 5][q]][:, 2 * TT * j:2 * TT * j + 2 * TT]
                            pw = slice(P * p, P * p + P)
                            mmul(o, utm[:, pw], ark[:, i, 2 * p:2 * p + 2, 0, :], start=True, stop=False)
                            mmul(o, vtm[:, pw], ark[:, i, 2 * p:2 * p + 2, 2, :], start=False, stop=False)
                            last = mmul(o, ytm[:, pw], two, start=False, stop=True)
                        if q < 3:
                            last.then_inc(out_part, 1)
                    last.then_inc(out_sum, 1)
                pe.wait_ge(out_taken, CT * NT)
                for p in range(CT):
                    mm = mmul(psum[p // 2][:, SEQ * (p % 2):SEQ * (p % 2) + SEQ], blk[:], yT[:, p, META:L],
                              start=True, stop=True)
                    if p % 2:
                        mm.then_inc(mean_sum, 1)
                pe.wait_ge(sel_ready, 5)
                for p in range(CT):
                    pe.wait_ge(sq_ready, p // 2 + 1)
                    mm = mmul(psum[4][0:HEADS, 0:SEQ], sel[:, p, :], sqy[:, p], start=p == 0, stop=p == CT - 1)
                mm.then_inc(var_sum, 1)
                pe.wait_ge(root_ready, 2)
                for p in range(CT):
                    mm = mmul(psum[p // 2][:, SEQ * (p % 2):SEQ * (p % 2) + SEQ],
                              selT[:, p].rearrange("h e c -> h (e c)"), root[:], start=True, stop=True)
                    if p % 2:
                        mm.then_inc(inv_sum, 1)

            @block.scalar
            def _(act):
                cp = lambda o, i: nc.scalar.activation(o, i, ACT.Copy)
                for i in range(NT):
                    wait(act, out_sum, i)
                    for q in range(4):
                        act.wait_ge(tm_ready, 4 * i + q + 1)
                        cp((ktm if q < 2 else vtm)[:, 512 * (q % 2):512 * (q % 2) + 512], psum[q][0:TT, :]).then_inc(tm_taken, 1)
                    for q in range(4):
                        act.wait_ge(wn_ready, 4 * i + q + 1)
                        for e in range(2):
                            r = slice(64 * e, 64 * e + 64)
                            src = psum[4 + q][r, 0:4 * TT].rearrange("p (j e c t) -> p j e c t", j=2, e=2, t=C)[:, :, e]
                            for j in range(2):
                                ins = cp(wr[r, 2 * q + j, :, 0:C], src[:, j])
                                if j == 1:
                                    ins.then_inc(wn_taken, 1)
                    for c in range(TC):
                        m = TC * i + c
                        if m < NCH - 1:
                            act.wait_ge(tm_taken, 4 * i + 4)
                            wait(act, st_sum, 2 * (m - 1))
                            cp(uv[m % 2][C:2 * C, :], vtm[C * c:C * c + C, :]).then_inc(v_stacked, 1)
                            for q in range(2):
                                act.wait_ge(bkt_ready, 2 * m + q + 1)
                                cp(bks[m % 2][:, 512 * q:512 * q + 512], psum[6 + q][0:2 * C, :]).then_inc(bks_ready, 1)
                        for q in range(2):
                            act.wait_ge(uy_sum, 2 * m + q + 1)
                            cp(ytm[C * c:C * c + C, 512 * q:512 * q + 512], psum[q][C:2 * C, :]).then_inc(y_taken, 1)
                        act.wait_ge(u_ready, 2 * m + 2)
                        cp(utm[C * c:C * c + C, :], uv[m % 2][0:C, :]).then_inc(u_kept, 1)
                    for q in range(4):
                        if q < 3:
                            act.wait_ge(out_part, 3 * i + q + 1)
                        else:
                            act.wait_ge(out_sum, i + 1)
                        src = psum[[2, 3, 4, 5][q]][:, 0:4 * TT].rearrange("p (j e t) -> p j e t", j=2, e=2)
                        for e in range(2):
                            r = slice(64 * e, 64 * e + 64)
                            cp(yT[r, 2 * q:2 * q + 2, TT * i:TT * i + TT], src[r, :, e]).then_inc(out_taken, 1)
                for q in range(4):
                    act.wait_ge(cent_ready, q + 1)
                    nc.scalar.activation(sqy[:, 2 * q:2 * q + 2], yT[:, 2 * q:2 * q + 2, META:L],
                                         ACT.Square).then_inc(sq_ready, 1)
                act.wait_ge(var_sum, 1)
                nc.scalar.activation(root[:], psum[4][0:HEADS, 0:SEQ], ACT.Sqrt, bias=eps[0:HEADS, 1:2],
                                     scale=1.0 / HD).then_inc(root_ready, 1)

            @block.vector
            def _(dve):
                ch = chain(dve, "dve")
                v = nc.vector
                tt = v.tensor_tensor
                for i in range(NT):
                    for q in range(2):
                        dve.wait_ge(z_sum, 2 * i + q + 1)
                        v.tensor_copy(zz[:, 512 * q:512 * q + 512], psum[q][0:TT, :]).then_inc(z_taken, 1)
                    for q in range(2):
                        dve.wait_ge(u0_sum, 2 * i + q + 1)
                        v.tensor_copy(u0[:, 512 * q:512 * q + 512], psum[2 + q][0:TT, :]).then_inc(u0_taken, 1)
                    dve.wait_ge(zeroed, 2)
                    for c in range(TC):
                        m = TC * i + c
                        if m < NCH - 1:
                            wait(dve, st_ready, 4 * m)
                            for e in range(2):
                                r = slice(64 * e, 64 * e + 64)
                                tt(Sp[r], S[r, :, r], pc[r, :, m:m + 1].broadcast_to([64, CT, HD]), ALU.mult).then_inc(sp_ready, 1)
                        dve.wait_ge(u0_taken, 2 * (i + 1))
                        wait(dve, u_kept, m - 1)
                        for q in range(2):
                            w = slice(512 * q, 512 * q + 512)
                            dve.wait_ge(uy_sum, 2 * m + q + 1)
                            tt(uv[m % 2][0:C, w], psum[q][0:C, :], u0[C * c:C * c + C, w], ALU.add).then_inc(u_ready, 1)
                        if m < NCH - 1:
                            dve.wait_ge(sp_ready, 2 * m + 2)
                            for q in range(2):
                                dve.wait_ge(st_sum, 2 * m + q + 1)
                                for e in range(2):
                                    r = slice(64 * e, 64 * e + 64)
                                    tt(S[r, 4 * q:4 * q + 4, r], psum[4 + q][r, :].rearrange("p (a b) -> p a b", b=P)[:, :, r],
                                       Sp[r, 4 * q:4 * q + 4, :], ALU.add).then_inc(st_ready, 1)
                dve.wait_ge(out_taken, CT * NT)
                def two(x, q):
                    return x[:, 2 * q:2 * q + 2]

                def bank(q):
                    return psum[q][:].rearrange("p (a t) -> p a t", a=2)
                for q in range(4):
                    y = two(yT, q)[:, :, META:L]
                    dve.wait_ge(mean_sum, q + 1)
                    v.scalar_tensor_tensor(y, bank(q), -1.0 / HD, y, ALU.mult, ALU.add).then_inc(cent_ready, 1)
                dve.wait_ge(folded, 2)
                for q in range(4):
                    y = two(yT, q)[:, :, META:L]
                    dve.wait_ge(sq_ready, q + 1)
                    ch(tt(y, y, two(gs, q), ALU.mult))
                dve.wait_ge(root_ready, 1)
                v.reciprocal(root[:], root[:]).then_inc(root_ready, 1)
                for q in range(4):
                    y = two(yT, q)[:, :, META:L]
                    dve.wait_ge(inv_sum, q + 1)
                    ch.link(tt(y, bank(q), y, ALU.mult))
                    ch(tt(two(gs, q), y, two(bon, q), ALU.add))
    p2.close()
    first.close()

    x1_in = [sem(f"x1_in{n}") for n in range(4)]
    OUT_PARTS = [slice(0, 4), slice(4, 8), slice(8, 11), slice(11, KT)]
    out_ready = [sem(f"out_ready{c}") for c in range(len(OUT_PARTS))]
    normed_out, gained = sem("normed_out"), sem("gained")
    gcol_ready, x_part, sq_part, acc_part, x1_scaled = (
        sem("gcol_ready"), sem("x_part"), sem("sq_part"), sem("acc_part"), sem("x1_scaled"))
    norm_sum, norm_mean, norm_root, norm_inv = sem("norm_sum"), sem("norm_mean"), sem("norm_root"), sem("norm_inv")
    sc_sum, sc_taken, max_ready, exp_ready, p_ready = (
        sem("sc_sum"), sem("sc_taken"), sem("max_ready"), sem("exp_ready"), sem("p_ready"))
    tr_ready, pt_taken, vt_taken, o_sum, gate_exp_ready = (
        sem("tr_ready"), sem("pt_taken"), sem("vt_taken"), sem("o_sum"), sem("gate_exp_ready"))
    vt_sum = sem("vt_sum")
    og_ready, oh_ready, ol_ready = sem("og_ready"), sem("oh_ready"), sem("ol_ready")
    table_in, table_ready, masked = sem("table_in"), sem("table_ready"), sem("masked")
    f_in, f_sum, f_abs, f_exp, f_one, f_ln, f_done, f_out = (
        sem("f_in"), sem("f_sum"), sem("f_abs"), sem("f_exp"), sem("f_one"), sem("f_ln"), sem("f_done"), sem("f_out"))
    nf_d = nc.dram_tensor("nf_scratch", [AH, SEQ], F32, kind="Internal").ap()
    SCALE = float(P) ** -0.5
    PER_HEAD = 4
    HEAD_CHAIN = 7

    ph = top.enter_context(ExitStack())
    st = Stream(ph, "b")
    x1 = sbuf(ph, "x1", [P, KT, SEQ])
    xhi = [sbuf(ph, f"xhi{i}", [P, KT, SEQ], F32R) for i in range(2)]
    xlo = [sbuf(ph, f"xlo{i}", [P, KT, SEQ], F32R) for i in range(2)]
    oh = sbuf(ph, "oh", [P, GH, SEQ], F32R)
    ol = sbuf(ph, "ol", [P, GH, SEQ], F32R)
    qT, kT, vT, gT, eg, og = (sbuf(ph, n, [P, SEQ]) for n in ("qT", "kT", "vT", "gT", "egT", "og"))
    vtm = sbuf(ph, "vtm_b", [P, SEQ])
    W3 = 3 * P
    sc, pr, pT = (sbuf(ph, n, [P, W3]) for n in ("sc", "pr", "pT"))
    parts = [slice(0, P), slice(P, W3)]
    table = sbuf(ph, "table", [P, W3])
    causal = sbuf(ph, "causal", [P, P])
    hidden = sbuf(ph, "hidden", [64, 64])
    nfq = sbuf(ph, "nfq", [P, 2])
    stat = sbuf(ph, "stat", [P, 6])
    fw = sbuf(ph, "fw", [P, KT, AH])
    fz = sbuf(ph, "fz", [AH, 4, SEQ])
    fb = sbuf(ph, "fb", [AH, 1])
    f_ones = sbuf(ph, "f_ones", [AH, SEQ])
    SC, PT, VT, OT, FZ, P2 = psum[2:8]

    w_out = A["w_out"].rearrange("(k p) n -> p k n", p=P)
    w_layer = [[A["a_w_in"]] * 4, [A["b_w_in"], A["kv_w"], A["kv_w"], A["b_w_in"]]]
    w_block = [[0, AH, 2 * AH, 3 * AH], [0, 0, AH, AH]]
    w_proj = [A["a_w_out"], A["b_w_out"]]
    rel = A["rel"]
    sqs = mix[:, 0:4].rearrange("p (b k) t -> p b (k t)", b=2)
    acc = mix[:, 4:6].rearrange("p k t -> p (k t)")
    xraw = mix[:, 6:8]
    inv_f = mix[:, 8]
    inv = rms_inv[:, 0:SEQ]
    gcol = sbuf(ph, "gcol", [P, 2, 6])
    GR = GROUPS - 1
    XH_W, XH_LA = 6 + KT, 6 + KT + GH
    ACC_0, SQ_W, ACC_W = 2, KT, 2 + KT

    def place(layer, g, h=None, n=0):
        base = [U_A, U_B][layer] + n
        loops = []
        for reg, per in ((g, PER_GROUP), (h, PER_HEAD)):
            if isinstance(reg, int):
                base += reg * per
            elif reg is not None:
                loops.append((reg, per))
        return At(base, loops)

    def head_no(layer, g, h):
        return g * GH + h + AH * layer

    def layers(eng, layer, head, project, ch=None):
        def group(g):
            with eng.Fori(0, GH) as h:
                if ch:
                    ch.enter(h, HEAD_CHAIN)
                head(g, h)
                if ch:
                    ch.leave(GH)
            project(g)
        with eng.Fori(0, GR) as g:
            if ch:
                ch.enter(g, GH * HEAD_CHAIN)
            group(g)
            if ch:
                ch.leave(GR)
        group(GR)

    def scale_out(vec, c):
        part = OUT_PARTS[c]
        vec.tensor_tensor(mix[:, part], x1[:, part], inv.rearrange("p (o t) -> p o t", o=1).broadcast_to(
            [P, part.stop - part.start, SEQ]), ALU.mult).then_inc(out_ready[c], 1)

    def ahead(step, at, h):
        j = 2 * at.u + h + AHEAD
        if at.loops or j < 2 * U_END:
            step(At(j // 2, at.loops), j % 2)

    with nc.Block() as block:
        @block.sync
        def _(sp):
            with sp.Fori(0, KT // 4) as i:
                for n in range(4):
                    st.load_columns(sp, At(U_WOUT + n, [(i, 4)]), w_out, bass.ds((i * 4 + n) * P, P))
                    one = bass.ds(i * 4 + n, 1)
                    sp.dma_start(x1[:, one, :], A["xt"][:, one, META:L]).then_inc(x1_in[n], 16)
            sp.dma_start(fw[:], A["f_w"].rearrange("(k p) n -> p k n", p=P)).then_inc(f_in, 16)
            sp.dma_start(fb[:], A["f_b"]).then_inc(f_in, 16)
            for layer in range(2):
                def head(g, h):
                    for n in range(4):
                        w = w_layer[layer][n].rearrange("(k p) n -> p k n", p=P)
                        col = (g * GH + h + w_block[layer][n]) * P
                        st.load_columns(sp, place(layer, g, h, n), w, bass.ds(col, P))

                def project(g):
                    w = w_proj[layer].rearrange("(k p) n -> p k n", p=P)
                    for m in range(GH):
                        rows = slice(g * GH, (g + 1) * GH) if isinstance(g, int) else bass.ds(g * GH, GH)
                        st.load(sp, place(layer, g, n=4 * GH + m),
                                lambda half: w[:, rows, P * (2 * m + half):P * (2 * m + half + 1)])
                layers(sp, layer, head, project)
            for part, ready in zip(OUT_PARTS, out_ready):
                sp.wait_ge(ready, 1)
                sp.dma_start(A["out"][:, part], mix[:, part]).then_inc(normed_out, 16)
            sp.wait_ge(normed_out, 16 * len(OUT_PARTS))

        @block.gpsimd
        def _(pool):
            g_ = nc.gpsimd
            ch = chain(pool, "pool")
            g_.memset(f_ones[:], 1.0).then_inc(f_in, 1)
            ch(g_.memset(hidden[:], NEG_INF))
            ch.link(g_.memset(causal[:], 0.0))
            ch.link(g_.affine_select(out=causal[:], in_=causal[:], compare_op=ALU.is_ge, fill=NEG_INF, base=0,
                                     pattern=[[-1, P]], channel_multiplier=1))

            pool.wait_ge(xlo_ready, 6)
            g_.memset(acc[:, 0:SEQ], 0.0).then_inc(acc_part, 1)
            g_.memset(acc[:, SEQ:], 0.0).then_inc(acc_part, 1)

            def accumulate(b, sq_count, acc_count, first=False):
                pool.wait_ge(sq_part, sq_count)
                pool.wait_ge(acc_part, acc_count)
                if first:
                    ins = g_.tensor_copy(acc, sqs[:, b])
                else:
                    ins = g_.tensor_tensor(acc, acc, sqs[:, b], ALU.add)
                ins.then_inc(acc_part, 1)
            with pool.Fori(0, KT // 4) as i:
                for n in range(4):
                    accumulate(n % 2, i * 4 + n + 1, i * 4 + n + ACC_0)
            pool.wait_ge(f_in, 33)
            g_.tensor_tensor(fw[:], fw[:], gain[:, :, G_KV:G_KV + 1].broadcast_to([P, KT, AH]), ALU.mult).then_inc(f_in, 1)
            pool.wait_ge(norm_inv, 2)
            pool.wait_ge(xlo_ready, XH_W)
            g_.tensor_tensor(x1[:], x1[:], inv_f.rearrange("p (o t) -> p o t", o=1).broadcast_to([P, KT, SEQ]),
                             ALU.mult).then_inc(x1_scaled, 1)
            for layer in range(2):
                if layer == 1:
                    pool.wait_ge(f_done, 1)
                    pool.dma_start(nf_d, fz[:, 3]).then_inc(f_out, 16)
                    pool.wait_ge(f_out, 16)

                def head(g, h):
                    n = head_no(layer, g, h)
                    pool.wait_ge(sc_taken, n + 1)
                    if layer == 0:
                        row = rel[bass.ds(n, 1), 1:1 + SEQ]
                        src = bass.AP(tensor=row.tensor, offset=row.offset + (N_REL // 2 + P - SEQ), ap=[[1, P], [1, SEQ]])
                        pool.dma_start(table[:, 0:SEQ], src).then_inc(table_in, 16)
                        pool.wait_ge(table_in, n * 16 + 16)
                        g_.tensor_tensor(table[0:64, 0:64], table[0:64, 0:64], hidden[:], ALU.add).then_inc(table_ready, 1)
                    else:
                        m = n - AH
                        row = nf_d[bass.ds(m, 1), :]
                        pool.dma_start(table[:, 0:P], row[:, 0:P].broadcast_to([P, P])).then_inc(table_in, 16)
                        pool.dma_start(table[:, P:W3], row.broadcast_to([P, SEQ])).then_inc(table_in, 16)
                        pool.dma_start(nfq[:], row.rearrange("o (q p) -> p (o q)", p=P),
                                       allow_slow_non_contiguous=True).then_inc(table_in, 16)
                        pool.wait_ge(table_in, m * 48 + (16 * AH + 48))
                        v = table[:].rearrange("p (b k) -> p b k", k=P)[:, 0:3:2]
                        g_.tensor_tensor(v, v, causal[:].rearrange("p (o k) -> p o k", o=1).broadcast_to([P, 2, P]),
                                         ALU.add).then_inc(masked, 1)

                def project(g):
                    if isinstance(g, int):
                        for m in range(GH):
                            if m == 0:
                                pool.wait_ge(norm_sum, layer + 1)
                            accumulate(m % 2, SQ_W + GH * layer + m + 1, ACC_W + GH * layer + m, first=m == 0)
                layers(pool, layer, head, project)
            pool.wait_ge(norm_inv, 3)
            pool.wait_ge(gained, GH)
            scale_out(g_, len(OUT_PARTS) - 1)

        @block.tensor
        def _(pe):
            pe.wait_ge(xlo_ready, 5)
            with pe.Fori(0, KT // 4) as i:
                for n in range(4):
                    before = ({}, {0: lambda: pe.wait_ge(xlo_ready, 6)}) if n == 0 else ({}, {})
                    st.unit(pe, At(U_WOUT + n, [(i, 4)]), SEQ, xhi[1], xlo[1], before)
            pe.wait_ge(acc_part, ACC_W)
            nc.tensor.matmul(FZ[:], ones[:], acc, start=True, stop=True).then_inc(norm_sum, 1)

            def total(n):
                pe.wait_ge(acc_part, ACC_W + GH * n)
                pe.wait_ge(norm_root, n + 1)
                nc.tensor.matmul(FZ[:, 0:SEQ], ones[:], acc[:, 0:SEQ], start=True, stop=False)
                nc.tensor.matmul(FZ[:, 0:SEQ], ones[:], acc[:, SEQ:], start=False, stop=True).then_inc(norm_sum, 1)
            for layer in range(2):
                if layer == 0:
                    pe.wait_ge(xlo_ready, XH_W)
                    src = [0, 0, 0, 0]
                else:
                    pe.wait_ge(f_in, 34)
                    for k in range(KT):
                        if k % 2 == 0:
                            last = At(U_B - 1 - max(KT - 1 - k, 0) // 2)
                            pe.wait_ge(taken[last.bank()], last.evacuated())
                        mm = nc.tensor.matmul(P2[0:AH, 0:SEQ], fw[:, k], x1[:, k], start=k == 0, stop=k == KT - 1)
                    mm.then_inc(f_sum, 1)
                    total(1)
                    pe.wait_ge(xlo_ready, XH_LA)
                    src = [1, 0, 0, 1]

                def head(g, h):
                    n = head_no(layer, g, h)
                    q, k, v, gg = (place(layer, g, h, m) for m in range(4))

                    def scores():
                        pe.wait_ge(taken[q.bank()], q.evacuated())
                        pe.wait_ge(taken[k.bank()], k.evacuated())
                        nc.tensor.matmul(SC[:, 0:P], qT[:, 0:P], kT[:, 0:P], start=True, stop=True)
                        nc.tensor.matmul(SC[:, P:W3], qT[:, P:SEQ], kT[:], start=True, stop=True).then_inc(sc_sum, 1)

                    def turn_values():
                        pe.wait_ge(taken[v.bank()], v.evacuated())
                        for m in range(2):
                            last = nc.tensor.transpose(VT[:, P * m:P * m + P], vT[:, P * m:P * m + P], ident[:])
                        last.then_inc(vt_sum, 1)

                    def turn_probs():
                        pe.wait_ge(p_ready, n * 2 + 2)
                        for m in range(3):
                            last = nc.tensor.transpose(PT[:, P * m:P * m + P], pr[:, P * m:P * m + P], ident[:])
                        last.then_inc(tr_ready, 1)
                    none = ({}, {})
                    for m, (at, before) in enumerate(((q, none), (k, none), (v, ({5: scores}, {})),
                                                      (gg, ({3: turn_values}, {3: turn_probs})))):
                        st.unit(pe, at, SEQ, xhi[src[m]], xlo[src[m]], before)
                    pe.wait_ge(pt_taken, n + 1)
                    pe.wait_ge(vt_taken, n + 1)
                    pe.wait_ge(og_ready, n + 1)
                    nc.tensor.matmul(OT[:, 0:SEQ], vtm[:, 0:P], pT[:, 0:SEQ], start=True, stop=False)
                    nc.tensor.matmul(OT[:, P:SEQ], vtm[:, P:SEQ], pT[:, SEQ:W3], start=False, stop=True).then_inc(o_sum, 1)

                def project(g):
                    def product(at, half, tiles):
                        out = GB[at.bank()][:, SEQ * half:SEQ * half + SEQ]
                        if half == 1 and len(tiles) < 8:
                            out = P2[:, 0:SEQ]
                        st.product(pe, at, half, out, lambda k: oh[:, k], lambda k: ol[:, k], start=True, stop=True, tiles=tiles)
                    for m in range(GH):
                        at = place(layer, g, n=4 * GH + m)
                        if m == 0:
                            pe.wait_ge(ol_ready, head_no(layer, g, GH - 1))
                            for half in range(2):
                                product(at, half, range(0, 7))
                            pe.wait_ge(ol_ready, head_no(layer, g, GH))
                            for half in range(2):
                                product(at, half, range(7, 8))
                        else:
                            for half in range(2):
                                product(at, half, range(8))
                layers(pe, layer, head, project)
            total(2)

        @block.scalar
        def _(act):
            a = nc.scalar.activation

            def split_hi(at, h):
                st.split_hi(act, at, h)

            for half in range(2):
                s = slice(half * KT // 2, (half + 1) * KT // 2)
                a(xhi[1][:, s], mix[:, s], ACT.Copy).then_inc(xhi_ready, 1)
            for j in range(2 * U_WOUT, 2 * U_WOUT + AHEAD):
                split_hi(At(j // 2), j % 2)
            act.wait_ge(xlo_ready, 6)
            with act.Fori(0, KT // 4) as i:
                for n in range(4):
                    for h in range(2):
                        ahead(split_hi, At(U_WOUT + n, [(i, 4)]), h)
                    b, j = n % 2, i * 4 + n
                    one = bass.ds(j, 1)
                    act.wait_ge(acc_part, j + (ACC_0 - 1))
                    at = At(U_WOUT + n, [(i, 4)])
                    act.wait_ge(taken[at.bank()], at.evacuated())
                    a(sqs[:, b, 0:SEQ], xraw[:, b], ACT.Square)
                    act.wait_ge(x_part, j + 1)
                    x1j = x1[:, one, :].rearrange("p a t -> p (a t)")
                    a(sqs[:, b, SEQ:], x1j, ACT.Square).then_inc(sq_part, 1)
                    a(xhi[0][:, one, :].rearrange("p a t -> p (a t)"), x1j, ACT.Copy,
                      scale=gcol[:, b, G_A:G_A + 1]).then_inc(xhi_ready, 1)
            act.wait_ge(norm_mean, 1)
            a(inv, inv, ACT.Sqrt).then_inc(norm_root, 1)
            a(inv_f, FZ[:, 0:SEQ], ACT.Sqrt, bias=eps[:, 0:1], scale=1.0 / D).then_inc(norm_root, 1)

            def root(n):
                act.wait_ge(norm_sum, n + 1)
                a(inv, FZ[:, 0:SEQ], ACT.Sqrt, bias=eps[:, 0:1], scale=1.0 / D).then_inc(norm_root, 1)
            for layer in range(2):
                if layer == 1:
                    root(1)
                    act.wait_ge(f_abs, 1)
                    a(fz[:, 2], fz[:, 2], ACT.Exp, scale=-1.0).then_inc(f_exp, 1)
                    act.wait_ge(f_one, 1)
                    a(fz[:, 2], fz[:, 2], ACT.Ln).then_inc(f_ln, 1)

                def head(g, h):
                    n = head_no(layer, g, h)
                    q, k, v, gg = (place(layer, g, h, m) for m in range(4))
                    for at in (q, k, v):
                        for hh in range(2):
                            ahead(split_hi, at, hh)
                    act.wait_ge(max_ready, n + 1)
                    for m in range(2):
                        a(pr[:, parts[m]], sc[:, parts[m]], ACT.Exp, bias=stat[:, 2 + m:3 + m],
                          accum_out=stat[:, 4 + m:5 + m]).then_inc(exp_ready, 1)
                    ahead(split_hi, gg, 0)
                    act.wait_ge(vt_sum, n + 1)
                    a(vtm[:], VT[:, 0:SEQ], ACT.Copy).then_inc(vt_taken, 1)
                    ahead(split_hi, gg, 1)
                    act.wait_ge(tr_ready, n + 1)
                    a(pT[:], PT[:, 0:W3], ACT.Copy).then_inc(pt_taken, 1)
                    act.wait_ge(taken[gg.bank()], gg.evacuated())
                    a(eg[:], gT[:], ACT.Exp, scale=-1.0).then_inc(gate_exp_ready, 1)
                    act.wait_ge(og_ready, n + 2)
                    dst = oh[:, bass.ds(h, 1), :].rearrange("p a t -> p (a t)")
                    a(dst, og[:], ACT.Copy).then_inc(oh_ready, 1)

                def finished(g, m):
                    at = place(layer, g, n=4 * GH + m)
                    act.wait_ge(taken[at.bank()], at.evacuated())
                    act.wait_ge(acc_part, ACC_W + GH * layer + m - 1)
                    pair = slice(2 * m, 2 * m + 2)
                    a(sqs[:, m % 2], x1[:, pair].rearrange("p a t -> p (a t)"), ACT.Square).then_inc(sq_part, 1)
                    if layer == 0:
                        for kt in (2 * m, 2 * m + 1):
                            for to, col in ((1, G_B), (0, G_KV)):
                                ins = a(xhi[to][:, kt], x1[:, kt], ACT.Copy, scale=gain[:, kt, col:col + 1])
                        ins.then_inc(xhi_ready, 1)
                    else:
                        act.wait_ge(sq_part, SQ_W + GH + m + 1)
                        for kt in (2 * m, 2 * m + 1):
                            ins = a(x1[:, kt], x1[:, kt], ACT.Copy, scale=gain[:, kt, G_OUT:G_OUT + 1])
                        ins.then_inc(gained, 1)

                def project(g):
                    for m in range(GH):
                        at = place(layer, g, n=4 * GH + m)
                        ahead(split_hi, at, 0)
                        if isinstance(g, int) and m > 0:
                            finished(g, m - 1)
                        ahead(split_hi, at, 1)
                    if isinstance(g, int):
                        finished(g, GH - 1)
                layers(act, layer, head, project)
            root(2)

        @block.vector
        def _(dve):
            ch = chain(dve, "dve")
            v_ = nc.vector
            tt, ts, stt = v_.tensor_tensor, v_.tensor_scalar, v_.scalar_tensor_tensor

            def split_lo(at, h):
                st.split_lo(dve, at, h)

            v_.memset(stat[:, 0:1], 0.0).then_inc(sc_taken, 1)
            v_.memset(stat[:, 1:2], 0.0).then_inc(og_ready, 1)
            for half in range(2):
                s = slice(half * KT // 2, (half + 1) * KT // 2)
                dve.wait_ge(xhi_ready, 5 + half)
                tt(xlo[1][:, s], mix[:, s], xhi[1][:, s].bitcast(F32), ALU.subtract).then_inc(xlo_ready, 1)
                split_lo(At(U_WOUT), half)
            for j in range(2 * U_WOUT + 2, 2 * U_WOUT + AHEAD):
                split_lo(At(j // 2), j % 2)
            dve.wait_ge(xlo_ready, 6)
            with dve.Fori(0, KT // 4) as i:
                for n in range(4):
                    at = At(U_WOUT + n, [(i, 4)])
                    ahead(split_lo, at, 0)
                    b, j = n % 2, i * 4 + n
                    one = bass.ds(j, 1)
                    x1j = x1[:, one, :].rearrange("p a t -> p (a t)")
                    v_.tensor_copy(gcol[:, b], gain[:, one, :].rearrange("p a n -> p (a n)")).then_inc(gcol_ready, 1)
                    dve.wait_ge(x1_in[n], i * 16 + 16)
                    computed(dve, at)
                    tt(xraw[:, b], GB[at.bank()][:, 0:SEQ], x1j, ALU.add).then_inc(taken[at.bank()], 1)
                    dve.wait_ge(gcol_ready, j + 1)
                    dve.wait_ge(taken[at.bank()], at.evacuated())
                    ts(x1j, xraw[:, b], gcol[:, b, G_F:G_F + 1], None, ALU.mult).then_inc(x_part, 1)
                    ahead(split_lo, at, 1)
                    dve.wait_ge(xhi_ready, j + 7)
                    stt(xlo[0][:, one, :].rearrange("p a t -> p (a t)"), x1j, gcol[:, b, G_A:G_A + 1],
                        xhi[0][:, one, :].rearrange("p a t -> p (a t)").bitcast(F32), ALU.mult,
                        ALU.subtract).then_inc(xlo_ready, 1)
            dve.wait_ge(norm_sum, 1)
            ch.link(ts(inv, FZ[:, 0:SEQ], 1e-6 / D, 1e-12, ALU.mult, ALU.add))
            stt(inv, FZ[:, SEQ:], 1.0 / D, inv, ALU.mult, ALU.add).then_inc(norm_mean, 1)
            dve.wait_ge(norm_root, 1)
            v_.reciprocal(inv, inv).then_inc(norm_inv, 1)
            dve.wait_ge(norm_root, 2)
            v_.reciprocal(inv_f, inv_f).then_inc(norm_inv, 1)
            dve.wait_ge(norm_inv, 1)

            def inverse(n):
                dve.wait_ge(norm_root, n + 2)
                ch.link(v_.reciprocal(inv, inv))
            for layer in range(2):
                if layer == 1:
                    inverse(1)
                    dve.wait_ge(f_sum, 1)
                    dve.wait_ge(f_in, 34)
                    ch.link(tt(fz[:, 0], P2[0:AH, 0:SEQ], inv[0:AH], ALU.mult))
                    ch.link(ts(fz[:, 0], fz[:, 0], fb[:, 0:1], None, ALU.add))
                    ch.link(ts(fz[:, 1], fz[:, 0], -1.0, None, ALU.mult))
                    tt(fz[:, 2], fz[:, 0], fz[:, 1], ALU.max).then_inc(f_abs, 1)
                    dve.wait_ge(f_exp, 1)
                    ts(fz[:, 2], fz[:, 2], 1.0, None, ALU.add).then_inc(f_one, 1)
                    dve.wait_ge(f_ln, 1)
                    ch.link(stt(fz[:, 0], fz[:, 1], 0.0, fz[:, 2], ALU.max, ALU.add))
                    v_.tensor_tensor_scan(fz[:, 3], f_ones[:], fz[:, 0], 0.0, ALU.mult, ALU.add).then_inc(f_done, 1)

                def head(g, h):
                    n = head_no(layer, g, h)
                    q, k, v, gg = (place(layer, g, h, m) for m in range(4))
                    def evacuate(at, dst):
                        computed(dve, at)
                        b = GB[at.bank()][:, 0:SEQ]
                        (stt(dst[:], b, SCALE, inv, ALU.mult, ALU.mult) if dst is qT
                         else tt(dst[:], b, inv, ALU.mult)).then_inc(taken[at.bank()], 1)
                    for at, dst in ((q, qT), (k, kT)):
                        ahead(split_lo, at, 0)
                        ahead(split_lo, at, 1)
                        evacuate(at, dst)
                    ahead(split_lo, v, 0)
                    dve.wait_ge(sc_sum, n + 1)
                    if layer == 0:
                        dve.wait_ge(table_ready, n + 1)
                        ch(tt(sc[:, parts[0]], SC[:, parts[0]], table[:, 0:P][:, ::-1], ALU.add))
                        tt(sc[:, parts[1]], SC[:, parts[1]], table[:, 0:SEQ][:, ::-1], ALU.add).then_inc(sc_taken, 1)
                        dve.wait_ge(sc_taken, n + 2)
                    else:
                        dve.wait_ge(masked, n - AH + 1)
                        for m in range(2):
                            ins = stt(sc[:, parts[m]], table[:, parts[m]], nfq[:, m:m + 1], SC[:, parts[m]],
                                      ALU.subtract, ALU.add)
                            ch(ins) if m == 0 else ins.then_inc(sc_taken, 1)
                        dve.wait_ge(sc_taken, n + 2)
                    ch(v_.tensor_reduce(stat[:, 0:1], sc[:, parts[0]], AX_X, ALU.max))
                    ch.link(v_.tensor_reduce(stat[:, 1:2], sc[:, parts[1]], AX_X, ALU.max))
                    ts(stat[:, 2:4], stat[:, 0:2], -1.0, None, ALU.mult).then_inc(max_ready, 1)
                    ahead(split_lo, v, 1)
                    dve.wait_ge(exp_ready, n * 2 + 2)
                    ch.link(v_.reciprocal(stat[:, 4:6], stat[:, 4:6]))
                    for m in range(2):
                        ts(pr[:, parts[m]], pr[:, parts[m]], stat[:, 4 + m:5 + m], None, ALU.mult).then_inc(p_ready, 1)
                    evacuate(v, vT)
                    ahead(split_lo, gg, 0)
                    ahead(split_lo, gg, 1)
                    evacuate(gg, gT)
                    dve.wait_ge(gate_exp_ready, n + 1)
                    ch.link(ts(eg[:], eg[:], 1.0, None, ALU.add))
                    ch.link(v_.reciprocal(eg[:], eg[:]))
                    ch.link(tt(eg[:], eg[:], gT[:], ALU.mult))
                    dve.wait_ge(o_sum, n + 1)
                    tt(og[:], OT[:, 0:SEQ], eg[:], ALU.mult).then_inc(og_ready, 1)
                    dve.wait_ge(oh_ready, n + 1)
                    one = bass.ds(h, 1)
                    tt(ol[:, one, :].rearrange("p a t -> p (a t)"), og[:],
                       oh[:, one, :].rearrange("p a t -> p (a t)").bitcast(F32), ALU.subtract).then_inc(ol_ready, 1)

                def low_parts(m):
                    dve.wait_ge(xhi_ready, XH_W + m + 1)
                    for kt in (2 * m, 2 * m + 1):
                        for to, col in ((1, G_B), (0, G_KV)):
                            ins = stt(xlo[to][:, kt], x1[:, kt], gain[:, kt, col:col + 1],
                                      xhi[to][:, kt].bitcast(F32), ALU.mult, ALU.subtract)
                    ins.then_inc(xlo_ready, 1)

                def project(g):
                    dve.wait_ge(x1_scaled, 1)
                    for m in range(GH):
                        at = place(layer, g, n=4 * GH + m)
                        ahead(split_lo, at, 0)
                        if isinstance(g, int) and layer == 0 and m > 0:
                            low_parts(m - 1)
                        ahead(split_lo, at, 1)
                        computed(dve, at)
                        if m == 0:
                            tt(x1[:, 1], P2[:, 0:SEQ], x1[:, 1], ALU.add)
                            tt(x1[:, 0], GB[at.bank()][:, 0:SEQ], x1[:, 0], ALU.add).then_inc(taken[at.bank()], 1)
                        else:
                            xs = x1[:, 2 * m:2 * m + 2].rearrange("p a t -> p (a t)")
                            tt(xs, GB[at.bank()][:], xs, ALU.add).then_inc(taken[at.bank()], 1)
                    if isinstance(g, int) and layer == 0:
                        low_parts(GH - 1)
                layers(dve, layer, head, project, ch)
            dve.wait_ge(norm_root, 4)
            v_.reciprocal(inv, inv).then_inc(norm_inv, 1)
            dve.wait_ge(norm_inv, 3)
            dve.wait_ge(gained, GH)
            for c in range(len(OUT_PARTS) - 1):
                scale_out(v_, c)


_SPEC = ["xt", "prm", "gain", "lora", "lmu", "w_in", "w_out", "a_w_in", "rel", "a_w_out", "kv_w", "f_w", "f_b",
         "b_w_in", "b_w_out"]


def _layout(i):
    import numpy as _np

    f = _np.ascontiguousarray
    x = _np.concatenate([i["meta_tokens"], i["x"][0]], 0).T

    def tiles(v):
        return _np.reshape(v, (-1, 128)).T
    mu = i["mu_shift"][0]
    conv = i["conv_w"][0]
    per_channel = [mu[1024:2048], mu[0:1024], mu[2048:3072], mu[3072:4096], i["w0"][0], i["a0"][0], i["k_k"][0],
                   i["k_a"][0], i["r_k"][0], conv[0], conv[1], conv[2], i["lnx_g"][0], i["lnx_b"][0]]
    gains = [i[n] for n in ("norm_in_g", "norm_f_g", "a_norm_2", "kv_norm_2", "b_norm_2", "final_norm_2")]
    return {
        "xt": f(x.reshape(16, 128, 272).transpose(1, 0, 2)),
        "prm": f(_np.stack([tiles(v) for v in per_channel], -1)),
        "gain": f(_np.stack([tiles(v) for v in gains], -1)),
        "lora": f(_np.concatenate([i["w_lora_up"][0], i["a_lora_up"][0]], 0)),
        "lmu": f(mu[4096:4224].reshape(128, 1)),
        "w_in": i["w_in"][0], "w_out": i["w_out"][0], "a_w_in": i["a_w_in_2"][0], "rel": i["a_rel_bias_2"][0],
        "a_w_out": i["a_w_out_2"][0], "kv_w": i["kv_w_2"], "f_w": i["f_w_2"], "f_b": i["f_b_2"].reshape(32, 1),
        "b_w_in": i["b_w_in_2"][0], "b_w_out": i["b_w_out_2"][0],
    }


def kernel(**inputs):
    import numpy as _np
    import concourse.bacc as _bacc
    from concourse import mybir as _mybir
    from concourse.bass_utils import run_bass_kernel_spmd as _run

    nc = _bacc.Bacc("TRN2", target_bir_lowering=False, num_devices=1)
    laid = _layout({k: _np.asarray(v) for k, v in inputs.items()})
    arrays, aps = {}, {}
    for name in _SPEC:
        a = _np.ascontiguousarray(laid[name])
        arrays[f"in_{name}_dram"] = a
        aps[name] = nc.dram_tensor(f"in_{name}_dram", a.shape, _mybir.dt.from_np(a.dtype), kind="ExternalInput").ap()
    aps["out"] = nc.dram_tensor("out_dram", (128, 16, 256), _mybir.dt.float32, kind="ExternalOutput").ap()
    fused_blocks(nc, aps)
    r = _run(nc, [arrays], core_ids=[0])
    y = r.results[0]["out_dram"]
    return _np.ascontiguousarray(_np.reshape(_np.transpose(y, (2, 1, 0)), (1, 256, 2048)))
```
